# Optimizing a Trainium2 kernel written in Bass

```python
import math
import jax, jax.numpy as jnp
from jax import lax
import numpy as np

D_MODEL = 1024
BATCH = 1
SEQ = 256
DEPTH = 1

SSM_GROUP = 16
SSM_STATE = 64
SSM_WIDTH = D_MODEL // 2
SSM_GROUPS = SSM_WIDTH // SSM_GROUP
HEAD_DIM = 64
N_HEADS = D_MODEL // HEAD_DIM
N_KV = N_HEADS // 4
HPG = N_HEADS // N_KV
ATTN_WIDTH = N_HEADS * HEAD_DIM
KV_WIDTH = N_KV * HEAD_DIM
CMP_BLOCK = 32
CMP_STRIDE = 16
CMP_HIDDEN = 4 * HEAD_DIM
SLC_BLOCK = 64
SLC_TOPK = 16
WINDOW = 512
Q_CHUNK = 64
FORCED_SCORE = 1e4
IN_WIDTH = ATTN_WIDTH + 6 * KV_WIDTH + 3 * N_HEADS + SSM_WIDTH + 2 * D_MODEL
N_GROUPS = 4
EXP_PER_GROUP = 8
N_EXPERTS = N_GROUPS * EXP_PER_GROUP
TOPK_IN_GROUP = 2
D_EXPERT = D_MODEL // 4
MOE_BLOCK = 128
EPS = 1e-6
NEG = -1e30


def rms_norm(x, g):
    xf = x.astype(jnp.float32)
    y = xf * lax.rsqrt(jnp.mean(xf * xf, axis=-1, keepdims=True) + EPS)
    return (y * g.astype(jnp.float32)).astype(x.dtype)

def masked_softmax(s, mask):
    p = jax.nn.softmax(jnp.where(mask, s.astype(jnp.float32), NEG), axis=-1)
    return p * mask

def s5_mixer(u, lam_re, lam_im, log_dt, b_re, b_im, c_re, c_im, d_skip, w_glu):
    f32 = jnp.float32
    Bsz, L, _ = u.shape
    ug = u.astype(f32).reshape(Bsz, L, SSM_GROUPS, SSM_GROUP)
    dt = jnp.exp(log_dt.astype(f32))[:, None]
    lr, li = lam_re.astype(f32), lam_im.astype(f32)
    mag = jnp.exp(lr * dt)
    ab_re, ab_im = mag * jnp.cos(li * dt), mag * jnp.sin(li * dt)
    den = lr * lr + li * li
    nr = ab_re - 1.0
    cr = (nr * lr + ab_im * li) / den
    cim = (ab_im * lr - nr * li) / den
    br, bim = b_re.astype(f32), b_im.astype(f32)
    bb_re = cr[..., None] * br - cim[..., None] * bim
    bb_im = cr[..., None] * bim + cim[..., None] * br
    bu_re = jnp.einsum('blgh,gph->blgp', ug, bb_re)
    bu_im = jnp.einsum('blgh,gph->blgp', ug, bb_im)
    a_re = jnp.broadcast_to(ab_re, bu_re.shape)
    a_im = jnp.broadcast_to(ab_im, bu_im.shape)

    def combine(e1, e2):
        a1r, a1i, b1r, b1i = e1
        a2r, a2i, b2r, b2i = e2
        return (a2r * a1r - a2i * a1i, a2r * a1i + a2i * a1r,
                a2r * b1r - a2i * b1i + b2r, a2r * b1i + a2i * b1r + b2i)

    _, _, s_re, s_im = lax.associative_scan(combine, (a_re, a_im, bu_re, bu_im), axis=1)
    y = (jnp.einsum('blgp,ghp->blgh', s_re, c_re.astype(f32))
         - jnp.einsum('blgp,ghp->blgh', s_im, c_im.astype(f32))
         + d_skip.astype(f32) * ug)
    y = jax.nn.gelu(y.reshape(Bsz, L, SSM_WIDTH))
    y = y * jax.nn.sigmoid(y @ w_glu.astype(f32))
    return y.astype(u.dtype)

def compress_kv(kv, pos, w1, w2):
    Bsz, L, G, hd = kv.shape
    n_cmp = (L - CMP_BLOCK) // CMP_STRIDE + 1
    idx = jnp.arange(n_cmp)[:, None] * CMP_STRIDE + jnp.arange(CMP_BLOCK)[None, :]
    blocks = kv[:, idx] + pos[:, None, :]
    blocks = jnp.swapaxes(blocks, 2, 3).reshape(Bsz, n_cmp, G, CMP_BLOCK * hd)
    return jax.nn.gelu(blocks @ w1) @ w2

def nsa_attention(q, k_cmp, v_cmp, k_slc, v_slc, k_win, v_win, gates, cmp_pos, cmp_w1, cmp_w2):
    Bsz, L = q.shape[:2]
    n_cmp = (L - CMP_BLOCK) // CMP_STRIDE + 1
    n_slc = L // SLC_BLOCK
    n_sel = min(SLC_TOPK, n_slc)
    n_chunks = L // Q_CHUNK
    scale = HEAD_DIM ** -0.5
    kc = compress_kv(k_cmp, cmp_pos[0], cmp_w1[0], cmp_w2[0])
    vc = compress_kv(v_cmp, cmp_pos[1], cmp_w1[1], cmp_w2[1])
    cmp_end = jnp.arange(n_cmp) * CMP_STRIDE + CMP_BLOCK - 1
    c_start = jnp.arange(n_cmp)[:, None] * CMP_STRIDE
    s_start = jnp.arange(n_slc)[None, :] * SLC_BLOCK
    overlap = ((c_start < s_start + SLC_BLOCK) & (c_start + CMP_BLOCK > s_start)).astype(jnp.float32)
    ks_blk = jnp.moveaxis(k_slc.reshape(Bsz, n_slc, SLC_BLOCK, N_KV, HEAD_DIM), 3, 1)
    vs_blk = jnp.moveaxis(v_slc.reshape(Bsz, n_slc, SLC_BLOCK, N_KV, HEAD_DIM), 3, 1)
    kw = jnp.pad(k_win, ((0, 0), (WINDOW, 0), (0, 0), (0, 0)))
    vw = jnp.pad(v_win, ((0, 0), (WINDOW, 0), (0, 0), (0, 0)))
    bi = jnp.arange(Bsz)[:, None, None, None]
    gi = jnp.arange(N_KV)[None, :, None, None]
    blk = jnp.arange(n_slc)

    def chunk(args):
        c_idx, qc, gc = args
        t = c_idx * Q_CHUNK + jnp.arange(Q_CHUNK)
        s = jnp.einsum('bqghd,bngd->bqghn', qc, kc) * scale
        m = cmp_end[None, :] <= t[:, None]
        p_cmp = masked_softmax(s, m[None, :, None, None, :])
        o_cmp = jnp.einsum('bqghn,bngd->bqghd', p_cmp.astype(vc.dtype), vc)
        imp = jnp.einsum('bqghn,ns->bqgs', p_cmp, overlap)
        cur = t[:, None] // SLC_BLOCK
        forced = (blk[None, :] == 0) | (blk[None, :] == cur) | (blk[None, :] == cur - 1)
        future = blk[None, :] * SLC_BLOCK > t[:, None]
        imp = jnp.where(forced[None, :, None, :], FORCED_SCORE, imp)
        imp = jnp.where(future[None, :, None, :], -1.0, imp)
        _, sel = lax.top_k(imp, n_sel)
        sel = jnp.transpose(sel, (0, 2, 1, 3))
        ks = ks_blk[bi, gi, sel].reshape(Bsz, N_KV, Q_CHUNK, n_sel * SLC_BLOCK, HEAD_DIM)
        vs = vs_blk[bi, gi, sel].reshape(Bsz, N_KV, Q_CHUNK, n_sel * SLC_BLOCK, HEAD_DIM)
        kpos = (sel[..., None] * SLC_BLOCK + jnp.arange(SLC_BLOCK)).reshape(Bsz, N_KV, Q_CHUNK, n_sel * SLC_BLOCK)
        m = jnp.transpose(kpos <= t[None, None, :, None], (0, 2, 1, 3))[:, :, :, None, :]
        s = jnp.einsum('bqghd,bgqkd->bqghk', qc, ks) * scale
        p = masked_softmax(s, m)
        o_slc = jnp.einsum('bqghk,bgqkd->bqghd', p.astype(vs.dtype), vs)
        start = c_idx * Q_CHUNK
        kwc = lax.dynamic_slice_in_dim(kw, start, WINDOW + Q_CHUNK, axis=1)
        vwc = lax.dynamic_slice_in_dim(vw, start, WINDOW + Q_CHUNK, axis=1)
        wpos = start - WINDOW + jnp.arange(WINDOW + Q_CHUNK)
        d = t[:, None] - wpos[None, :]
        m = (d >= 0) & (d < WINDOW) & (wpos[None, :] >= 0)
        s = jnp.einsum('bqghd,bkgd->bqghk', qc, kwc) * scale
        p = masked_softmax(s, m[None, :, None, None, :])
        o_win = jnp.einsum('bqghk,bkgd->bqghd', p.astype(vwc.dtype), vwc)
        return (gc[:, :, 0, :, :, None] * o_cmp + gc[:, :, 1, :, :, None] * o_slc
                + gc[:, :, 2, :, :, None] * o_win)

    q_ch = jnp.moveaxis(q.reshape(Bsz, n_chunks, Q_CHUNK, N_KV, HPG, HEAD_DIM), 1, 0)
    g_ch = jnp.moveaxis(gates.reshape(Bsz, n_chunks, Q_CHUNK, 3, N_KV, HPG), 1, 0)
    o = lax.map(chunk, (jnp.arange(n_chunks), q_ch, g_ch))
    return jnp.moveaxis(o, 0, 1).reshape(Bsz, L, ATTN_WIDTH)

def token_mixer(h, w_in, ssm_lam_re, ssm_lam_im, ssm_log_dt, ssm_b_re, ssm_b_im, ssm_c_re, ssm_c_im,
                ssm_d, ssm_w_glu, ssm_w_o, nsa_cmp_pos, nsa_cmp_w1, nsa_cmp_w2, nsa_w_o, w_out):
    Bsz, L, _ = h.shape
    proj = h @ w_in
    o1 = ATTN_WIDTH
    o2 = o1 + 6 * KV_WIDTH
    o3 = o2 + 3 * N_HEADS
    o4 = o3 + SSM_WIDTH
    q, kv, nsa_g, u, merge_g = jnp.split(proj, [o1, o2, o3, o4], axis=-1)
    k_cmp, v_cmp, k_slc, v_slc, k_win, v_win = [t.reshape(Bsz, L, N_KV, HEAD_DIM) for t in jnp.split(kv, 6, axis=-1)]
    attn = nsa_attention(q.reshape(Bsz, L, N_KV, HPG, HEAD_DIM), k_cmp, v_cmp, k_slc, v_slc, k_win, v_win,
                         jax.nn.sigmoid(nsa_g).reshape(Bsz, L, 3, N_KV, HPG), nsa_cmp_pos, nsa_cmp_w1, nsa_cmp_w2)
    ssm = s5_mixer(u, ssm_lam_re, ssm_lam_im, ssm_log_dt, ssm_b_re, ssm_b_im, ssm_c_re, ssm_c_im, ssm_d, ssm_w_glu)
    g_attn, g_ssm = jnp.split(jax.nn.sigmoid(merge_g), 2, axis=-1)
    merged = g_attn * (attn @ nsa_w_o) + g_ssm * (ssm @ ssm_w_o)
    return merged @ w_out

def hier_moe(h, w_group, b_group, w_expert, b_expert, w_gate, w_up, w_down):
    Bsz, L, D = h.shape
    xt = h.reshape(-1, D)
    N = xt.shape[0]
    g_prob = jax.nn.softmax((xt @ w_group + b_group).astype(jnp.float32), axis=-1)
    g_p, g_idx = lax.top_k(g_prob, 1)
    e_logits = (xt @ w_expert + b_expert).astype(jnp.float32).reshape(N, N_GROUPS, EXP_PER_GROUP)
    e_logits = jnp.take_along_axis(e_logits, jnp.broadcast_to(g_idx[:, :, None], (N, 1, EXP_PER_GROUP)), axis=1)[:, 0]
    e_p, e_idx = lax.top_k(jax.nn.softmax(e_logits, axis=-1), TOPK_IN_GROUP)
    w = g_p * e_p / jnp.sum(e_p, axis=-1, keepdims=True)
    eid = g_idx * EXP_PER_GROUP + e_idx
    A = N * TOPK_IN_GROUP
    flat_e = eid.reshape(-1)
    flat_t = jnp.repeat(jnp.arange(N, dtype=jnp.int32), TOPK_IN_GROUP)
    flat_w = w.reshape(-1)
    order = jnp.argsort(flat_e)
    se = flat_e[order]
    counts = jnp.zeros(N_EXPERTS, jnp.int32).at[flat_e].add(1)
    starts = jnp.cumsum(counts) - counts
    pcounts = (counts + MOE_BLOCK - 1) // MOE_BLOCK * MOE_BLOCK
    pends = jnp.cumsum(pcounts)
    pstarts = pends - pcounts
    dest = pstarts[se] + jnp.arange(A) - starts[se]
    P = A + N_EXPERTS * MOE_BLOCK
    n_blk = P // MOE_BLOCK
    buf_t = jnp.zeros(P, jnp.int32).at[dest].set(flat_t[order])
    buf_w = jnp.zeros(P, jnp.float32).at[dest].set(flat_w[order])
    blk_e = jnp.minimum(jnp.searchsorted(pends, jnp.arange(n_blk) * MOE_BLOCK, side='right'), N_EXPERTS - 1)
    xs = xt[buf_t].reshape(n_blk, MOE_BLOCK, D)

    def expert_block(args):
        xb, e = args
        return (jax.nn.silu(xb @ w_gate[e]) * (xb @ w_up[e])) @ w_down[e]

    ys = lax.map(expert_block, (xs, blk_e)).reshape(P, D)
    out = jnp.zeros((N, D), jnp.float32).at[buf_t].add(ys.astype(jnp.float32) * buf_w[:, None])
    return out.astype(h.dtype).reshape(Bsz, L, D)

def first_inputs(seed: int = 0) -> dict:
    key = jax.random.key(seed)
    ks = jax.random.split(key, 32)
    f32 = jnp.float32

    def nrm(k, shape, s):
        return jax.random.normal(k, shape, f32) * s

    n_idx = jnp.arange(SSM_STATE, dtype=f32)
    return {
        'x': nrm(ks[0], (BATCH, SEQ, D_MODEL), 1.0),
        'c': nrm(ks[1], (BATCH, D_MODEL), 1.0),
        'ada_w': nrm(ks[2], (DEPTH, D_MODEL, 6 * D_MODEL), 0.5 * D_MODEL ** -0.5),
        'ada_b': nrm(ks[3], (DEPTH, 6 * D_MODEL), 0.01),
        'norm1_g': 1.0 + nrm(ks[4], (DEPTH, D_MODEL), 0.02),
        'w_in': nrm(ks[5], (DEPTH, D_MODEL, IN_WIDTH), D_MODEL ** -0.5),
        'ssm_lam_re': -0.5 + nrm(ks[6], (DEPTH, SSM_GROUPS, SSM_STATE), 0.01),
        'ssm_lam_im': math.pi * n_idx + nrm(ks[7], (DEPTH, SSM_GROUPS, SSM_STATE), 0.01),
        'ssm_log_dt': jax.random.uniform(ks[8], (DEPTH, SSM_GROUPS), f32, math.log(1e-3), math.log(1e-1)),
        'ssm_b_re': nrm(ks[9], (DEPTH, SSM_GROUPS, SSM_STATE, SSM_GROUP), (2 * SSM_GROUP) ** -0.5),
        'ssm_b_im': nrm(ks[10], (DEPTH, SSM_GROUPS, SSM_STATE, SSM_GROUP), (2 * SSM_GROUP) ** -0.5),
        'ssm_c_re': nrm(ks[11], (DEPTH, SSM_GROUPS, SSM_GROUP, SSM_STATE), SSM_STATE ** -0.5),
        'ssm_c_im': nrm(ks[12], (DEPTH, SSM_GROUPS, SSM_GROUP, SSM_STATE), SSM_STATE ** -0.5),
        'ssm_d': nrm(ks[13], (DEPTH, SSM_GROUPS, SSM_GROUP), 1.0),
        'ssm_w_glu': nrm(ks[14], (DEPTH, SSM_WIDTH, SSM_WIDTH), SSM_WIDTH ** -0.5),
        'ssm_w_o': nrm(ks[15], (DEPTH, SSM_WIDTH, D_MODEL), SSM_WIDTH ** -0.5),
        'nsa_cmp_pos': nrm(ks[16], (DEPTH, 2, CMP_BLOCK, HEAD_DIM), 0.02),
        'nsa_cmp_w1': nrm(ks[17], (DEPTH, 2, CMP_BLOCK * HEAD_DIM, CMP_HIDDEN), (CMP_BLOCK * HEAD_DIM) ** -0.5),
        'nsa_cmp_w2': nrm(ks[18], (DEPTH, 2, CMP_HIDDEN, HEAD_DIM), CMP_HIDDEN ** -0.5),
        'nsa_w_o': nrm(ks[19], (DEPTH, ATTN_WIDTH, D_MODEL), ATTN_WIDTH ** -0.5),
        'w_out': nrm(ks[20], (DEPTH, D_MODEL, D_MODEL), D_MODEL ** -0.5),
        'norm2_g': 1.0 + nrm(ks[21], (DEPTH, D_MODEL), 0.02),
        'moe_w_group': nrm(ks[22], (DEPTH, D_MODEL, N_GROUPS), D_MODEL ** -0.5),
        'moe_b_group': nrm(ks[23], (DEPTH, N_GROUPS), 0.01),
        'moe_w_expert': nrm(ks[24], (DEPTH, D_MODEL, N_EXPERTS), D_MODEL ** -0.5),
        'moe_b_expert': nrm(ks[25], (DEPTH, N_EXPERTS), 0.01),
        'moe_w_gate': nrm(ks[26], (DEPTH, N_EXPERTS, D_MODEL, D_EXPERT), D_MODEL ** -0.5),
        'moe_w_up': nrm(ks[27], (DEPTH, N_EXPERTS, D_MODEL, D_EXPERT), D_MODEL ** -0.5),
        'moe_w_down': nrm(ks[28], (DEPTH, N_EXPERTS, D_EXPERT, D_MODEL), D_EXPERT ** -0.5),
        'final_g': 1.0 + nrm(ks[29], (D_MODEL,), 0.02),
    }

def first_block(x, c, ada_w, ada_b, norm1_g, w_in, ssm_lam_re, ssm_lam_im, ssm_log_dt, ssm_b_re, ssm_b_im,
              ssm_c_re, ssm_c_im, ssm_d, ssm_w_glu, ssm_w_o, nsa_cmp_pos, nsa_cmp_w1, nsa_cmp_w2, nsa_w_o,
              w_out, norm2_g, moe_w_group, moe_b_group, moe_w_expert, moe_b_expert, moe_w_gate, moe_w_up,
              moe_w_down, final_g):
    cs = jax.nn.silu(c)
    for l in range(DEPTH):
        mod = cs @ ada_w[l] + ada_b[l]
        sh1, sc1, g1, sh2, sc2, g2 = jnp.split(mod[:, None, :], 6, axis=-1)
        h = rms_norm(x, norm1_g[l]) * (1.0 + sc1) + sh1
        x = x + g1 * token_mixer(h, w_in[l], ssm_lam_re[l], ssm_lam_im[l], ssm_log_dt[l], ssm_b_re[l],
                                 ssm_b_im[l], ssm_c_re[l], ssm_c_im[l], ssm_d[l], ssm_w_glu[l], ssm_w_o[l],
                                 nsa_cmp_pos[l], nsa_cmp_w1[l], nsa_cmp_w2[l], nsa_w_o[l], w_out[l])
        h = rms_norm(x, norm2_g[l]) * (1.0 + sc2) + sh2
        x = x + g2 * hier_moe(h, moe_w_group[l], moe_b_group[l], moe_w_expert[l], moe_b_expert[l],
                              moe_w_gate[l], moe_w_up[l], moe_w_down[l])
    return rms_norm(x, final_g)


GRID_W = 64
CTX_LEN = 256
NA_HEADS = 8
NA_WIN_R = 8
NA_WIN_C = 16
GQA_HEADS = 8
GQA_KV_HEADS = 2
Q_BLOCK = 128
ROPE_THETA = 10000.0
N_EXPERTS_2 = 32
TOP_K = 4
D_FF = D_MODEL
SWIGLU_LIMIT = 7.0
SWIGLU_ALPHA = 1.702
EXPERT_BLOCK = 128
NORM_EPS = 1e-6

NA_WIDTH = NA_HEADS * HEAD_DIM
GQA_WIDTH = GQA_HEADS * HEAD_DIM
GQA_KV_WIDTH = GQA_KV_HEADS * HEAD_DIM
IN_SPLITS = (NA_WIDTH, NA_WIDTH, GQA_KV_WIDTH, GQA_KV_WIDTH, NA_WIDTH, GQA_WIDTH, D_MODEL, D_MODEL)
KV_COLS = 2 * NA_WIDTH + 2 * GQA_KV_WIDTH
IN_COLS = sum(IN_SPLITS)


def rmsnorm(x, g):
    xf = x.astype(jnp.float32)
    y = xf * lax.rsqrt(jnp.mean(xf * xf, axis=-1, keepdims=True) + NORM_EPS)
    return (y * g.astype(jnp.float32)).astype(x.dtype)

def split_cols(p, sizes):
    return jnp.split(p, np.cumsum(sizes)[:-1].tolist(), axis=-1)

def to_heads(t, n):
    return t.reshape(t.shape[0], t.shape[1], n, HEAD_DIM)

def axial_rope(x, row, col):
    half = HEAD_DIM // 2
    nf = half // 2
    freqs = ROPE_THETA ** (-jnp.arange(nf, dtype=jnp.float32) / nf)

    def rot(xp, pos):
        ang = pos.astype(jnp.float32)[:, None] * freqs
        cos = jnp.cos(ang)[None, :, None, :]
        sin = jnp.sin(ang)[None, :, None, :]
        x1 = xp[..., :nf].astype(jnp.float32)
        x2 = xp[..., nf:].astype(jnp.float32)
        return jnp.concatenate([x1 * cos - x2 * sin, x2 * cos + x1 * sin], axis=-1)

    return jnp.concatenate([rot(x[..., :half], row), rot(x[..., half:], col)], axis=-1).astype(x.dtype)

def gqa_attend(q, k, v):
    s = jnp.einsum('btkgd,bskd->bkgts', q, k)
    p = jax.nn.softmax(s.astype(jnp.float32), axis=-1).astype(q.dtype)
    return jnp.einsum('bkgts,bskd->btkgd', p, v)

def blocked_gqa(q, k, v):
    B, S = q.shape[0], q.shape[1]
    nb = S // Q_BLOCK
    qb = q.reshape(B, nb, Q_BLOCK, *q.shape[2:]).swapaxes(0, 1)
    out = lax.map(lambda blk: gqa_attend(blk, k, v), qb)
    return out.swapaxes(0, 1).reshape(B, S, -1)

def neighbourhood_attention(q, k, v, k_ctx, v_ctx, rpb):
    B, S, H, Dh = q.shape
    rows = S // GRID_W
    kr = min(NA_WIN_R, rows)
    kc = min(NA_WIN_C, GRID_W)
    qg = q.reshape(B, rows, GRID_W, H, Dh)
    kg = k.reshape(B, rows, GRID_W, H, Dh)
    vg = v.reshape(B, rows, GRID_W, H, Dh)
    cols = np.arange(GRID_W)
    c0 = np.clip(cols - kc // 2, 0, GRID_W - kc)
    col_idx = (c0[:, None] + np.arange(kc)[None, :]).astype(np.int32)
    col_off = (col_idx - cols[:, None] + (NA_WIN_C - 1)).astype(np.int32)

    def row_block(r):
        r0 = jnp.clip(r - kr // 2, 0, rows - kr)
        q_r = lax.dynamic_index_in_dim(qg, r, axis=1, keepdims=False)
        k_nb = lax.dynamic_slice_in_dim(kg, r0, kr, axis=1)[:, :, col_idx]
        v_nb = lax.dynamic_slice_in_dim(vg, r0, kr, axis=1)[:, :, col_idx]
        row_off = r0 + jnp.arange(kr, dtype=jnp.int32) - r + (NA_WIN_R - 1)
        bias = rpb[:, row_off[:, None, None], col_off[None, :, :]].transpose(0, 2, 1, 3)
        s_loc = jnp.einsum('bwhd,brwchd->bhwrc', q_r, k_nb) + bias.astype(q.dtype)
        s_ctx = jnp.einsum('bwhd,bnhd->bhwn', q_r, k_ctx)
        s = jnp.concatenate([s_loc.reshape(B, H, GRID_W, kr * kc), s_ctx], axis=-1)
        p = jax.nn.softmax(s.astype(jnp.float32), axis=-1).astype(q.dtype)
        p_loc = p[..., :kr * kc].reshape(B, H, GRID_W, kr, kc)
        p_ctx = p[..., kr * kc:]
        return (jnp.einsum('bhwrc,brwchd->bwhd', p_loc, v_nb)
                + jnp.einsum('bhwn,bnhd->bwhd', p_ctx, v_ctx))

    out = lax.map(row_block, jnp.arange(rows, dtype=jnp.int32))
    return out.transpose(1, 0, 2, 3, 4).reshape(B, S, H * Dh)

def merge_branches(o_a, o_b, g_a, g_b, w_out_a, w_out_b, w_o):
    return (jax.nn.sigmoid(g_a) * (o_a @ w_out_a) + jax.nn.sigmoid(g_b) * (o_b @ w_out_b)) @ w_o

def hybrid_mixer(h, h_ctx, w_in, rpb, g_qn, g_kn, w_out_a, w_out_b, w_o, row, col, update_ctx):
    B, S, _ = h.shape
    C = h_ctx.shape[1]
    scale = HEAD_DIM ** -0.5
    G = GQA_HEADS // GQA_KV_HEADS
    k_a, v_a, k_b, v_b, q_a, q_b, g_a, g_b = split_cols(h @ w_in, IN_SPLITS)
    if update_ctx:
        parts = split_cols(h_ctx @ w_in, IN_SPLITS)
    else:
        parts = split_cols(h_ctx @ w_in[:, :KV_COLS], IN_SPLITS[:4])
    k_ca = to_heads(parts[0], NA_HEADS)
    v_ca = to_heads(parts[1], NA_HEADS)
    k_cb = rmsnorm(to_heads(parts[2], GQA_KV_HEADS), g_kn)
    v_cb = to_heads(parts[3], GQA_KV_HEADS)

    o_a = neighbourhood_attention(to_heads(q_a, NA_HEADS) * scale, to_heads(k_a, NA_HEADS),
                                  to_heads(v_a, NA_HEADS), k_ca, v_ca, rpb)
    qb = axial_rope(rmsnorm(to_heads(q_b, GQA_HEADS), g_qn), row, col) * scale
    kb = axial_rope(rmsnorm(to_heads(k_b, GQA_KV_HEADS), g_kn), row, col)
    k_all = jnp.concatenate([kb, k_cb], axis=1)
    v_all = jnp.concatenate([to_heads(v_b, GQA_KV_HEADS), v_cb], axis=1)
    o_b = blocked_gqa(qb.reshape(B, S, GQA_KV_HEADS, G, HEAD_DIM), k_all, v_all)
    y = merge_branches(o_a, o_b, g_a, g_b, w_out_a, w_out_b, w_o)

    y_ctx = None
    if update_ctx:
        q_ca, q_cb, g_ca, g_cb = parts[4:]
        o_ca = gqa_attend(to_heads(q_ca, NA_HEADS)[:, :, :, None, :] * scale, k_ca, v_ca).reshape(B, C, -1)
        qcb = rmsnorm(to_heads(q_cb, GQA_HEADS), g_qn) * scale
        o_cb = gqa_attend(qcb.reshape(B, C, GQA_KV_HEADS, G, HEAD_DIM), k_cb, v_cb).reshape(B, C, -1)
        y_ctx = merge_branches(o_ca, o_cb, g_ca, g_cb, w_out_a, w_out_b, w_o)
    return y, y_ctx

def moe_ffn(h, w_router, b_router, w_gu, b_gu, w_dn, b_dn):
    T, D = h.shape
    logits = (h @ w_router + b_router).astype(jnp.float32)
    top_logits, top_e = lax.top_k(logits, TOP_K)
    top_w = jax.nn.softmax(top_logits, axis=-1).astype(h.dtype)
    n_assign = T * TOP_K
    flat_e = top_e.reshape(-1)
    flat_tok = jnp.arange(n_assign, dtype=jnp.int32) // TOP_K
    order = jnp.argsort(flat_e)
    e_sorted = flat_e[order]
    counts = jnp.bincount(flat_e, length=N_EXPERTS_2)
    padded = (counts + EXPERT_BLOCK - 1) // EXPERT_BLOCK * EXPERT_BLOCK
    pad_end = jnp.cumsum(padded)
    pad_start = pad_end - padded
    start = jnp.cumsum(counts) - counts
    dest = pad_start[e_sorted] + jnp.arange(n_assign, dtype=jnp.int32) - start[e_sorted]
    n_blocks = -(-n_assign // EXPERT_BLOCK) + N_EXPERTS_2
    n_slots = n_blocks * EXPERT_BLOCK
    slot_tok = jnp.full((n_slots,), T, dtype=jnp.int32).at[dest].set(flat_tok[order])
    slot_w = jnp.zeros((n_slots,), h.dtype).at[dest].set(top_w.reshape(-1)[order])
    block_e = jnp.minimum(jnp.searchsorted(pad_end, jnp.arange(n_blocks, dtype=jnp.int32) * EXPERT_BLOCK,
                                           side='right'), N_EXPERTS_2 - 1)
    h_pad = jnp.concatenate([h, jnp.zeros((1, D), h.dtype)], axis=0)
    xb = h_pad[slot_tok].reshape(n_blocks, EXPERT_BLOCK, D)

    def expert_block(args):
        xe, e = args
        gu = xe @ w_gu[e] + b_gu[e]
        x_glu = jnp.minimum(gu[:, :D_FF], SWIGLU_LIMIT)
        x_lin = jnp.clip(gu[:, D_FF:], -SWIGLU_LIMIT, SWIGLU_LIMIT)
        act = (x_lin + 1) * (x_glu * jax.nn.sigmoid(SWIGLU_ALPHA * x_glu))
        return act @ w_dn[e] + b_dn[e]

    yb = lax.map(expert_block, (xb, block_e))
    y = jnp.zeros((T + 1, D), h.dtype).at[slot_tok].add(yb.reshape(n_slots, D) * slot_w[:, None])
    return y[:T]

def second_inputs(seed: int = 0) -> dict:
    key = jax.random.key(seed)
    ks = jax.random.split(key, 23)
    f32 = jnp.float32
    L = DEPTH

    def nrm(k, shape, s):
        return jax.random.normal(k, shape, f32) * s

    def gain(k, shape):
        return 1.0 + 0.05 * jax.random.normal(k, shape, f32)

    return {
        'x': nrm(ks[0], (BATCH, SEQ, D_MODEL), 1.0),
        'c': nrm(ks[1], (BATCH, D_MODEL), 1.0),
        'ctx': nrm(ks[2], (BATCH, CTX_LEN, D_MODEL), 1.0),
        'c_ctx': nrm(ks[3], (D_MODEL,), 1.0),
        'w_mod': nrm(ks[4], (L, D_MODEL, 6 * D_MODEL), 0.5 * D_MODEL ** -0.5),
        'b_mod': nrm(ks[5], (L, 6 * D_MODEL), 0.02),
        'g_pre_mix': gain(ks[6], (L, D_MODEL)),
        'g_post_mix': gain(ks[7], (L, D_MODEL)),
        'g_pre_ffn': gain(ks[8], (L, D_MODEL)),
        'g_post_ffn': gain(ks[9], (L, D_MODEL)),
        'w_in': nrm(ks[10], (L, D_MODEL, IN_COLS), D_MODEL ** -0.5),
        'rpb': nrm(ks[11], (L, NA_HEADS, 2 * NA_WIN_R - 1, 2 * NA_WIN_C - 1), 0.1),
        'g_qnorm': gain(ks[12], (L, HEAD_DIM)),
        'g_knorm': gain(ks[13], (L, HEAD_DIM)),
        'w_out_a': nrm(ks[14], (L, NA_WIDTH, D_MODEL), NA_WIDTH ** -0.5),
        'w_out_b': nrm(ks[15], (L, GQA_WIDTH, D_MODEL), GQA_WIDTH ** -0.5),
        'w_o': nrm(ks[16], (L, D_MODEL, D_MODEL), D_MODEL ** -0.5),
        'w_router': nrm(ks[17], (L, D_MODEL, N_EXPERTS_2), D_MODEL ** -0.5),
        'b_router': nrm(ks[18], (L, N_EXPERTS_2), 0.01),
        'w_gu': nrm(ks[19], (L, N_EXPERTS_2, D_MODEL, 2 * D_FF), D_MODEL ** -0.5),
        'b_gu': nrm(ks[20], (L, N_EXPERTS_2, 2 * D_FF), 0.02),
        'w_dn': nrm(ks[21], (L, N_EXPERTS_2, D_FF, D_MODEL), D_FF ** -0.5),
        'b_dn': nrm(ks[22], (L, N_EXPERTS_2, D_MODEL), 0.02),
    }

def second_block(x, c, ctx, c_ctx, w_mod, b_mod, g_pre_mix, g_post_mix, g_pre_ffn, g_post_ffn,
              w_in, rpb, g_qnorm, g_knorm, w_out_a, w_out_b, w_o,
              w_router, b_router, w_gu, b_gu, w_dn, b_dn):
    B, S, D = x.shape
    C = ctx.shape[1]
    t = jnp.arange(S, dtype=jnp.int32)
    row = t // GRID_W
    col = t % GRID_W
    silu_c = jax.nn.silu(c)
    silu_cc = jax.nn.silu(c_ctx)
    for i in range(DEPTH):
        update_ctx = i < DEPTH - 1
        sh1, sc1, gt1, sh2, sc2, gt2 = jnp.split((silu_c @ w_mod[i] + b_mod[i])[:, None, :], 6, axis=-1)
        n_mod = 6 if update_ctx else 2
        mod_c = jnp.split(silu_cc @ w_mod[i][:, :n_mod * D] + b_mod[i][:n_mod * D], n_mod)

        h = rmsnorm(x, g_pre_mix[i]) * (1 + sc1) + sh1
        h_ctx = rmsnorm(ctx, g_pre_mix[i]) * (1 + mod_c[1]) + mod_c[0]
        y, y_ctx = hybrid_mixer(h, h_ctx, w_in[i], rpb[i], g_qnorm[i], g_knorm[i],
                                w_out_a[i], w_out_b[i], w_o[i], row, col, update_ctx)
        x = x + gt1 * rmsnorm(y, g_post_mix[i])

        h2 = rmsnorm(x, g_pre_ffn[i]) * (1 + sc2) + sh2
        tokens = h2.reshape(B * S, D)
        if update_ctx:
            ctx = ctx + mod_c[2] * rmsnorm(y_ctx, g_post_mix[i])
            h2_ctx = rmsnorm(ctx, g_pre_ffn[i]) * (1 + mod_c[4]) + mod_c[3]
            tokens = jnp.concatenate([tokens, h2_ctx.reshape(B * C, D)], axis=0)
        f = moe_ffn(tokens, w_router[i], b_router[i], w_gu[i], b_gu[i], w_dn[i], b_dn[i])
        x = x + gt2 * rmsnorm(f[:B * S].reshape(B, S, D), g_post_ffn[i])
        if update_ctx:
            ctx = ctx + mod_c[5] * rmsnorm(f[B * S:].reshape(B, C, D), g_post_ffn[i])
    return x


def setup_inputs(seed=0):
    out = dict(first_inputs(seed))
    for name, value in second_inputs(seed + 1).items():
        if name != "x":
            out[name + "_2"] = value
    return out


def reference(
    x, c, ada_w, ada_b, norm1_g, w_in, ssm_lam_re, ssm_lam_im, ssm_log_dt, ssm_b_re, ssm_b_im,
    ssm_c_re, ssm_c_im, ssm_d, ssm_w_glu, ssm_w_o, nsa_cmp_pos, nsa_cmp_w1, nsa_cmp_w2, nsa_w_o,
    w_out, norm2_g, moe_w_group, moe_b_group, moe_w_expert, moe_b_expert, moe_w_gate, moe_w_up,
    moe_w_down, final_g, c_2, ctx_2, c_ctx_2, w_mod_2, b_mod_2, g_pre_mix_2, g_post_mix_2,
    g_pre_ffn_2, g_post_ffn_2, w_in_2, rpb_2, g_qnorm_2, g_knorm_2, w_out_a_2, w_out_b_2, w_o_2,
    w_router_2, b_router_2, w_gu_2, b_gu_2, w_dn_2, b_dn_2,
):
    x = first_block(
        x, c, ada_w, ada_b, norm1_g, w_in, ssm_lam_re, ssm_lam_im, ssm_log_dt, ssm_b_re,
        ssm_b_im, ssm_c_re, ssm_c_im, ssm_d, ssm_w_glu, ssm_w_o, nsa_cmp_pos, nsa_cmp_w1,
        nsa_cmp_w2, nsa_w_o, w_out, norm2_g, moe_w_group, moe_b_group, moe_w_expert,
        moe_b_expert, moe_w_gate, moe_w_up, moe_w_down, final_g,
    )
    return second_block(
        x, c_2, ctx_2, c_ctx_2, w_mod_2, b_mod_2, g_pre_mix_2, g_post_mix_2, g_pre_ffn_2,
        g_post_ffn_2, w_in_2, rpb_2, g_qnorm_2, g_knorm_2, w_out_a_2, w_out_b_2, w_o_2,
        w_router_2, b_router_2, w_gu_2, b_gu_2, w_dn_2, b_dn_2,
    )


_drawn_inputs = setup_inputs


def setup_inputs(seed=0):
    import zlib

    import numpy as np

    out = dict(_drawn_inputs(seed))
    spreads = {}
    factors = {'ada_b': 2.86,
     'norm1_g': 8.0,
     'ssm_lam_re': 8.0,
     'ssm_lam_im': 3.211,
     'ssm_log_dt': 3.302,
     'ssm_b_re': 4.525,
     'ssm_b_im': 6.224,
     'ssm_c_re': 5.281,
     'ssm_c_im': 4.282,
     'nsa_cmp_pos': 8.0,
     'norm2_g': 2.701,
     'moe_b_group': 8.0,
     'moe_b_expert': 7.041,
     'g_pre_mix_2': 2.766,
     'g_post_ffn_2': 4.008,
     'rpb_2': 4.691,
     'g_qnorm_2': 4.212,
     'g_knorm_2': 6.384,
     'b_router_2': 3.074,
     'b_gu_2': 8.0,
     'b_dn_2': 8.0}
    for name, (base, spread) in spreads.items():
        noise = np.random.default_rng([zlib.crc32(name.encode()), seed]).standard_normal(out[name].shape)
        drawn = base * np.exp(spread * noise) if base else spread * noise
        out[name] = __import__('jax').numpy.asarray(drawn.astype(out[name].dtype))
    for name, factor in factors.items():
        out[name] = (out[name] * factor).astype(out[name].dtype)
    return out
```

```python
from contextlib import ExitStack

import numpy as np
import concourse.bass as bass
from concourse import mybir

F32 = mybir.dt.float32
I32 = mybir.dt.int32
ALU = mybir.AluOpType
ACT = mybir.ActivationFunctionType
AX = mybir.AxisListType

P = 128
T = 256
D = 1024
KD = D // P
TT = T // P
HD = 64
NCMP = 15
EPS = 1e-6
NEG = -1e30
E = 32
SLOTS = 64
MAXB = T // SLOTS
RING = 12
SLOT = 2048
TWO_PI = 2 * np.pi
SIN2PI = 6.283185
MAGIC = 1.5 * 2.0 ** 23

CONST = {}


def constants():
    p = np.arange(P)
    parts = {}
    parts["ident"] = np.eye(P)
    parts["ones"] = np.ones((P, P))
    parts["causal"] = np.where(p[None, :] > p[:, None], NEG, 0.0)
    t = (np.arange(TT)[None, :] * P + p[:, None])
    end = np.arange(NCMP) * 16 + 31
    parts["cmpmask"] = np.where(end[None, None, :] <= t[:, :, None], 0.0, NEG).reshape(P, -1)
    parts["cmprow"] = (t >= 31).astype(np.float64)
    parts["before"] = (p[:, None] < p[None, :]).astype(np.float64)
    mirror = np.zeros((P, P))
    mirror[p, (p // 64) * 64 + 63 - p % 64] = 1.0
    parts["mirror"] = mirror
    parts["time"] = np.broadcast_to(np.arange(T)[None, :], (P, T))
    col = 63 - p % 64
    c0 = np.clip(col - 8, 0, 48)
    kc = np.arange(64)
    parts["namask"] = np.where((kc[None, :] >= c0[:, None]) & (kc[None, :] < c0[:, None] + 16), 0.0, NEG)
    nf = 16
    freqs = 10000.0 ** (-np.arange(nf) / nf)
    row, cl = t // 64, t % 64
    angr, angc = row[:, :, None] * freqs, cl[:, :, None] * freqs
    parts["ropecos"] = np.concatenate([np.cos(angr), np.cos(angr), np.cos(angc), np.cos(angc)], -1).reshape(P, -1)
    parts["ropesin"] = np.concatenate([-np.sin(angr), np.sin(angr), -np.sin(angc), np.sin(angc)], -1).reshape(P, -1)
    parts["parity"] = ((p[:, None] // 16) % 2 == (p[None, :] // 64)).astype(np.float64)
    parts["half"] = (p[:, None] // 64 == np.arange(2)[None, :]).astype(np.float64)
    at, cols = 0, []
    for name, a in parts.items():
        CONST[name] = (at, a.shape[1])
        at += a.shape[1]
        cols.append(a)
    return np.ascontiguousarray(np.concatenate(cols, 1).astype(np.float32))


CONST_ARRAY = constants()
NCONST = CONST_ARRAY.shape[1]


class Counts:

    def __init__(self, known):
        self.known, self.names, self.values, self.n = known, {}, {}, {}

    def mark(self, sem, key):
        name = self.names[id(sem)]
        assert (name, key) not in self.values, (name, key)
        self.n[name] = self.values[name, key] = self.n.get(name, 0) + 1
        return 1

    def nth(self, sem, key):
        return 1 if self.known is None else self.known[self.names[id(sem)], key]


def program(nc, A, const, out, known):
    counts = Counts(known)
    mark, nth = counts.mark, counts.nth
    with ExitStack() as ctx:
        def sb(name, shape, dt=F32):
            return ctx.enter_context(nc.sbuf_tensor(name, shape, dt))

        def sem(name):
            return ctx.enter_context(nc.semaphore(name))

        def signal(name):
            s = sem(name)
            counts.names[id(s)] = name
            return s

        K = sb("consts", [P, NCONST])

        def cst(name, a=None, b=None):
            at, n = CONST[name]
            return K[:, at + (a or 0):at + (n if b is None else b)]

        ring = sb("ring", [P, RING, SLOT])
        xT = sb("xT", [P, KD, T])
        hT = sb("hT", [P, KD, 2 * T])
        hN = sb("hN", [P, TT, D])
        packs = sb("packs", [P, 3, P])
        cols = sb("cols", [P, 3, P])
        csil = sb("csil", [P, 24])
        cpair = sb("cpair", [P, KD, 2])
        mod1 = sb("mod1", [P, 48])
        mod2 = sb("mod2", [P, 48, 2])
        gain = sb("gain", [P, 6, KD])
        wr1 = sb("wr1", [P, KD, 36])
        wr2 = sb("wr2", [P, KD, 32])
        rb = sb("rb", [1, 68])
        w2c = sb("w2c", [P, 2, 2, HD])
        gqk = sb("gqk", [P, 2, HD])
        rstd = sb("rstd", [P, 2 * T])
        ARENA = 16100
        arena = sb("arena", [P, ARENA])
        ps = ctx.enter_context(nc.psum_tensor("ps", [P, 8, 512], F32))

        def carve(at, *shape):
            n = int(np.prod(shape))
            assert at + n <= ARENA, (at, n)
            v = arena[:, at:at + n]
            if len(shape) == 2:
                v = v.rearrange("p (a b) -> p a b", b=shape[1])
            if len(shape) == 3:
                v = v.rearrange("p (a b c) -> p a b c", b=shape[1], c=shape[2])
            return v

        class Lay:
            def __init__(self, at=0):
                self.at = at

            def __call__(self, *shape):
                v = carve(self.at, *shape)
                self.at += int(np.prod(shape))
                return v

        L = Lay()
        qT = L(KD, T)
        kslc = L(4, T)
        kwin = L(4, T)
        vslc = L(TT, 256)
        vwin = L(TT, 256)
        gates = L(TT, 48)
        uT = L(4, T)
        kcT = L(60)
        vcN = L(4, HD)
        s_at = L.at
        kcmp = hN[:, 0, :].rearrange("p (g t) -> p g t", t=T)
        vcmp = hN[:, 1, :].rearrange("p (g t) -> p g t", t=T)
        bbT = L(2, 4, P)
        cT = L(2, 4, P)
        yT = L(4, T)
        fr = [L(T), L(T)]
        tabs = [L(2, T), L(2, T)]
        sa = L(2, T)
        sb_ = L(2, T)
        sw = L(2, T)
        sz = L(2, T)
        ss2 = [L(2, T), L(2, T)]
        hid = L(2, 2, 60)
        cbias = L(4)
        small = L(24, 16)
        assert L.at <= ARENA, L.at
        bd = carve(0, 2, 4 * P)
        cR = carve(1024, 2, 4 * P)
        bR = carve(2048, 2, 256)
        bbuf = carve(2560, 2, 256)
        LA = Lay(s_at)
        Eb = [LA(1024), LA(1024)]
        PT = [LA(1024), LA(1024)]
        sgl = LA(2, 2, T)
        mgd = hN[:, :, :].rearrange("p a b -> p (a b)").rearrange("p (k t) -> p k t", t=T)
        yS = LA(4, T)
        oT = LA(KD, T)
        stat = sb("stat", [P, 2, 16])
        rn = sb("rn", [P, 24])
        dt2 = sb("dt2", [P, 2])
        L2 = Lay()
        kaT = L2(4, 2 * T)
        qaT = L2(4, T)
        qbT = L2(4, T)
        kbT = L2(2, 2 * T)
        vN = L2(4, 512)
        vbN = L2(4, P)
        o2 = L2(KD, T)
        at2 = L2.at
        E2 = [L2(1024), L2(1024)]
        PT2 = [L2(1024), L2(1024)]
        nab2 = L2(8, T)
        L3 = Lay(at2)
        qbN = L3(TT, 512)
        qt1 = L3(TT, 512)
        qt2 = L3(TT, 512)
        kbN = L3(4, P)
        kt1 = L3(4, P)
        M = Lay()
        biasB = M(3072)
        xsT = M(KD, SLOTS)
        ohG = M(TT, SLOTS)
        ohS = M(TT, P)
        ohT = M(T)
        glu = M(512)
        lin = M(512)
        sg = M(512)
        act = M(512)
        actT = M(4, P)
        ysS = M(512)
        esel = M(SLOTS)
        zero = M(512)
        lg = M(TT, 36)
        Am = M(TT, E)
        Wt = M(TT, E)
        sel = M(TT, E)
        t1 = M(E * E)
        t2 = M(E * E)
        gx = M(TT, 8)
        m8 = M(TT, 8)
        rt = M(TT, 16)
        crow = M(4, E)
        tabI = sb("tabI", [1, 2, E], I32)

        def wcols(name, a, b):
            w = A[name][:, a:b].rearrange("(k p) c -> p k c", p=P)
            return w

        chunks = []

        def chunk(key, src, *shape):
            chunks.append((key, src, shape))

        for c in range(24):
            chunk(("mod1", c), wcols("ada_w", c * 256, c * 256 + 256), KD, 256)
        IN1 = [("u", 0, 2608), ("u", 1, 2864)] + [("q", c, c * 256) for c in range(4)] + \
              [("kcmp", 0, 1024), ("vcmp", 0, 1280), ("kslc", 0, 1536), ("kwin", 0, 2048),
               ("vslc", 0, 1792), ("vwin", 0, 2304)]
        for n, c, at in IN1:
            chunk((n, c), wcols("w_in", at, at + 256), KD, 256)
        chunk(("ng", 0), wcols("w_in", 2560, 2608), KD, 48)
        for kv in range(2):
            w = A["nsa_cmp_w1"][kv].rearrange("(c p) h -> p c h", p=P)
            for c in range(2):
                chunk(("cw1", kv, c), w[:, 8 * c:8 * c + 8, :], 8, 256)
        chunk(("glu", 0), A["ssm_w_glu"].rearrange("(k p) c -> p k c", p=P), 4, 512)
        for c in range(4):
            chunk(("mga", c), wcols("w_in", 3120 + c * 256, 3376 + c * 256), KD, 256)
            chunk(("mgs", c), wcols("w_in", 4144 + c * 256, 4400 + c * 256), KD, 256)
            chunk(("no", c), wcols("nsa_w_o", c * 256, c * 256 + 256), KD, 256)
            if c % 2 == 0:
                chunk(("so", c // 2), A["ssm_w_o"][:, c * 256:c * 256 + 512].rearrange("(k p) c -> p k c", p=P), 4, 512)
        for c in range(4):
            chunk(("wo", c), wcols("w_out", c * 256, c * 256 + 256), KD, 256)
        n_front1 = len(chunks)
        moe1_at = n_front1
        front2_at = moe1_at + 3 * E
        n1 = len(chunks)
        for c in range(24):
            chunk(("mod2", c), wcols("w_mod_2", c * 256, c * 256 + 256), KD, 256)
        IN2 = [("ka", 0, 0), ("ka", 1, 256), ("va", 0, 512), ("va", 1, 768), ("kvb", 0, 1024),
               ("qa", 0, 1280), ("qa", 1, 1536), ("qb", 0, 1792), ("qb", 1, 2048)]
        for n, c, at in IN2:
            chunk((n + "2", c), wcols("w_in_2", at, at + 256), KD, 256)
        for c in range(4):
            chunk(("ga2", c), wcols("w_in_2", 2304 + c * 256, 2560 + c * 256), KD, 256)
            chunk(("gb2", c), wcols("w_in_2", 3328 + c * 256, 3584 + c * 256), KD, 256)
            if c % 2 == 0:
                for x in "ab":
                    chunk(("oo" + x, c // 2), A["w_out_" + x + "_2"][:, c * 256:c * 256 + 512].rearrange("(k p) c -> p k c", p=P), 4, 512)
        for c in range(4):
            chunk(("w_o2", c), wcols("w_o_2", c * 256, c * 256 + 256), KD, 256)
        moe2_at = front2_at + len(chunks) - n1
        index = {}
        for i, (key, _, _) in enumerate(chunks):
            index[key] = i if i < n1 else front2_at + i - n1

        full = [sem(f"ring_full{s}") for s in range(RING)]
        freed = sem("ring_freed")

        def slot_ap(i, shape):
            v = ring[:, i % RING, 0:int(np.prod(shape))]
            return v.rearrange("p (a b) -> p a b", b=shape[1])

        def weights(eng, key):
            i = index[key]
            eng.wait_ge(full[i % RING], 16 * (i // RING + 1))
            return slot_ap(i, chunks[i if i < n1 else i - front2_at + n1][2])

        def load(sp, key, i, src, shape):
            if i >= RING:
                sp.wait_ge(freed, i - RING + 1)
            sp.dma_start(slot_ap(i, shape), src).then_inc(full[i % RING], 16)

        small_in = sem("small_in")
        ctx_in = sem("ctx_in")
        bias_in = [sem("bias_in0"), sem("bias_in1")]
        biasb_in = sem("expert_biases_in")
        xin = sem("x_in")
        filled = signal("psum_filled")
        emptied = signal("psum_emptied")
        vemptied = signal("psum_emptied_by_vector")
        madeV = signal("made_by_vector")
        madeA = signal("made_by_scalar")
        out_sem = sem("out_stored")
        STEPS = ("onehot", "gathered", "xs", "spreadT", "spread", "hidden", "glu", "sig", "act", "turned",
                 "actT", "down", "ys", "scattered")
        S = {(n, kind): {x: sem(f"moe{n}_{kind}_{x}") for x in STEPS} for n in (1, 2) for kind in ("first", "more")}

        def run_experts(eng, n, body):
            U = 4 if n == 1 else 1
            with eng.Fori(0, E // U) as it:
                for u in range(U):
                    e = it * U + u
                    more = eng.value_load(tabI[0:1, 0, bass.ds(e, 1)], min_val=0, max_val=MAXB - 1)
                    before = eng.value_load(tabI[0:1, 1, bass.ds(e, 1)], min_val=0, max_val=E * (MAXB - 1))
                    with eng.If(more > 0):
                        with eng.Fori(0, more) as b:
                            body(it, u, e, S[n, "more"], before + b, b + 1, False)
                    body(it, u, e, S[n, "first"], e, 0, True)

        block = ctx.enter_context(nc.Block())
        pending = [0]

        def mm(*a, start, stop, **k):
            ins = nc.tensor.matmul(*a, start=start, stop=stop, **k)
            if pending[0] and start and not stop:
                ins.then_inc(freed, pending[0])
                pending[0] = 0
            return ins


        @block.sync
        def _(sp):
            sp.dma_start(K[:, :], const[:, :]).then_inc(xin, 16)
            sp.dma_start(hN[:, :, :], A["x"].rearrange("(a p) d -> p a d", p=P)).then_inc(xin, 16)
            for i in range(n1):
                key, src, shape = chunks[i]
                load(sp, key, i, src, shape)
            with sp.Fori(0, E // 4) as it:
                for u in range(4):
                    e = it * 4 + u
                    for j, nm in enumerate(("gate", "up", "down")):
                        i = moe1_at + 3 * u + j
                        sp.wait_ge(freed, it * 12 + (i - RING + 1))
                        w = A["moe_w_" + nm][bass.ds(e, 1)]
                        if j < 2:
                            src = w.rearrange("e (k p) c -> p (e k) c", p=P)
                            dst = slot_ap(i, (KD, 256))
                        else:
                            src = w.rearrange("e (k p) c -> p (e k) c", p=P)
                            dst = slot_ap(i, (2, D))
                        sp.dma_start(dst, src).then_inc(full[i % RING], 16)
            for i in range(n1, len(chunks)):
                key, src, shape = chunks[i]
                load(sp, key, index[key], src, shape)
            with sp.Fori(0, E) as e:
                for j in range(12):
                    i = moe2_at + j
                    sp.wait_ge(freed, e * 12 + (i - RING + 1))
                    if j < 8:
                        src = A["w_gu_2"][bass.ds(e, 1), j * P:(j + 1) * P, :].rearrange("e p c -> p (e c)")
                        sp.dma_start(ring[:, i % RING, :], src).then_inc(full[i % RING], 16)
                    else:
                        j2 = j - 8
                        src = A["w_dn_2"][bass.ds(e, 1), j2 * 256:(j2 + 1) * 256, :].rearrange("e (k p) c -> p (e k) c", p=P)
                        sp.dma_start(slot_ap(i, (2, D)), src).then_inc(full[i % RING], 16)
            sp.wait_ge(madeA, nth(madeA, "out"))
            for a in range(TT):
                sp.dma_start(out.rearrange("(a p) d -> p a d", p=P)[:, a, :], hN[:, a, :]).then_inc(out_sem, 16)
            sp.wait_ge(out_sem, 16 * TT)

        smalls = []

        def rows(pk, at, src, n):
            smalls.append((packs[at:at + n, pk, :], src.rearrange("(r c) -> r c", c=P)))

        rows(0, 0, A["ada_b"], 48)
        rows(0, 48, A["norm1_g"], 8)
        rows(0, 56, A["norm2_g"], 8)
        rows(0, 64, A["final_g"], 8)
        rows(0, 72, A["nsa_cmp_pos"].rearrange("a l h -> (a l h)"), 32)
        rows(0, 104, A["c"].rearrange("a d -> (a d)"), 8)
        rows(0, 112, A["c_2"].rearrange("a d -> (a d)"), 8)
        rows(0, 120, A["c_ctx_2"], 8)
        rows(1, 0, A["b_mod_2"], 48)
        for n, k in enumerate(("g_pre_mix_2", "g_post_mix_2", "g_pre_ffn_2", "g_post_ffn_2")):
            rows(1, 48 + 8 * n, A[k], 8)
        rows(2, 0, A["ssm_lam_re"].rearrange("g p -> (g p)"), 16)
        rows(2, 16, A["ssm_lam_im"].rearrange("g p -> (g p)"), 16)
        ldt = A["ssm_log_dt"].rearrange("(j s) -> j s", s=2)
        smalls.append((dt2[32:48, :], ldt))
        rows(2, 48, A["ssm_d"].rearrange("g h -> (g h)"), 4)
        smalls.append((packs[80:128, 1, :], A["ada_b"].rearrange("(r c) -> r c", c=P)))
        smalls.append((packs[52:128, 2, :], const[0:76, 0:P]))
        for n, k in enumerate(("ssm_b_re", "ssm_b_im")):
            smalls.append((bR[:, n, :].rearrange("p (j h) -> p j h", h=16),
                           A[k].rearrange("g p h -> (g p) h").rearrange("(j q) h -> q j h", q=P)))
        for n, k in enumerate(("ssm_c_re", "ssm_c_im")):
            src = A[k].rearrange("g h p -> (g h) p").rearrange("(t q) p -> q t p", q=P)
            dst = cR[:, n, :].rearrange("p (t s c) -> p t s c", t=4, s=2)
            smalls += [(dst[:, :, 0, :], src), (dst[:, :, 1, :], src)]
        smalls.append((wr1[:, :, 0:4], A["moe_w_group"].rearrange("(k p) c -> p k c", p=P)))
        smalls.append((wr1[:, :, 4:36], A["moe_w_expert"].rearrange("(k p) c -> p k c", p=P)))
        smalls.append((wr2[:, :, :], A["w_router_2"].rearrange("(k p) c -> p k c", p=P)))
        smalls.append((rb[:, 0:4], A["moe_b_group"].rearrange("(a c) -> a c", a=1)))
        smalls.append((rb[:, 4:36], A["moe_b_expert"].rearrange("(a c) -> a c", a=1)))
        smalls.append((rb[:, 36:68], A["b_router_2"].rearrange("(a c) -> a c", a=1)))
        for kv in range(2):
            smalls.append((w2c[:, kv, :, :], A["nsa_cmp_w2"][kv].rearrange("(k p) c -> p k c", p=P)))
        for n, k in enumerate(("g_qnorm_2", "g_knorm_2")):
            smalls.append((gqk[:, n, :], A[k][None, :].broadcast_to([P, HD])))
        SMALL = 16 * len(smalls)

        @block.gpsimd
        def _(g):
            for dst, src in smalls:
                g.dma_start(dst, src).then_inc(small_in, 16)
            g.wait_ge(madeV, nth(madeV, "moe1 out"))
            g.dma_start(hN[:, :, :], A["ctx_2"].rearrange("(a p) d -> p a d", p=P)).then_inc(ctx_in, 16)
            for tt in range(TT):
                if tt == 1:
                    g.wait_ge(filled, nth(filled, ("S", 2, 3)))
                for h in range(8):
                    for r in range(2):
                        row = 2 * tt + r
                        src = bass.AP(tensor=A["rpb_2"].tensor, offset=h * 465 + (7 - row) * 31 + 15 - 63,
                                      ap=[[1, 64], [31, 4], [1, 64]])
                        g.dma_start(nab2[64 * r:64 * r + 64, h, :].rearrange("p (a b) -> p a b", b=64), src).then_inc(bias_in[tt], 16)
            g.wait_ge(madeV, nth(madeV, "biasB"))
            g.dma_start(biasB[0:E, 0:2048], A["b_gu_2"]).then_inc(biasb_in, 16)
            g.dma_start(biasB[0:E, 2048:3072], A["b_dn_2"]).then_inc(biasb_in, 16)

        units1 = [(g, tt, a) for g in range(4) for tt in range(TT) for a in ("cmp", "slc", "win")]
        units2 = [(a, hp, tt) for tt in range(TT) for a in ("na", "gqa") for hp in range(4)]

        @block.tensor
        def _(pe):
            ident = cst("ident")
            ones = cst("ones")

            def free_chunk(ins):
                ins.then_inc(freed, 1)

            def transpose(dst, src):
                return nc.tensor.transpose(dst, src, ident[0:src.shape[0], 0:src.shape[0]])

            pe.wait_ge(xin, 32)
            for tt in range(TT):
                for k in range(KD):
                    last = transpose(ps[:, 1 + tt * 2 + k // 4, (k % 4) * P:(k % 4 + 1) * P], hN[:, tt, k * P:(k + 1) * P])
            last.then_inc(filled, mark(filled, "x"))
            pe.wait_ge(small_in, SMALL)
            pe.wait_ge(madeV, nth(madeV, "dt rows"))
            for n in range(3):
                last = transpose(ps[:, 0, n * P:(n + 1) * P], packs[:, n, :])
            last.then_inc(filled, mark(filled, "cols"))

            def sumsq(key, bank, sq, n=T):
                pe.wait_ge(madeA, nth(madeA, ("sq", key)))
                for k in range(KD):
                    last = mm(ps[:, bank, 0:n], ones, sq[:, k, :], start=k == 0, stop=k == KD - 1)
                last.then_inc(filled, mark(filled, ("ss", key)))

            sumsq("n1", 5, hT[:, :, T:2 * T])
            pe.wait_ge(madeV, nth(madeV, "csil"))
            for c in range(24):
                w = weights(pe, ("mod1", c))
                for m in range(2):
                    for k in range(KD):
                        last = mm(ps[:, 6, 2 * c + m:2 * c + m + 1], w[:, k, m * P:(m + 1) * P], csil[:, k:k + 1],
                                  start=k == 0, stop=k == KD - 1)
                free_chunk(last)
            last = mm(ps[:, 7, 0:1], ones, csil[:, 0:1], start=True, stop=True)
            last.then_inc(filled, mark(filled, "mod1"))
            pe.wait_ge(madeV, nth(madeV, "bd"))
            for n in range(2):
                for q in range(4):
                    last = transpose(ps[:, 4 + n, q * P:(q + 1) * P], bd[:, n, q * P:(q + 1) * P])
            last.then_inc(filled, mark(filled, "bbT"))
            for n in range(2):
                for q in range(4):
                    last = transpose(ps[:, n, q * P:(q + 1) * P], cR[:, n, q * P:(q + 1) * P])
            last.then_inc(filled, mark(filled, "cT"))

            pe.wait_ge(madeV, nth(madeV, "h1"))
            turn = [0]

            def take_bank():
                b = turn[0] % 4
                g = turn[0]
                if g >= 4:
                    pe.wait_ge(emptied, nth(emptied, ("p1", g - 4)))
                else:
                    pe.wait_ge(emptied, nth(emptied, "cT"))
                turn[0] += 1
                return b, g

            def projT(key, c):
                w = weights(pe, (key, c))
                b, g = take_bank()
                for m in range(2):
                    for k in range(KD):
                        last = mm(ps[:, b, m * T:(m + 1) * T], w[:, k, m * P:(m + 1) * P], hT[:, k, 0:T],
                                  start=k == 0, stop=k == KD - 1)
                last.then_inc(filled, mark(filled, ("p1", g)))
                return last

            def projdup(key, half, last_half=True):
                w = weights(pe, (key, 0))
                b, g = take_bank()
                for m in range(2):
                    gg = 2 * half + m
                    for k in range(KD):
                        for s in range(2):
                            last = mm(ps[64 * s:64 * s + 64, b, m * T:(m + 1) * T], w[:, k, gg * 64:gg * 64 + 64],
                                      hT[:, k, 0:T], start=k == 0, stop=k == KD - 1)
                last.then_inc(filled, mark(filled, ("p1", g)))

            def projN(key, n):
                w = weights(pe, (key, 0))
                b, g = take_bank()
                for tt in range(TT):
                    for k in range(KD):
                        last = mm(ps[:, b, tt * n:(tt + 1) * n], hT[:, k, tt * P:(tt + 1) * P], w[:, k, :],
                                  start=k == 0, stop=k == KD - 1)
                last.then_inc(filled, mark(filled, ("p1", g)))

            def ssm_in(j):
                if j >= 2:
                    pe.wait_ge(vemptied, nth(vemptied, ("bu", j - 2)))
                elif j == 0:
                    pe.wait_ge(emptied, nth(emptied, ("p1", 1)))
                q, r = j // 4, 32 * (j % 4)
                for n in range(2):
                    last = mm(ps[:, 4 + j % 2, n * T:(n + 1) * T], bbT[r:r + 32, n, q, :], uT[r:r + 32, q, :],
                              start=True, stop=True)
                last.then_inc(filled, mark(filled, ("bu", j)))

            def ssm_out(j):
                pe.wait_ge(madeV, nth(madeV, ("s", j)))
                q, r = j // 4, 32 * (j % 4)
                for n in range(2):
                    last = mm(ps[r:r + 32, 6 + q // 2, (q % 2) * T:(q % 2 + 1) * T], cT[:, n, q, r:r + 32],
                              ss2[j % 2][:, n, :], start=n == 0, stop=n == 1)
                last.then_inc(filled, mark(filled, ("y", j)))

            done_j = [0, 0]

            def ssm_step():
                if done_j[0] < 16:
                    ssm_in(done_j[0])
                    done_j[0] += 1
                if done_j[0] >= 3 and done_j[1] < 16:
                    ssm_out(done_j[1])
                    done_j[1] += 1

            def freeing(n=1):
                pending[0] += n

            for n, c, _ in IN1:
                if n in ("u", "q"):
                    projT(n, c)
                elif n in ("kcmp", "vcmp", "kslc", "kwin"):
                    projdup(n, 0)
                    ssm_step()
                    projdup(n, 1)
                else:
                    projN(n, 256)
                freeing()
                if n != "u":
                    ssm_step()
            projN("ng", 48)
            freeing()
            pe.wait_ge(emptied, nth(emptied, ("p1", turn[0] - 1)))
            for kv in range(2):
                src = (kcmp, vcmp)[kv]
                w = [weights(pe, ("cw1", kv, c)) for c in range(2)]
                for m in range(2):
                    for c in range(16):
                        last = mm(ps[:, kv, m * 60:(m + 1) * 60], w[c // 8][:, c % 8, m * P:(m + 1) * P],
                                  src[:, :, 2 * c:2 * c + 16 * 14 + 1:16], start=c == 0, stop=c == 15)
                for m in range(2):
                    for c in range(16):
                        last = mm(ps[:, kv, 128 + m:129 + m], w[c // 8][:, c % 8, m * P:(m + 1) * P],
                                  cols[:, 0, 72 + 16 * kv + c:73 + 16 * kv + c], start=c == 0, stop=c == 15)
                last.then_inc(filled, mark(filled, ("hid", kv)))
                freeing(2)
            while done_j[1] < 16:
                ssm_step()
            pe.wait_ge(madeA, nth(madeA, "hid"))
            for s in range(2):
                for m in range(2):
                    last = mm(ps[64 * s:64 * s + 64, 2, 0:60], w2c[:, 0, m, :], hid[:, 0, m, :], start=m == 0, stop=m == 1)
            for g in range(4):
                for m in range(2):
                    last = mm(ps[0:NCMP, 3, g * HD:(g + 1) * HD], hid[:, 1, m, g * NCMP:(g + 1) * NCMP], w2c[:, 1, m, :],
                              start=m == 0, stop=m == 1)
            last.then_inc(filled, mark(filled, "kc"))
            pe.wait_ge(madeA, nth(madeA, "ygelu"))
            w = weights(pe, ("glu", 0))
            for m in range(4):
                for k in range(4):
                    last = mm(ps[:, 4 + m // 2, (m % 2) * T:(m % 2 + 1) * T], w[:, k, m * P:(m + 1) * P], yT[:, k, :],
                              start=k == 0, stop=k == 3)
            last.then_inc(filled, mark(filled, "z"))
            freeing()

            def seg(n, u):
                if n == 1:
                    g, tt, a = u
                    return (4, 16 if a == "cmp" else P * (tt + 1))
                return (2, 512)

            def scores(n, i, u):
                b = 2 * (i % 2)
                if i >= 2:
                    pe.wait_ge(madeA, nth(madeA, ("exp", n, i - 2)))
                if n == 1:
                    g, tt, a = u
                    nk = seg(1, u)[1]
                    for s in range(4):
                        par, half = s // 2, s % 2
                        hb = 64 * par
                        q = qT[hb:hb + 64, 2 * g + half, tt * P:(tt + 1) * P]
                        o = ps[:, b + par, half * nk:(half + 1) * nk]
                        if a == "cmp":
                            o = o[:, 0:NCMP]
                            mm(o, q, kcT[hb:hb + 64, g * NCMP:(g + 1) * NCMP], start=True, stop=False)
                            last = mm(o, ident, cst("cmpmask", tt * NCMP, (tt + 1) * NCMP), start=False, stop=True)
                        else:
                            kk = (kslc if a == "slc" else kwin)[hb:hb + 64, g, 0:nk]
                            mm(o, q, kk, start=True, stop=True)
                            last = mm(o[:, nk - P:nk], ident, cst("causal"), start=False, stop=True, skip_group_check=True)
                else:
                    a, hp, tt = u
                    for s in range(2):
                        q = (qaT if a == "na" else qbT)[64 * s:64 * s + 64, hp, tt * P:(tt + 1) * P]
                        kk = kaT[64 * s:64 * s + 64, hp, :] if a == "na" else kbT[64 * s:64 * s + 64, hp // 2, :]
                        o = ps[:, b + s, :]
                        last = mm(o, q, kk, start=True, stop=True)
                        if a == "na":
                            last = mm(o[:, 0:T], cst("mirror"), nab2[:, 2 * hp + s, :], start=False, stop=True, skip_group_check=True)
                last.then_inc(filled, mark(filled, ("S", n, i)))

            def turned(n, i, u):
                pe.wait_ge(madeV, nth(madeV, ("P", n, i)))
                if i >= 1:
                    pe.wait_ge(madeA, nth(madeA, ("PT", n, i - 1)))
                E_ = (Eb if n == 1 else E2)[i % 2]
                ns, nk = seg(n, u)
                if nk == 16:
                    for s in range(ns):
                        last = nc.tensor.transpose(ps[0:NCMP, 4, s * P:(s + 1) * P], E_[:, s * 16:s * 16 + NCMP], ident)
                else:
                    for kb in range(nk // P):
                        for s in range(ns):
                            x = kb * ns + s
                            last = transpose(ps[:, 4 + x // 4, (x % 4) * P:(x % 4 + 1) * P], E_[:, s * nk + kb * P:s * nk + (kb + 1) * P])
                last.then_inc(filled, mark(filled, ("T", n, i)))

            def values(n, i, u):
                pe.wait_ge(madeA, nth(madeA, ("PT", n, i)))
                ns, nk = seg(n, u)
                pt = (PT if n == 1 else PT2)[i % 2].rearrange("p (k s q) -> p k s q", s=ns, q=P)
                if n == 1:
                    g, tt, a = u
                    if a == "cmp" and i >= 3:
                        pe.wait_ge(emptied, nth(emptied, ("O", n, i - 1)))
                    for par in range(2):
                        o = ps[64 * par:64 * par + 64, 6, 0:2 * P]
                        if a == "cmp":
                            last = mm(o, vcN[0:NCMP, g, :], pt[0:NCMP, 0, 2 * par:2 * par + 2, :], start=True, stop=False, skip_group_check=True)
                        else:
                            v = vslc if a == "slc" else vwin
                            for kb in range(nk // P):
                                last = mm(o, v[:, kb, g * HD:(g + 1) * HD], pt[:, kb, 2 * par:2 * par + 2, :], start=False,
                                          stop=a == "win" and kb == nk // P - 1, skip_group_check=True)
                    last.then_inc(filled, mark(filled, ("O", n, i)))
                else:
                    a, hp, tt = u
                    if i >= 1:
                        pe.wait_ge(emptied, nth(emptied, ("O", n, i - 1)))
                    for par in range(2):
                        o = ps[64 * par:64 * par + 64, 6, 0:P]
                        for kb in range(4):
                            h = 2 * hp + par
                            v = vN[:, kb, h * HD:(h + 1) * HD] if a == "na" else vbN[:, kb, (hp // 2) * HD:(hp // 2 + 1) * HD]
                            last = mm(o, v, pt[:, kb, par, :], start=kb == 0, stop=kb == 3)
                    last.then_inc(filled, mark(filled, ("O", n, i)))

            def attention(n, units):
                scores(n, 0, units[0])
                for i, u in enumerate(units):
                    if i + 1 < len(units):
                        if n == 2 and units[i + 1] == ("na", 0, 1):
                            pe.wait_ge(madeV, nth(madeV, ("bias", 1)))
                        scores(n, i + 1, units[i + 1])
                    turned(n, i, u)
                    values(n, i, u)

            pe.wait_ge(madeA, nth(madeA, "kc"))
            pe.wait_ge(madeA, nth(madeA, "ysig"))
            attention(1, units1)

            pe.wait_ge(emptied, nth(emptied, ("O", 1, len(units1) - 1)))
            pe.wait_ge(madeV, nth(madeV, "yS"))
            so = None
            for c in range(4):
                if c >= 1:
                    pe.wait_ge(madeV, nth(madeV, ("mgd", c - 1)))
                if c % 2 == 0:
                    so = weights(pe, ("so", c // 2))
                for n, key in enumerate(("mga", "mgs")):
                    w = weights(pe, (key, c))
                    for m in range(2):
                        for k in range(KD):
                            last = mm(ps[:, 2 + n, m * T:(m + 1) * T], w[:, k, m * P:(m + 1) * P], hT[:, k, 0:T],
                                      start=k == 0, stop=k == KD - 1)
                last.then_inc(filled, mark(filled, ("gates", c)))
                w = weights(pe, ("no", c))
                for m in range(2):
                    for k in range(KD):
                        last = mm(ps[:, 0, m * T:(m + 1) * T], w[:, k, m * P:(m + 1) * P], oT[:, k, :],
                                  start=k == 0, stop=k == KD - 1)
                for m in range(2):
                    mc = (c % 2) * 2 + m
                    for k in range(4):
                        last = mm(ps[:, 1, m * T:(m + 1) * T], so[:, k, mc * P:(mc + 1) * P], yS[:, k, :],
                                  start=k == 0, stop=k == 3)
                last.then_inc(filled, mark(filled, ("branch", c)))
                freeing(3 if c % 2 == 0 else 4)
            for c in range(4):
                if c == 0:
                    pe.wait_ge(madeV, nth(madeV, ("mgd", 3)))
                w = weights(pe, ("wo", c))
                for m in range(2):
                    for k in range(KD):
                        last = mm(ps[:, 4 + c, m * T:(m + 1) * T] if c < 4 else None, w[:, k, m * P:(m + 1) * P], mgd[:, k, :],
                                  start=k == 0, stop=k == KD - 1)
                last.then_inc(filled, mark(filled, ("tm", c)))
                freeing()

            def moe_front(n, wr, nr, rbias):
                key = f"f{n}"
                sumsq(key, 0, hT[:, :, T:2 * T])
                pe.wait_ge(madeV, nth(madeV, "h" + key))
                for tt in range(TT):
                    for k in range(KD):
                        last = transpose(ps[:, 1 + tt * 2 + k // 4, (k % 4) * P:(k % 4 + 1) * P], hT[:, k, tt * P:(tt + 1) * P])
                last.then_inc(filled, mark(filled, "hN" + key))
                for tt in range(TT):
                    for k in range(KD):
                        mm(ps[:, 5, tt * 64:tt * 64 + nr], hT[:, k, tt * P:(tt + 1) * P], wr[:, k, :], start=k == 0, stop=False)
                    last = mm(ps[:, 5, tt * 64:tt * 64 + nr], ones[0:1, :], rbias, start=False, stop=True)
                last.then_inc(filled, mark(filled, "logits" + key))
                pe.wait_ge(madeV, nth(madeV, "chosen" + key))
                for tt in range(TT):
                    mm(ps[:, 5, 128 + tt * E:128 + (tt + 1) * E], cst("before"), Am[:, tt, :], start=True, stop=tt == 0)
                    if tt == 1:
                        last = mm(ps[:, 5, 128 + E:128 + 2 * E], ones, Am[:, 0, :], start=False, stop=True)
                for tt in range(TT):
                    last = mm(ps[0:1, 5, 256:256 + E], ones[:, 0:1], Am[:, tt, :], start=tt == 0, stop=tt == 1)
                last.then_inc(filled, mark(filled, "places" + key))
                pe.wait_ge(madeV, nth(madeV, "tables" + key))
                for b in range(4):
                    last = mm(ps[:, 4 + b, :], zero[:, 0:P], zero, start=True, stop=True)
                last.then_inc(filled, mark(filled, "zeroed" + key))

            def expert(n, s, q, wg, wd, final):
                pe.wait_ge(s["onehot"], q + 1)
                for k in range(KD):
                    for tt in range(TT):
                        last = mm(ps[:, 0, k * SLOTS:(k + 1) * SLOTS], hN[:, tt, k * P:(k + 1) * P], ohG[:, tt, :],
                                  start=tt == 0, stop=tt == 1)
                last.then_inc(s["gathered"], 1)
                pe.wait_ge(s["xs"], q + 1)
                for tt in range(TT):
                    last = transpose(ps[:, 0, tt * P:(tt + 1) * P], ohS[:, tt, :])
                last.then_inc(s["spreadT"], 1)
                for k in range(KD):
                    wg(k, s)
                pe.wait_ge(s["act"], q + 1)
                nt = 4 if n == 2 else 1
                for j in range(nt):
                    last = transpose(ps[:, 3, j * P:(j + 1) * P], act[:, j * P:(j + 1) * P])
                last.then_inc(s["turned"], 1)
                pe.wait_ge(s["actT"], q + 1)
                wd(s)
                pe.wait_ge(s["ys"], q + 1)
                pe.wait_ge(s["spread"], q + 1)
                for c in (0, 4, 1, 5, 2, 6, 3, 7):
                    r = 64 * (c // 4)
                    if c == 4 and final:
                        last.then_inc(freed, 1)
                    last = mm(ps[:, 4 + c // 2, (c % 2) * T:(c % 2 + 1) * T], ysS[r:r + 64, (c % 4) * P:(c % 4 + 1) * P],
                              ohT[r:r + 64, :], start=False, stop=False, skip_group_check=True)
                last.then_inc(s["scattered"], 1)

            def expert1(e, u, it, s, q, final):
                i = moe1_at + 3 * u
                tile = [slot_ap(i, (KD, 256)), slot_ap(i + 1, (KD, 256)), slot_ap(i + 2, (2, D))]

                def ready(j):
                    pe.wait_ge(full[(i + j) % RING], it * 16 + 16 * ((i + j) // RING + 1))

                def wg(k, s):
                    if k == 0:
                        ready(0)
                        ready(1)
                    for r in range(2):
                        for n, w in enumerate(tile[:2]):
                            last = mm(ps[64 * r:64 * r + 64, 1 + n, 0:P], xsT[:, k, :], w[:, k, r * P:(r + 1) * P],
                                      start=k == 0, stop=k == KD - 1)
                    if k == KD - 1:
                        last.then_inc(s["hidden"], 1)
                        if final:
                            pending[0] += 2

                def wd(s):
                    ready(2)
                    for f in range(2):
                        for r in range(2):
                            last = mm(ps[64 * r:64 * r + 64, 3, :], actT[:, 0, f * 64:(f + 1) * 64], tile[2][:, f, r * 512:(r + 1) * 512],
                                      start=f == 0, stop=f == 1)
                    last.then_inc(s["down"], 1)
                expert(1, s, q, wg, wd, final)

            def expert2(e, s, q, final):
                def ready(j):
                    i = moe2_at + j
                    pe.wait_ge(full[i % RING], e * 16 + 16 * (i // RING + 1))
                    return slot_ap(i, (2, D))

                def wg(k, s):
                    if k == 0:
                        for n in range(2):
                            for r in range(2):
                                mm(ps[64 * r:64 * r + 64, 1 + n, :], esel, biasB[:, n * D + r * 512:n * D + (r + 1) * 512],
                                   start=True, stop=False)
                    w = ready(k)
                    for n in range(2):
                        for r in range(2):
                            last = mm(ps[64 * r:64 * r + 64, 1 + n, :], xsT[:, k, :], w[:, n, r * 512:(r + 1) * 512],
                                      start=False, stop=k == KD - 1)
                    if k == KD - 1:
                        last.then_inc(s["hidden"], 1)
                        if final:
                            pending[0] += 1
                    elif final:
                        last.then_inc(freed, 1)

                def wd(s):
                    for r in range(2):
                        mm(ps[64 * r:64 * r + 64, 3, :], esel, biasB[:, 2048 + r * 512:2048 + (r + 1) * 512], start=True, stop=False)
                    for f in range(8):
                        w = ready(8 + f // 2)
                        for r in range(2):
                            last = mm(ps[64 * r:64 * r + 64, 3, :], actT[:, f % 4, (f // 4) * 64:(f // 4 + 1) * 64],
                                      w[:, f % 2, r * 512:(r + 1) * 512], start=False, stop=f == 7)
                        if final and f % 2 == 1 and f < 7:
                            last.then_inc(freed, 1)
                    last.then_inc(s["down"], 1)
                expert(2, s, q, wg, wd, final)

            moe_front(1, wr1, 36, rb[0:1, 0:36])
            run_experts(pe, 1, lambda it, u, e, s, q, b, final: expert1(e, u, it, s, q, final))

            last = mm(ps[:, 0, 0:1], ones, csil[:, 0:1], start=True, stop=True)
            last.then_inc(filled, mark(filled, "moe1"))
            sumsq("fin", 0, hT[:, :, T:2 * T])
            for c in range(24):
                w = weights(pe, ("mod2", c))
                for m in range(2):
                    for k in range(KD):
                        mcol = 2 * (2 * c + m)
                        last = mm(ps[:, 6, mcol:mcol + 2], w[:, k, m * P:(m + 1) * P], cpair[:, k, :],
                                  start=k == 0, stop=k == KD - 1)
                free_chunk(last)
            last = mm(ps[:, 7, 0:1], ones, csil[:, 0:1], start=True, stop=True)
            last.then_inc(filled, mark(filled, "mod2"))
            sumsq("n2", 0, hT[:, :, T:2 * T])
            pe.wait_ge(ctx_in, 16)
            for tt in range(TT):
                for k in range(KD):
                    last = transpose(ps[:, 1 + tt * 2 + k // 4, (k % 4) * P:(k % 4 + 1) * P], hN[:, tt, k * P:(k + 1) * P])
            last.then_inc(filled, mark(filled, "ctx"))
            pe.wait_ge(madeA, nth(madeA, ("sq", "ctx")))
            for k in range(KD):
                last = mm(ps[:, 5, 0:T], ones, mgd[:, k, :], start=k == 0, stop=k == KD - 1)
            last.then_inc(filled, mark(filled, ("ss", "ctx")))
            pe.wait_ge(madeV, nth(madeV, "h2"))
            pe.wait_ge(madeV, nth(madeV, "hctx"))
            turn2 = [0]

            def bank2():
                g = turn2[0]
                if g >= 4:
                    pe.wait_ge(emptied, nth(emptied, ("p2", g - 4)))
                turn2[0] += 1
                return g % 4, g

            def fill2(outs):
                b, g = bank2()
                for o, lhs, rhs in outs:
                    for k in range(KD):
                        last = mm(o(b), lhs(k), rhs(k), start=k == 0, stop=k == KD - 1)
                last.then_inc(filled, mark(filled, ("p2", g)))

            for c in range(2):
                w = weights(pe, ("ka2", c))
                for m in range(2):
                    fill2([(lambda b: ps[:, b, :], lambda k, m=m: w[:, k, m * P:(m + 1) * P], lambda k: hT[:, k, :])])
                freeing()
            for c in range(2):
                w = weights(pe, ("va2", c))
                for h in range(2):
                    fill2([(lambda b, x=x: ps[:, b, x * 256:(x + 1) * 256],
                            lambda k, x=x, h=h: hT[:, k, (2 * h + x) * P:(2 * h + x + 1) * P], lambda k: w[:, k, :]) for x in range(2)])
                freeing()
            w = weights(pe, ("kvb2", 0))
            for h in range(2):
                fill2([(lambda b, x=x: ps[:, b, x * 256:(x + 1) * 256],
                        lambda k, x=x, h=h: hT[:, k, (2 * h + x) * P:(2 * h + x + 1) * P], lambda k: w[:, k, :]) for x in range(2)])
            freeing()
            for c in range(2):
                w = weights(pe, ("qa2", c))
                fill2([(lambda b, m=m: ps[:, b, m * T:(m + 1) * T], lambda k, m=m: w[:, k, m * P:(m + 1) * P],
                        lambda k: hT[:, k, 0:T]) for m in range(2)])
                freeing()
            for c in range(2):
                w = weights(pe, ("qb2", c))
                fill2([(lambda b, x=x: ps[:, b, x * 256:(x + 1) * 256],
                        lambda k, x=x: hT[:, k, x * P:(x + 1) * P], lambda k: w[:, k, :]) for x in range(2)])
                freeing()
            pe.wait_ge(madeV, nth(madeV, "rope"))
            for tt in range(TT):
                for m in range(4):
                    x = m * TT + tt
                    last = transpose(ps[:, 4 + x // 4, (x % 4) * P:(x % 4 + 1) * P], qbN[:, tt, m * P:(m + 1) * P])
            last.then_inc(filled, mark(filled, "qbT"))
            for kb in range(4):
                last = transpose(ps[:, 6, kb * P:(kb + 1) * P], kbN[:, kb, :])
            for kb in range(4):
                last = transpose(ps[:, 7, kb * P:(kb + 1) * P], kt1[:, kb, :])
            last.then_inc(filled, mark(filled, "kbT"))
            pe.wait_ge(emptied, nth(emptied, "kbT"))
            pe.wait_ge(emptied, nth(emptied, ("p2", turn2[0] - 1)))
            pe.wait_ge(madeV, nth(madeV, ("bias", 0)))
            attention(2, units2)
            pe.wait_ge(emptied, nth(emptied, ("O", 2, len(units2) - 1)))
            for c in range(4):
                if c >= 1:
                    pe.wait_ge(madeV, nth(madeV, ("mgd2", c - 1)))
                for n, key in enumerate(("ga2", "gb2")):
                    w = weights(pe, (key, c))
                    for m in range(2):
                        for k in range(KD):
                            last = mm(ps[:, 2 + n, m * T:(m + 1) * T], w[:, k, m * P:(m + 1) * P], hT[:, k, 0:T],
                                      start=k == 0, stop=k == KD - 1)
                last.then_inc(filled, mark(filled, ("gates2", c)))
                if c % 2 == 0:
                    oo = [weights(pe, ("oo" + x, c // 2)) for x in "ab"]
                for n in range(2):
                    for m in range(2):
                        mc = (c % 2) * 2 + m
                        for k in range(4):
                            last = mm(ps[:, n, m * T:(m + 1) * T], oo[n][:, k, mc * P:(mc + 1) * P], o2[:, 4 * n + k, :],
                                      start=k == 0, stop=k == 3)
                last.then_inc(filled, mark(filled, ("branch2", c)))
                freeing(2 if c % 2 == 0 else 4)
            for c in range(4):
                if c == 0:
                    pe.wait_ge(madeV, nth(madeV, ("mgd2", 3)))
                w = weights(pe, ("w_o2", c))
                for m in range(2):
                    for k in range(KD):
                        last = mm(ps[:, 4 + c, m * T:(m + 1) * T], w[:, k, m * P:(m + 1) * P], mgd[:, k, :],
                                  start=k == 0, stop=k == KD - 1)
                last.then_inc(filled, mark(filled, ("y2", c)))
                freeing()
            sumsq("post", 0, hT[:, :, T:2 * T])
            moe_front(2, wr2, 32, rb[0:1, 36:68])
            pe.wait_ge(biasb_in, 32)
            run_experts(pe, 2, lambda it, u, e, s, q, b, final: expert2(e, s, q, final))
            last = mm(ps[:, 0, 0:1], ones, csil[:, 0:1], start=True, stop=True)
            last.then_inc(filled, mark(filled, "moe2"))
            sumsq("postf", 0, hT[:, :, T:2 * T])
            pe.wait_ge(madeV, nth(madeV, "xout"))
            for tt in range(TT):
                for k in range(KD):
                    last = transpose(ps[:, 1 + tt * 2 + k // 4, (k % 4) * P:(k % 4 + 1) * P], xT[:, k, tt * P:(tt + 1) * P])
            last.then_inc(filled, mark(filled, "out"))

        @block.scalar
        def _(act_):
            a = nc.scalar.activation

            def copy(dst, src, scale=1.0):
                return a(dst, src, ACT.Copy, scale=scale)

            def sqrt(key, dst):
                act_.wait_ge(madeV, nth(madeV, ("var", key)))
                a(dst, dst, ACT.Sqrt).then_inc(madeA, mark(madeA, ("std", key)))

            def square(key, src):
                a(hT[:, :, T:2 * T], src, ACT.Square).then_inc(madeA, mark(madeA, ("sq", key)))

            def four_banks(dst_of):
                for tt in range(TT):
                    for q in range(2):
                        src = ps[:, 1 + tt * 2 + q, :]
                        last = copy(dst_of(tt, q), src)
                return last

            act_.wait_ge(filled, nth(filled, "x"))
            for tt in range(TT):
                for q in range(2):
                    last = copy(xT[:, 4 * q:4 * q + 4, tt * P:(tt + 1) * P], ps[:, 1 + tt * 2 + q, :].rearrange("p (k t) -> p k t", t=P))
            act_.drain()
            square("n1", xT[:, :, :])
            act_.wait_ge(filled, nth(filled, "cols"))
            copy(cols[:, :, :].rearrange("p a b -> p (a b)"), ps[:, 0, 0:3 * P])
            act_.drain()
            a(csil[:, :], cols[:, 0, 104:128], ACT.Sigmoid).then_inc(madeA, mark(madeA, "cols"))
            a(small[:, 0, :], cols[:, 2, 32:48], ACT.Exp).then_inc(madeA, mark(madeA, "dt"))
            sqrt("n1", rstd[:, 0:T])
            act_.wait_ge(madeV, nth(madeV, "angle"))
            a(small[:, 4, :], small[:, 1, :], ACT.Exp)
            a(small[:, 5, :], small[:, 3, :], ACT.Sin, scale=SIN2PI)
            a(small[:, 6, :], small[:, 3, :], ACT.Sin, scale=SIN2PI / 2).then_inc(madeA, mark(madeA, "trig"))
            act_.wait_ge(filled, nth(filled, "bbT"))
            for n in range(2):
                last = copy(bbT[:, n, :, :].rearrange("p a b -> p (a b)"), ps[:, 4 + n, :])
            last.then_inc(emptied, mark(emptied, "bbT"))
            act_.wait_ge(filled, nth(filled, "cT"))
            for n in range(2):
                last = copy(cT[:, n, :, :].rearrange("p a b -> p (a b)"), ps[:, n, :])
            last.then_inc(emptied, mark(emptied, "cT"))

            turn = [0]
            nsin = [0]

            def take(fn):
                g = turn[0]
                act_.wait_ge(filled, nth(filled, ("p1", g)))
                fn(ps[:, g % 4, :]).then_inc(emptied, mark(emptied, ("p1", g)))
                turn[0] += 1

            def sines():
                j = nsin[0]
                if j >= 16:
                    return
                act_.wait_ge(madeV, nth(madeV, ("fr", j)))
                if j >= 2:
                    act_.wait_ge(madeV, nth(madeV, ("s", j - 2)))
                a(tabs[j % 2][:, 1, :], fr[j % 2], ACT.Sin, scale=SIN2PI)
                a(tabs[j % 2][:, 0, :], fr[j % 2], ACT.Sin, scale=SIN2PI / 2)
                act_.drain()
                a(tabs[j % 2][:, 0, :], tabs[j % 2][:, 0, :], ACT.Square).then_inc(madeA, mark(madeA, ("sin", j)))
                nsin[0] += 1

            two = lambda v: v.rearrange("p (a b) -> p a b", a=2)
            for n, c, _ in IN1:
                if n in ("u", "q"):
                    dst = (uT if n == "u" else qT)[:, 2 * c:2 * c + 2, :]
                    take(lambda b: copy(dst, two(b), 0.125 if n == "q" else 1.0))
                    sines()
                elif n in ("kslc", "kwin"):
                    for h in range(2):
                        take(lambda b: copy((kslc if n == "kslc" else kwin)[:, 2 * h:2 * h + 2, :], two(b)))
                        sines()
                elif n in ("kcmp", "vcmp"):
                    kv = kcmp if n == "kcmp" else vcmp

                    def shifted(b, h):
                        copy(kv[0:64, 2 * h:2 * h + 2, :], two(b)[0:64])
                        return copy(kv[64:128, 2 * h:2 * h + 2, 0:T - 1], two(b)[64:128, :, 1:T])
                    for h in range(2):
                        take(lambda b: shifted(b, h))
                        sines()
                else:
                    take(lambda b: copy((vslc if n == "vslc" else vwin)[:, :, :], two(b)))
                    sines()
            take(lambda b: a(gates[:, :, :], b[:, 0:96].rearrange("p (a b) -> p a b", a=2), ACT.Sigmoid))
            for kv in range(2):
                act_.wait_ge(filled, nth(filled, ("hid", kv)))
                copy(cbias[:, 2 * kv:2 * kv + 2], ps[:, kv, 128:130])
                act_.drain()
                for m in range(2):
                    last = a(hid[:, kv, m, :], ps[:, kv, m * 60:(m + 1) * 60], ACT.Gelu_apprx_tanh, bias=cbias[:, 2 * kv + m:2 * kv + m + 1])
            last.then_inc(madeA, mark(madeA, "hid"))
            while nsin[0] < 16:
                sines()
            act_.wait_ge(filled, nth(filled, "kc"))
            copy(kcT, ps[:, 2, 0:60])
            copy(vcN[0:NCMP, :, :].rearrange("p a b -> p (a b)"), ps[0:NCMP, 3, 0:256]).then_inc(madeA, mark(madeA, "kc"))
            act_.wait_ge(madeV, nth(madeV, "yD"))
            a(yT, yT, ACT.Gelu_apprx_tanh).then_inc(madeA, mark(madeA, "ygelu"))
            act_.wait_ge(filled, nth(filled, "z"))
            for m in range(2):
                last = a(yS[:, 2 * m:2 * m + 2, :].rearrange("p a b -> p (a b)"), ps[:, 4 + m, :], ACT.Sigmoid)
            last.then_inc(madeA, mark(madeA, "ysig"))
            act_.wait_ge(madeV, nth(madeV, "yS"))

            def seg(n, u):
                if n == 1:
                    g, tt, x = u
                    return (4, 16 if x == "cmp" else P * (tt + 1))
                return (2, 512)

            def exp(n, i, u):
                act_.wait_ge(madeV, nth(madeV, ("mx", n, i)))
                if i >= 2:
                    act_.wait_ge(filled, nth(filled, ("T", n, i - 2)))
                ns, nk = seg(n, u)
                e_ = (Eb if n == 1 else E2)[i % 2]
                m = NCMP if nk == 16 else nk
                for s in range(ns):
                    bank, at = (2 * (i % 2) + s // 2, (s % 2) * nk) if n == 1 else (2 * (i % 2) + s, 0)
                    last = a(e_[:, s * nk:s * nk + m], ps[:, bank, at:at + m], ACT.Exp,
                             bias=stat[:, i % 2, s:s + 1], accum_out=stat[:, i % 2, 4 + s:5 + s])
                last.then_inc(madeA, mark(madeA, ("exp", n, i)))

            def turned(n, i, u):
                act_.wait_ge(filled, nth(filled, ("T", n, i)))
                ns, nk = seg(n, u)
                pt = (PT if n == 1 else PT2)[i % 2]
                if nk == 16:
                    last = copy(pt[0:NCMP, 0:4 * P], ps[0:NCMP, 4, :])
                else:
                    w = ns * nk
                    last = copy(pt[:, 0:w], ps[:, 4:6, :].rearrange("p a b -> p (a b)")[:, 0:w])
                last.then_inc(madeA, mark(madeA, ("PT", n, i)))

            def outs(n, i, u):
                if n == 1:
                    g, tt, x = u
                    if x != "win":
                        return
                    act_.wait_ge(filled, nth(filled, ("O", n, i)))
                    last = copy(oT[:, 2 * g:2 * g + 2, tt * P:(tt + 1) * P], ps[:, 6, 0:2 * P].rearrange("p (a b) -> p a b", a=2))
                else:
                    x, hp, tt = u
                    act_.wait_ge(filled, nth(filled, ("O", n, i)))
                    last = copy(o2[:, (0 if x == "na" else 4) + hp, tt * P:(tt + 1) * P], ps[:, 6, 0:P])
                last.then_inc(emptied, mark(emptied, ("O", n, i)))

            def attention(n, units):
                exp(n, 0, units[0])
                for i, u in enumerate(units):
                    if i + 1 < len(units):
                        exp(n, i + 1, units[i + 1])
                    turned(n, i, u)
                    outs(n, i, u)

            def sigmoids(key, c, prev):
                act_.wait_ge(filled, nth(filled, (key, c)))
                if c >= 1:
                    act_.wait_ge(madeV, nth(madeV, (prev, c - 1)))
                for n in range(2):
                    last = a(sgl[:, n, :, :].rearrange("p a b -> p (a b)"), ps[:, 2 + n, :], ACT.Sigmoid)
                last.then_inc(madeA, mark(madeA, ("sgl", key, c)))

            def moe_front(key, do_square=True):
                if do_square:
                    act_.wait_ge(madeV, nth(madeV, "x" + key))
                    square(key, xT[:, :, :])
                sqrt(key, rstd[:, 0:T])
                act_.wait_ge(filled, nth(filled, "hN" + key))
                for tt in range(TT):
                    for q in range(2):
                        last = copy(hN[:, tt, q * 512:(q + 1) * 512], ps[:, 1 + tt * 2 + q, :])
                last.then_inc(madeA, mark(madeA, "hN" + key))
                act_.wait_ge(madeV, nth(madeV, "shifted" + key))
                last = a(Wt[:, :, :], lg[:, :, 0:E], ACT.Exp)
                if key == "f1":
                    last = a(rt[:, :, 0:4], gx[:, :, 0:4], ACT.Exp)
                last.then_inc(madeA, mark(madeA, "exp" + key))
                act_.wait_ge(madeV, nth(madeV, "ready" + key))

            def one(n):
                def body(it, u, e, s, q, b, final):
                    act_.wait_ge(s["spreadT"], q + 1)
                    copy(ohT, ps[:, 0, 0:T]).then_inc(s["spread"], 1)
                    act_.wait_ge(s["glu"], q + 1)
                    if n == 1:
                        a(sg[:, 0:P], ps[:, 1, 0:P], ACT.Sigmoid).then_inc(s["sig"], 1)
                    else:
                        a(sg, glu, ACT.Sigmoid, scale=1.702).then_inc(s["sig"], 1)
                return body

            attention(1, units1)
            for c in range(4):
                sigmoids("gates", c, "mgd")
            moe_front("f1")
            run_experts(act_, 1, one(1))
            act_.wait_ge(madeV, nth(madeV, "moe1 out"))
            square("fin", xT[:, :, :])
            sqrt("fin", rstd[:, 0:T])
            act_.wait_ge(madeV, nth(madeV, "x2"))
            square("n2", xT[:, :, :])
            sqrt("n2", rstd[:, 0:T])
            act_.wait_ge(filled, nth(filled, "ctx"))
            for tt in range(TT):
                for q in range(2):
                    last = copy(hT[:, 4 * q:4 * q + 4, T + tt * P:T + (tt + 1) * P], ps[:, 1 + tt * 2 + q, :].rearrange("p (k t) -> p k t", t=P))
            act_.drain()
            a(mgd, hT[:, :, T:2 * T], ACT.Square).then_inc(madeA, mark(madeA, ("sq", "ctx")))
            sqrt("ctx", rstd[:, T:2 * T])
            turn2 = [0]

            def take2(fn):
                g = turn2[0]
                act_.wait_ge(filled, nth(filled, ("p2", g)))
                fn(ps[:, g % 4, :]).then_inc(emptied, mark(emptied, ("p2", g)))
                turn2[0] += 1

            for m in range(4):
                take2(lambda b: copy(kaT[:, m, :], b))
            for c in range(2):
                for h in range(2):
                    take2(lambda b: copy(vN[:, 2 * h:2 * h + 2, c * 256:(c + 1) * 256], two(b)))
            for h in range(2):
                def kv_b(b):
                    copy(kbN[:, 2 * h:2 * h + 2, :], two(b)[:, :, 0:P])
                    return copy(vbN[:, 2 * h:2 * h + 2, :], two(b)[:, :, P:2 * P])
                take2(kv_b)
            for c in range(2):
                take2(lambda b: copy(qaT[:, 2 * c:2 * c + 2, :], two(b), 0.125))
            for c in range(2):
                take2(lambda b: copy(qbN[:, :, c * 256:(c + 1) * 256], two(b)))
            sqrt("heads", rn[:, 0:24])
            act_.wait_ge(filled, nth(filled, "qbT"))
            for n in range(2):
                last = copy(qbT[:, 2 * n:2 * n + 2, :], two(ps[:, 4 + n, :]), 0.125)
            act_.wait_ge(filled, nth(filled, "kbT"))
            copy(kbT[0:64, 0, :], ps[0:64, 6, :])
            copy(kbT[64:128, 1, :], ps[64:128, 6, :])
            copy(kbT[64:128, 0, :], ps[64:128, 7, :])
            copy(kbT[0:64, 1, :], ps[0:64, 7, :]).then_inc(emptied, mark(emptied, "kbT"))
            attention(2, units2)
            for c in range(4):
                sigmoids("gates2", c, "mgd2")
            for c in range(4):
                act_.wait_ge(filled, nth(filled, ("y2", c)))
                copy(o2[:, 2 * c:2 * c + 2, :], two(ps[:, 4 + c, :]))
                last = a(hT[:, 2 * c:2 * c + 2, T:2 * T], two(ps[:, 4 + c, :]), ACT.Square)
            last.then_inc(madeA, mark(madeA, ("sq", "post")))
            sqrt("post", rstd[:, 0:T])
            moe_front("f2")
            run_experts(act_, 2, one(2))
            act_.wait_ge(filled, nth(filled, "moe2"))
            for c in range(4):
                copy(o2[:, 2 * c:2 * c + 2, :], two(ps[:, 4 + c, :]))
                last = a(hT[:, 2 * c:2 * c + 2, T:2 * T], two(ps[:, 4 + c, :]), ACT.Square)
            last.then_inc(madeA, mark(madeA, ("sq", "postf")))
            sqrt("postf", rstd[:, 0:T])
            act_.wait_ge(filled, nth(filled, "out"))
            for tt in range(TT):
                for q in range(2):
                    last = copy(hN[:, tt, q * 512:(q + 1) * 512], ps[:, 1 + tt * 2 + q, :])
            last.then_inc(madeA, mark(madeA, "out"))

        @block.vector
        def _(v):
            V = nc.vector
            tt_, ts, stt = V.tensor_tensor, V.tensor_scalar, V.scalar_tensor_tensor

            def B(x, n):
                return x[:, :, None].broadcast_to([P, x.shape[1], n])

            def over(x, n):
                return x[:, None, :].broadcast_to([P, n, x.shape[1]])

            def rms(key, bank, dst, n=D):
                v.wait_ge(filled, nth(filled, ("ss", key)))
                ts(dst, ps[:, bank, 0:T], 1.0 / n, EPS, ALU.mult, ALU.add).then_inc(madeV, mark(madeV, ("var", key)))
                v.wait_ge(madeA, nth(madeA, ("std", key)))
                V.reciprocal(dst, dst)
                v.drain()

            def modulate(dst, src, r, gs, sh, key):
                tt_(dst, src, over(r, KD), ALU.mult)
                v.drain()
                for k in range(KD):
                    last = ts(dst[:, k, :], dst[:, k, :], gs[:, k:k + 1], sh[:, k:k + 1] if sh is not None else None,
                              ALU.mult, ALU.add if sh is not None else None) if sh is not None else \
                        ts(dst[:, k, :], dst[:, k, :], gs[:, k:k + 1], None, ALU.mult)
                last.then_inc(madeV, mark(madeV, key))

            v.wait_ge(small_in, SMALL)
            V.tensor_copy(packs[32:48, 2, :].rearrange("p (s c) -> p s c", s=2),
                                     dt2[32:48, :, None].broadcast_to([16, 2, 64])).then_inc(madeV, mark(madeV, "dt rows"))
            v.wait_ge(madeA, nth(madeA, "cols"))
            tt_(csil[:, :], csil[:, :], cols[:, 0, 104:128], ALU.mult)
            v.drain()
            V.tensor_copy(cpair[:, :, 0], csil[:, 8:16])
            V.tensor_copy(cpair[:, :, 1], csil[:, 16:24]).then_inc(madeV, mark(madeV, "csil"))
            rms("n1", 5, rstd[:, 0:T])
            lr, li = cols[:, 2, 0:16], cols[:, 2, 16:32]
            sm = lambda i: small[:, i, :]
            v.wait_ge(madeA, nth(madeA, "dt"))

            def step(ins):
                v.drain()
            step(tt_(sm(1), lr, sm(0), ALU.mult))
            step(tt_(sm(2), li, sm(0), ALU.mult))
            step(ts(sm(2), sm(2), 1.0 / TWO_PI, None, ALU.mult))
            step(ts(sm(3), sm(2), MAGIC, None, ALU.add))
            step(ts(sm(3), sm(3), -MAGIC, None, ALU.add))
            tt_(sm(3), sm(2), sm(3), ALU.subtract).then_inc(madeV, mark(madeV, "angle"))
            v.wait_ge(madeA, nth(madeA, "trig"))
            step(tt_(sm(7), sm(6), sm(6), ALU.mult))
            step(ts(sm(7), sm(7), -2.0, 1.0, ALU.mult, ALU.add))
            tt_(sm(8), sm(4), sm(7), ALU.mult)
            tt_(sm(9), sm(4), sm(5), ALU.mult)
            tt_(sm(10), lr, lr, ALU.mult)
            step(tt_(sm(11), li, li, ALU.mult))
            tt_(sm(10), sm(10), sm(11), ALU.add)
            step(ts(sm(8), sm(8), -1.0, None, ALU.add))
            V.reciprocal(sm(10), sm(10))
            tt_(sm(12), sm(8), lr, ALU.mult)
            tt_(sm(13), sm(9), li, ALU.mult)
            tt_(sm(14), sm(9), lr, ALU.mult)
            step(tt_(sm(15), sm(8), li, ALU.mult))
            tt_(sm(12), sm(12), sm(13), ALU.add)
            step(tt_(sm(14), sm(14), sm(15), ALU.subtract))
            tt_(sm(12), sm(12), sm(10), ALU.mult)
            step(tt_(sm(13), sm(14), sm(10), ALU.mult))
            b3 = lambda x: x.rearrange("p (j h) -> p j h", h=16)
            v.wait_ge(small_in, SMALL)
            cr_, ci_ = B(sm(12), 16), B(sm(13), 16)
            tmp = b3(sa[:, 0, :])
            tmp2 = b3(sa[:, 1, :])
            tt_(b3(bbuf[:, 0, :]), cr_, b3(bR[:, 0, :]), ALU.mult)
            tt_(tmp, ci_, b3(bR[:, 1, :]), ALU.mult)
            tt_(b3(bbuf[:, 1, :]), cr_, b3(bR[:, 1, :]), ALU.mult)
            step(tt_(tmp2, ci_, b3(bR[:, 0, :]), ALU.mult))
            tt_(b3(bbuf[:, 0, :]), b3(bbuf[:, 0, :]), tmp, ALU.subtract)
            step(tt_(b3(bbuf[:, 1, :]), b3(bbuf[:, 1, :]), tmp2, ALU.add))
            for n in range(2):
                d_ = bd[:, n, :].rearrange("p (j s h) -> p j s h", s=2, h=16)
                for s in range(2):
                    ts(d_[:, :, s, :], b3(bbuf[:, n, :]), cst("half", s, s + 1), None, ALU.mult)
                c3 = cR[:, n, :].rearrange("p (t c) -> p t c", c=P)
                last = stt(c3, c3, 1.0 if n == 0 else -1.0, over(cst("parity"), 4), ALU.mult, ALU.mult)
            last.then_inc(madeV, mark(madeV, "bd"))
            v.wait_ge(filled, nth(filled, "mod1"))
            tt_(mod1[:, :], ps[:, 6, 0:48], cols[:, 0, 0:48], ALU.add)
            v.drain()
            stt(gain[:, 0, :], mod1[:, 8:16], 1.0, cols[:, 0, 48:56], ALU.add, ALU.mult)
            stt(gain[:, 1, :], mod1[:, 32:40], 1.0, cols[:, 0, 56:64], ALU.add, ALU.mult)
            v.drain()
            modulate(hT[:, :, 0:T], xT[:, :, :], rstd[:, 0:T], gain[:, 0, :], mod1[:, 0:8], "h1")

            def fraction(j):
                if j >= 2:
                    v.wait_ge(madeA, nth(madeA, ("sin", j - 2)))
                f, th = fr[j % 2], small[:, 2, j:j + 1]
                step(ts(f, cst("time"), th, MAGIC, ALU.mult, ALU.add))
                step(ts(f, f, -MAGIC, None, ALU.add))
                stt(f, cst("time"), th, f, ALU.mult, ALU.subtract).then_inc(madeV, mark(madeV, ("fr", j)))

            fraction(0)
            fraction(1)
            for j in range(16):
                tb = tabs[j % 2]
                v.wait_ge(madeA, nth(madeA, ("sin", j)))
                step(ts(tb[:, 0, :], tb[:, 0, :], -2.0, 1.0, ALU.mult, ALU.add))
                if j + 2 < 16:
                    fraction(j + 2)
                v.wait_ge(filled, nth(filled, ("bu", j)))
                bu = ps[:, 4 + j % 2, :].rearrange("p (a b) -> p a b", a=2)
                C, S_ = over(tb[:, 0, :], 2), over(tb[:, 1, :], 2)
                tt_(sa, bu, C, ALU.mult)
                tt_(sb_, bu, S_, ALU.mult).then_inc(vemptied, mark(vemptied, ("bu", j)))
                v.drain()
                tt_(sw[:, 0, :], sa[:, 0, :], sb_[:, 1, :], ALU.add)
                step(tt_(sw[:, 1, :], sa[:, 1, :], sb_[:, 0, :], ALU.subtract))
                r = small[:, 4, j:j + 1].broadcast_to([P, T])
                V.tensor_tensor_scan(sz[:, 0, :], r, sw[:, 0, :], 0.0, ALU.mult, ALU.add)
                step(V.tensor_tensor_scan(sz[:, 1, :], r, sw[:, 1, :], 0.0, ALU.mult, ALU.add))
                tt_(sa, sz, C, ALU.mult)
                step(tt_(sb_, sz, S_, ALU.mult))
                if j >= 2:
                    v.wait_ge(filled, nth(filled, ("y", j - 2)))
                tt_(ss2[j % 2][:, 0, :], sa[:, 0, :], sb_[:, 1, :], ALU.subtract)
                tt_(ss2[j % 2][:, 1, :], sa[:, 1, :], sb_[:, 0, :], ALU.add).then_inc(madeV, mark(madeV, ("s", j)))
            v.wait_ge(filled, nth(filled, ("y", 15)))
            for k in range(4):
                last = stt(yT[:, k, :], uT[:, k, :], cols[:, 2, 48 + k:49 + k], ps[:, 6 + k // 2, (k % 2) * T:(k % 2 + 1) * T],
                           ALU.mult, ALU.add)
            last.then_inc(madeV, mark(madeV, "yD"))
            v.wait_ge(madeA, nth(madeA, "ysig"))
            tt_(yS, yS, yT, ALU.mult).then_inc(madeV, mark(madeV, "yS"))

            def seg(n, u):
                if n == 1:
                    g, tt, x = u
                    return (4, 16 if x == "cmp" else P * (tt + 1))
                return (2, 512)

            def view(x, ns, nk):
                w = x[:, 0:ns * nk].rearrange("p (s k) -> p s k", s=ns)
                return w[:, :, 0:NCMP] if nk == 16 else w

            def maxima(n, i, u):
                v.wait_ge(filled, nth(filled, ("S", n, i)))
                ns, nk = seg(n, u)
                sc = ps[:, 2 * (i % 2):2 * (i % 2) + 2, 0:ns * nk // 2].rearrange("p a (s k) -> p a s k", k=nk)
                m = NCMP if nk == 16 else nk
                dst = stat[:, i % 2, 0:ns].rearrange("p (a s) -> p a s", a=2)
                V.tensor_reduce(dst, sc[:, :, :, 0:m], AX.X, ALU.max, negate=True).then_inc(madeV, mark(madeV, ("mx", n, i)))

            def normalise(n, i, u):
                v.wait_ge(madeA, nth(madeA, ("exp", n, i)))
                ns, nk = seg(n, u)
                st = stat[:, i % 2, :]
                c = st[:, 8:8 + ns]
                step(V.reciprocal(c, st[:, 4:4 + ns]))
                if n == 1:
                    g, tt, x = u
                    at = ("cmp", "slc", "win").index(x) * 16 + 4 * g
                    c2 = c.rearrange("p (par half) -> p par half", par=2)
                    step(tt_(c2, c2, gates[:, tt, at:at + 4].rearrange("p (half par) -> p par half", par=2), ALU.mult))
                    if x == "cmp":
                        step(ts(c, c, cst("cmprow", tt, tt + 1), None, ALU.mult))
                e_ = view((Eb if n == 1 else E2)[i % 2], ns, nk)
                m = NCMP if nk == 16 else nk
                tt_(e_, e_, B(c, m), ALU.mult).then_inc(madeV, mark(madeV, ("P", n, i)))

            def bias(tt):
                v.wait_ge(bias_in[tt], 256)
                x = nab2[:, :, :].rearrange("p h (r c) -> p (h r) c", c=64)
                tt_(x, x, over(cst("namask"), 32), ALU.add).then_inc(madeV, mark(madeV, ("bias", tt)))

            def attention(n, units):
                maxima(n, 0, units[0])
                for i, u in enumerate(units):
                    if n == 2 and i == 6:
                        bias(1)
                    if i + 1 < len(units):
                        maxima(n, i + 1, units[i + 1])
                    normalise(n, i, u)

            v.wait_ge(emptied, nth(emptied, ("p1", 16)))
            attention(1, units1)

            def merge(key, gkey, out_key, tmpb):
                for c in range(4):
                    v.wait_ge(madeA, nth(madeA, ("sgl", gkey, c)))
                    v.wait_ge(filled, nth(filled, (key, c)))
                    for n in range(2):
                        s_ = sgl[:, n, :, :].rearrange("p a b -> p (a b)")
                        tt_(s_, ps[:, n, :], s_, ALU.mult)
                    v.drain()
                    tt_(mgd[:, 2 * c:2 * c + 2, :], sgl[:, 0, :, :], sgl[:, 1, :, :], ALU.add).then_inc(madeV, mark(madeV, (out_key, c)))

            merge("branch", "gates", "mgd", None)
            for c in range(4):
                v.wait_ge(filled, nth(filled, ("tm", c)))
                for m in range(2):
                    k = 2 * c + m
                    last = stt(xT[:, k, :], ps[:, 4 + c, m * T:(m + 1) * T], mod1[:, 16 + k:17 + k], xT[:, k, :], ALU.mult, ALU.add)
            last.then_inc(madeV, mark(madeV, "xf1"))

            def top(scores, n, kth, chosen, a1, a2):
                x = a1[:, 0:n * n].rearrange("p (i j) -> p i j", j=n)
                y = a2[:, 0:n * n].rearrange("p (i j) -> p i j", j=n)
                mine, other = B(scores, n), over(scores, n)
                idx = cst("time", 0, n)
                tt_(x, B(idx, n), over(idx, n), ALU.is_gt)
                step(tt_(y, other, mine, ALU.is_equal))
                step(tt_(y, y, x, ALU.mult))
                step(tt_(x, other, mine, ALU.is_gt))
                step(tt_(x, x, y, ALU.add))
                step(V.tensor_reduce(chosen, x, AX.X, ALU.add))
                step(ts(chosen, chosen, kth - 0.5, None, ALU.is_lt))

            def moe_front(key, gs, sh, nr):
                rms(key, 0, rstd[:, 0:T])
                modulate(hT[:, :, 0:T], xT[:, :, :], rstd[:, 0:T], gs, sh, "h" + key)
                v.wait_ge(filled, nth(filled, "logits" + key))
                for tt in range(TT):
                    last = V.tensor_copy(lg[:, tt, 0:nr], ps[:, 5, tt * 64:tt * 64 + nr])
                step(last)
                if key == "f1":
                    step(V.tensor_copy(gx[:, :, 0:4], lg[:, :, 0:4]))
                    step(V.tensor_reduce(rt[:, :, 8], gx[:, :, 0:4], AX.X, ALU.max))
                    for tt in range(TT):
                        top(gx[:, tt, 0:4], 4, 1, gx[:, tt, 4:8], t1, t2)
                    for tt in range(TT):
                        e4 = t1[:, 0:E].rearrange("p (g e) -> p g e", e=8)
                        step(ts(gx[:, tt, 4:8], gx[:, tt, 4:8], -1.0, -NEG, ALU.add, ALU.mult))
                        step(tt_(e4, lg[:, tt, 4:36].rearrange("p (g e) -> p g e", e=8), B(gx[:, tt, 4:8], 8), ALU.add))
                        step(V.tensor_copy(lg[:, tt, 0:E], t1[:, 0:E]))
                        step(ts(gx[:, tt, 0:4], gx[:, tt, 0:4], rt[:, tt, 8:9], None, ALU.subtract))
                for tt in range(TT):
                    top(lg[:, tt, 0:E], E, 2 if key == "f1" else 4, Am[:, tt, :], t1, t2)
                ts(zero, hT[:, 0:2, 0:T], 0.0, None, ALU.mult) if False else V.memset(zero, 0.0).then_inc(madeV, mark(madeV, "chosen" + key))
                step(V.tensor_reduce(rt[:, :, 9], lg[:, :, 0:E], AX.X, ALU.max))
                for tt in range(TT):
                    last = ts(lg[:, tt, 0:E], lg[:, tt, 0:E], rt[:, tt, 9:10], None, ALU.subtract)
                last.then_inc(madeV, mark(madeV, "shifted" + key))
                v.wait_ge(filled, nth(filled, "places" + key))
                cnt = ps[0:1, 5, 256:256 + E]
                c0, c1, c2 = crow[0:1, 0, :], crow[0:1, 1, :], crow[0:1, 2, :]
                step(ts(c0, cnt, SLOTS + 0.5, None, ALU.is_gt))
                for b in range(2, MAXB):
                    step(stt(c0, cnt, SLOTS * b + 0.5, c0, ALU.is_gt, ALU.add))
                step(V.memset(c2, 1.0))
                step(V.tensor_tensor_scan(c1, c2, c0, 0.0, ALU.mult, ALU.add))
                step(tt_(c1, c1, c0, ALU.subtract))
                V.tensor_copy(tabI[0:1, 0, :], c0)
                V.tensor_copy(tabI[0:1, 1, :], c1)
                for tt in range(TT):
                    step(stt(sel[:, tt, :], ps[:, 5, 128 + tt * E:128 + (tt + 1) * E], 1.0, Am[:, tt, :], ALU.add, ALU.mult))
                step(ts(sel[:, :, :], sel[:, :, :], -1.0, None, ALU.add))
                v.wait_ge(madeA, nth(madeA, "exp" + key))
                step(tt_(Wt[:, :, :], Wt[:, :, :], Am[:, :, :], ALU.mult))
                step(V.tensor_reduce(rt[:, :, 10], Wt[:, :, :], AX.X, ALU.add))
                if key == "f1":
                    step(V.tensor_reduce(rt[:, :, 11], rt[:, :, 0:4], AX.X, ALU.add))
                    step(tt_(rt[:, :, 10], rt[:, :, 10], rt[:, :, 11], ALU.mult))
                step(V.reciprocal(rt[:, :, 10], rt[:, :, 10]))
                for tt in range(TT):
                    last = ts(Wt[:, tt, :], Wt[:, tt, :], rt[:, tt, 10:11], None, ALU.mult)
                step(last)
                if key == "f2":
                    V.memset(biasB, 0.0).then_inc(madeV, mark(madeV, "biasB"))
                V.memset(t1, 0.0).then_inc(madeV, mark(madeV, "ready" + key))
                V.memset(t2, 0.0).then_inc(madeV, mark(madeV, "tables" + key))

            def one(n):
                def body(it, u, e, s, q, b, final):
                    slots = cst("time", 0, SLOTS) if final else cst("time")[:, bass.ds(b * SLOTS, SLOTS)]
                    ec = bass.ds(e, 1)
                    if n == 2:
                        V.tensor_copy(esel, cst("ident")[:, ec].broadcast_to([P, SLOTS]))
                    for tt in range(TT):
                        ts(ohG[:, tt, :], slots, sel[:, tt, ec], None, ALU.is_equal)
                        for half in range(2):
                            last = ts(ohS[:, tt, half * SLOTS:(half + 1) * SLOTS], slots, sel[:, tt, ec], Wt[:, tt, ec],
                                      ALU.is_equal, ALU.mult)
                    last.then_inc(s["onehot"], 1)
                    v.wait_ge(s["gathered"], q + 1)
                    V.tensor_copy(xsT.rearrange("p a b -> p (a b)"), ps[:, 0, :]).then_inc(s["xs"], 1)
                    v.wait_ge(s["hidden"], q + 1)
                    if n == 1:
                        V.tensor_copy(glu[:, 0:P], ps[:, 1, 0:P]).then_inc(s["glu"], 1)
                        V.tensor_copy(lin[:, 0:P], ps[:, 2, 0:P])
                        v.drain()
                        tt_(lin[:, 0:P], lin[:, 0:P], glu[:, 0:P], ALU.mult)
                        v.drain()
                        v.wait_ge(s["sig"], q + 1)
                        tt_(act[:, 0:P], lin[:, 0:P], sg[:, 0:P], ALU.mult).then_inc(s["act"], 1)
                    else:
                        ts(glu, ps[:, 1, :], 7.0, None, ALU.min).then_inc(s["glu"], 1)
                        ts(lin, ps[:, 2, :], 7.0, -7.0, ALU.min, ALU.max)
                        v.drain()
                        stt(lin, lin, 1.0, glu, ALU.add, ALU.mult)
                        v.drain()
                        v.wait_ge(s["sig"], q + 1)
                        tt_(act, lin, sg, ALU.mult).then_inc(s["act"], 1)
                    v.wait_ge(s["turned"], q + 1)
                    w = 512 if n == 2 else P
                    V.tensor_copy(actT.rearrange("p a b -> p (a b)")[:, 0:w], ps[:, 3, 0:w]).then_inc(s["actT"], 1)
                    v.wait_ge(s["down"], q + 1)
                    V.tensor_copy(ysS, ps[:, 3, :]).then_inc(s["ys"], 1)
                return body

            moe_front("f1", gain[:, 1, :], mod1[:, 24:32], 36)
            run_experts(v, 1, one(1))
            v.wait_ge(filled, nth(filled, "moe1"))
            for k in range(KD):
                last = stt(xT[:, k, :], ps[:, 4 + k // 2, (k % 2) * T:(k % 2 + 1) * T], mod1[:, 40 + k:41 + k], xT[:, k, :], ALU.mult, ALU.add)
            last.then_inc(madeV, mark(madeV, "moe1 out"))
            rms("fin", 0, rstd[:, 0:T])
            modulate(xT[:, :, :], xT[:, :, :], rstd[:, 0:T], cols[:, 0, 64:72], None, "x2")
            v.wait_ge(filled, nth(filled, "mod2"))
            tt_(mod2[:, :, :], ps[:, 6, 0:96].rearrange("p (a b) -> p a b", b=2), B(cols[:, 1, 0:48], 2), ALU.add)
            v.drain()
            stt(gain[:, 2, :], mod2[:, 8:16, 0], 1.0, cols[:, 1, 48:56], ALU.add, ALU.mult)
            stt(gain[:, 3, :], mod2[:, 8:16, 1], 1.0, cols[:, 1, 48:56], ALU.add, ALU.mult)
            tt_(gain[:, 4, :], mod2[:, 16:24, 0], cols[:, 1, 56:64], ALU.mult)
            stt(gain[:, 5, :], mod2[:, 32:40, 0], 1.0, cols[:, 1, 64:72], ALU.add, ALU.mult)
            tt_(gain[:, 0, :], mod2[:, 40:48, 0], cols[:, 1, 72:80], ALU.mult)
            v.drain()
            rms("n2", 0, rstd[:, 0:T])
            modulate(hT[:, :, 0:T], xT[:, :, :], rstd[:, 0:T], gain[:, 2, :], mod2[:, 0:8, 0], "h2")
            rms("ctx", 5, rstd[:, T:2 * T])
            modulate(hT[:, :, T:2 * T], hT[:, :, T:2 * T], rstd[:, T:2 * T], gain[:, 3, :], mod2[:, 0:8, 1], "hctx")
            v.wait_ge(emptied, nth(emptied, ("p2", 13)))
            q3 = lambda x: x.rearrange("p t (h d) -> p (t h) d", d=HD)
            tt_(q3(qt1), q3(qbN), q3(qbN), ALU.mult)
            step(tt_(q3(kt1), q3(kbN), q3(kbN), ALU.mult))
            V.tensor_reduce(rn[:, 0:16], q3(qt1), AX.X, ALU.add)
            step(V.tensor_reduce(rn[:, 16:24], q3(kt1), AX.X, ALU.add))
            ts(rn[:, 0:24], rn[:, 0:24], 1.0 / HD, EPS, ALU.mult, ALU.add).then_inc(madeV, mark(madeV, ("var", "heads")))
            bias(0)
            v.wait_ge(madeA, nth(madeA, ("std", "heads")))
            step(V.reciprocal(rn[:, 0:24], rn[:, 0:24]))
            tt_(q3(qbN), q3(qbN), B(rn[:, 0:16], HD), ALU.mult)
            step(tt_(q3(kbN), q3(kbN), B(rn[:, 16:24], HD), ALU.mult))
            tt_(q3(qbN), q3(qbN), over(gqk[:, 0, :], 16), ALU.mult)
            step(tt_(q3(kbN), q3(kbN), over(gqk[:, 1, :], 8), ALU.mult))
            for x, x1, x2, nh in ((qbN, qt1, qt2, 8), (kbN, kt1, qt2, 2)):
                for tt in range(TT):
                    h3 = lambda y: y[:, tt, 0:nh * HD].rearrange("p (h d) -> p h d", d=HD)
                    h5 = lambda y: y[:, tt, 0:nh * HD].rearrange("p (h a b c) -> p h a b c", a=2, b=2, c=16)
                    tt_(h3(x1), h3(x), over(cst("ropecos", tt * HD, (tt + 1) * HD), nh), ALU.mult)
                    sn = cst("ropesin", tt * HD, (tt + 1) * HD).rearrange("p (a b c) -> p a b c", a=2, b=2)
                    for b in range(2):
                        tt_(h5(x2)[:, :, :, b, :], h5(x)[:, :, :, 1 - b, :],
                            sn[:, None, :, b, :].broadcast_to([P, nh, 2, 16]), ALU.mult)
                    v.drain()
                    step(tt_(h3(x), h3(x1), h3(x2), ALU.add))
            V.tensor_copy(kt1[:, :, 0:HD], kbN[:, :, HD:2 * HD])
            V.tensor_copy(kt1[:, :, HD:2 * HD], kbN[:, :, 0:HD]).then_inc(madeV, mark(madeV, "rope"))
            attention(2, units2)
            merge("branch2", "gates2", "mgd2", None)

            def residual(key, g_, out_key):
                rms(key, 0, rstd[:, 0:T])
                step(tt_(o2[:, :, :], o2[:, :, :], over(rstd[:, 0:T], KD), ALU.mult))
                for k in range(KD):
                    last = stt(xT[:, k, :], o2[:, k, :], g_[:, k:k + 1], xT[:, k, :], ALU.mult, ALU.add)
                last.then_inc(madeV, mark(madeV, out_key))

            residual("post", gain[:, 4, :], "xf2")
            moe_front("f2", gain[:, 5, :], mod2[:, 24:32, 0], 32)
            run_experts(v, 2, one(2))
            residual("postf", gain[:, 0, :], "xout")
    return counts.values


_SQUEEZE = ["ada_w", "ada_b", "norm1_g", "w_in", "ssm_lam_re", "ssm_lam_im", "ssm_log_dt", "ssm_b_re", "ssm_b_im",
            "ssm_c_re", "ssm_c_im", "ssm_d", "ssm_w_glu", "ssm_w_o", "nsa_cmp_pos", "nsa_cmp_w1", "nsa_cmp_w2",
            "nsa_w_o", "w_out", "norm2_g", "moe_w_group", "moe_b_group", "moe_w_expert", "moe_b_expert",
            "moe_w_gate", "moe_w_up", "moe_w_down", "w_mod_2", "b_mod_2", "g_pre_mix_2", "g_post_mix_2",
            "g_pre_ffn_2", "g_post_ffn_2", "w_in_2", "rpb_2", "g_qnorm_2", "g_knorm_2", "w_out_a_2", "w_out_b_2",
            "w_o_2", "w_router_2", "b_router_2", "w_gu_2", "b_gu_2", "w_dn_2", "b_dn_2"]
_SMALLER = ["x", "ctx_2"]
_PLAIN = ["c", "final_g", "c_2", "c_ctx_2"]


def kernel(**inputs):
    import concourse.bacc as _bacc
    from concourse.bass_utils import run_bass_kernel_spmd as _run

    arrays, shapes = {}, {}
    for name in _SQUEEZE + _SMALLER + _PLAIN:
        a = np.ascontiguousarray(inputs[name])
        if name not in _PLAIN:
            a = a.reshape(a.shape[1:])
        arrays[f"in_{name}_dram"] = a
        shapes[name] = a.shape
    arrays["constants_dram"] = CONST_ARRAY
    known = None
    for _ in range(2):
        nc = _bacc.Bacc("TRN2", target_bir_lowering=False, num_devices=1)
        A = {name: nc.dram_tensor(f"in_{name}_dram", shape, F32, kind="ExternalInput").ap()
             for name, shape in shapes.items()}
        const = nc.dram_tensor("constants_dram", CONST_ARRAY.shape, F32, kind="ExternalInput").ap()
        out = nc.dram_tensor("out_0_dram", (T, D), F32, kind="ExternalOutput").ap()
        known = program(nc, A, const, out, known)
    r = _run(nc, [arrays], core_ids=[0])
    return r.results[0]["out_0_dram"].reshape(1, T, D)
```

```python
from contextlib import ExitStack

import numpy as np
import concourse.bass as bass
from concourse import mybir

F32 = mybir.dt.float32
I32 = mybir.dt.int32
ALU = mybir.AluOpType
ACT = mybir.ActivationFunctionType
AX = mybir.AxisListType

P = 128
T = 256
D = 1024
KD = D // P
TT = T // P
HD = 64
NCMP = 15
EPS = 1e-6
NEG = -1e30
E = 32
SLOTS = 64
MAXB = T // SLOTS
RING = 12
SLOT = 2048
TWO_PI = 2 * np.pi
SIN2PI = 6.283185
MAGIC = 1.5 * 2.0 ** 23

CONST = {}


def constants():
    p = np.arange(P)
    parts = {}
    parts["ident"] = np.eye(P)
    parts["ones"] = np.ones((P, P))
    parts["causal"] = np.where(p[None, :] > p[:, None], NEG, 0.0)
    t = (np.arange(TT)[None, :] * P + p[:, None])
    end = np.arange(NCMP) * 16 + 31
    parts["cmpmask"] = np.where(end[None, None, :] <= t[:, :, None], 0.0, NEG).reshape(P, -1)
    parts["cmprow"] = (t >= 31).astype(np.float64)
    parts["before"] = (p[:, None] < p[None, :]).astype(np.float64)
    mirror = np.zeros((P, P))
    mirror[p, (p // 64) * 64 + 63 - p % 64] = 1.0
    parts["mirror"] = mirror
    parts["time"] = np.broadcast_to(np.arange(T)[None, :], (P, T))
    col = 63 - p % 64
    c0 = np.clip(col - 8, 0, 48)
    kc = np.arange(64)
    parts["namask"] = np.where((kc[None, :] >= c0[:, None]) & (kc[None, :] < c0[:, None] + 16), 0.0, NEG)
    nf = 16
    freqs = 10000.0 ** (-np.arange(nf) / nf)
    row, cl = t // 64, t % 64
    angr, angc = row[:, :, None] * freqs, cl[:, :, None] * freqs
    parts["ropecos"] = np.concatenate([np.cos(angr), np.cos(angr), np.cos(angc), np.cos(angc)], -1).reshape(P, -1)
    parts["ropesin"] = np.concatenate([-np.sin(angr), np.sin(angr), -np.sin(angc), np.sin(angc)], -1).reshape(P, -1)
    parts["parity"] = ((p[:, None] // 16) % 2 == (p[None, :] // 64)).astype(np.float64)
    parts["half"] = (p[:, None] // 64 == np.arange(2)[None, :]).astype(np.float64)
    at, cols = 0, []
    for name, a in parts.items():
        CONST[name] = (at, a.shape[1])
        at += a.shape[1]
        cols.append(a)
    return np.ascontiguousarray(np.concatenate(cols, 1).astype(np.float32))


CONST_ARRAY = constants()
NCONST = CONST_ARRAY.shape[1]


class Counts:

    def __init__(self, known):
        self.known, self.names, self.values, self.n = known, {}, {}, {}

    def mark(self, sem, key):
        name = self.names[id(sem)]
        assert (name, key) not in self.values, (name, key)
        self.n[name] = self.values[name, key] = self.n.get(name, 0) + 1
        return 1

    def nth(self, sem, key):
        return 1 if self.known is None else self.known[self.names[id(sem)], key]


def program(nc, A, const, out, known):
    counts = Counts(known)
    mark, nth = counts.mark, counts.nth
    with ExitStack() as ctx:
        def sb(name, shape, dt=F32):
            return ctx.enter_context(nc.sbuf_tensor(name, shape, dt))

        def sem(name):
            return ctx.enter_context(nc.semaphore(name))

        def signal(name):
            s = sem(name)
            counts.names[id(s)] = name
            return s

        K = sb("consts", [P, NCONST])

        def cst(name, a=None, b=None):
            at, n = CONST[name]
            return K[:, at + (a or 0):at + (n if b is None else b)]

        ring = sb("ring", [P, RING, SLOT])
        xT = sb("xT", [P, KD, T])
        hT = sb("hT", [P, KD, 2 * T])
        hN = sb("hN", [P, TT, D])
        packs = sb("packs", [P, 3, P])
        cols = sb("cols", [P, 3, P])
        csil = sb("csil", [P, 24])
        mod1 = sb("mod1", [P, 48])
        mod2 = sb("mod2", [P, 48, 2])
        gain = sb("gain", [P, 6, KD])
        wr1 = sb("wr1", [P, KD, 36])
        wr2 = sb("wr2", [P, KD, 32])
        rb = sb("rb", [1, 68])
        w2c = sb("w2c", [P, 2, 2, HD])
        gqk = sb("gqk", [P, 2, HD])
        rstd = sb("rstd", [P, 2 * T])
        ARENA = 16100
        arena = sb("arena", [P, ARENA])
        ps = ctx.enter_context(nc.psum_tensor("ps", [P, 8, 512], F32))

        def carve(at, *shape):
            n = int(np.prod(shape))
            assert at + n <= ARENA, (at, n)
            v = arena[:, at:at + n]
            if len(shape) == 2:
                v = v.rearrange("p (a b) -> p a b", b=shape[1])
            if len(shape) == 3:
                v = v.rearrange("p (a b c) -> p a b c", b=shape[1], c=shape[2])
            return v

        class Lay:
            def __init__(self, at=0):
                self.at = at

            def __call__(self, *shape):
                v = carve(self.at, *shape)
                self.at += int(np.prod(shape))
                return v

        L = Lay()
        qT = L(KD, T)
        kslc = L(4, T)
        kwin = L(4, T)
        vslc = L(TT, 256)
        vwin = L(TT, 256)
        gates = L(TT, 48)
        uT = L(4, T)
        kcT = L(60)
        vcN = L(4, HD)
        s_at = L.at
        kcmp = hN[:, 0, :].rearrange("p (g t) -> p g t", t=T)
        vcmp = hN[:, 1, :].rearrange("p (g t) -> p g t", t=T)
        bbT = L(2, 4, P)
        cT = L(2, 4, P)
        yT = L(4, T)
        fr = [L(T), L(T)]
        tabs = [L(2, T), L(2, T)]
        sa = L(2, T)
        sb_ = L(2, T)
        sw = L(2, T)
        sz = L(2, T)
        ss2 = [L(2, T), L(2, T)]
        hid = L(2, 2, 60)
        cbias = L(4)
        small = L(24, 16)
        assert L.at <= ARENA, L.at
        cpad1 = hN[:, 0, 0:KD * 32].rearrange("p (k c) -> p k c", c=32)
        cpad2 = L(KD, 32)
        mod_rows = [hT[:, 2 * i:2 * i + 2, T:2 * T] for i in range(3)]
        bd = carve(0, 2, 4 * P)
        cR = carve(1024, 2, 4 * P)
        bR = carve(2048, 2, 256)
        bbuf = carve(2560, 2, 256)
        LA = Lay(s_at)
        Eb = [LA(1024), LA(1024)]
        PT = [LA(1024), LA(1024)]
        sgl = LA(2, 2, T)
        mgd = hN[:, :, :].rearrange("p a b -> p (a b)").rearrange("p (k t) -> p k t", t=T)
        yS = LA(4, T)
        oT = LA(KD, T)
        stat = sb("stat", [P, 2, 16])
        rn = sb("rn", [P, 24])
        dt2 = sb("dt2", [P, 2])
        L2 = Lay()
        kaT = L2(4, 2 * T)
        qaT = L2(4, T)
        qbT = L2(4, T)
        kbT = L2(2, 2 * T)
        vN = L2(4, 512)
        vbN = L2(4, P)
        o2 = L2(KD, T)
        at2 = L2.at
        E2 = [L2(1024), L2(1024)]
        PT2 = [L2(1024), L2(1024)]
        nab2 = L2(8, T)
        L3 = Lay(at2)
        qbN = L3(TT, 512)
        qt1 = L3(TT, 512)
        qt2 = L3(TT, 512)
        kbN = L3(4, P)
        kt1 = L3(4, P)
        M = Lay()
        biasB = M(3072)
        xsF, xsM = M(KD, SLOTS), M(KD, SLOTS)
        ohgF, ohgM = M(TT, SLOTS), M(TT, SLOTS)
        ohsF, ohsM = M(TT, P), M(TT, P)
        ohtF, ohtM = [M(T), M(T)], M(T)
        ysF, ysM = M(512), M(512)
        glu = M(512)
        lin = M(512)
        sg = M(512)
        act = M(512)
        actT = M(4, P)
        esel = [M(SLOTS), M(SLOTS)]
        zero = M(512)
        lg = M(TT, 36)
        Am = M(TT, E)
        Wt = M(TT, E + 2)
        sel = M(TT, E + 2)
        t1 = M(E * E)
        t2 = M(E * E)
        gx = M(TT, 8)
        m8 = M(TT, 8)
        rt = M(TT, 16)
        crow = M(4, E)
        tabI = sb("tabI", [1, 2, E], I32)

        def wcols(name, a, b):
            w = A[name][:, a:b].rearrange("(k p) c -> p k c", p=P)
            return w

        chunks = []

        def chunk(key, src, *shape):
            chunks.append((key, src, shape))

        for c in range(24):
            chunk(("mod1", c), wcols("ada_w", c * 256, c * 256 + 256), KD, 256)
        IN1 = [("u", 0, 2608), ("u", 1, 2864)] + [("q", c, c * 256) for c in range(4)] + \
              [("kcmp", 0, 1024), ("vcmp", 0, 1280), ("kslc", 0, 1536), ("kwin", 0, 2048),
               ("vslc", 0, 1792), ("vwin", 0, 2304)]
        for n, c, at in IN1:
            chunk((n, c), wcols("w_in", at, at + 256), KD, 256)
        chunk(("ng", 0), wcols("w_in", 2560, 2608), KD, 48)
        for kv in range(2):
            w = A["nsa_cmp_w1"][kv].rearrange("(c p) h -> p c h", p=P)
            for c in range(2):
                chunk(("cw1", kv, c), w[:, 8 * c:8 * c + 8, :], 8, 256)
        chunk(("glu", 0), A["ssm_w_glu"].rearrange("(k p) c -> p k c", p=P), 4, 512)
        for c in range(24):
            chunk(("mod2", c), wcols("w_mod_2", c * 256, c * 256 + 256), KD, 256)
        for c in range(4):
            chunk(("mga", c), wcols("w_in", 3120 + c * 256, 3376 + c * 256), KD, 256)
            chunk(("mgs", c), wcols("w_in", 4144 + c * 256, 4400 + c * 256), KD, 256)
            chunk(("no", c), wcols("nsa_w_o", c * 256, c * 256 + 256), KD, 256)
            if c % 2 == 0:
                chunk(("so", c // 2), A["ssm_w_o"][:, c * 256:c * 256 + 512].rearrange("(k p) c -> p k c", p=P), 4, 512)
        for c in range(4):
            chunk(("wo", c), wcols("w_out", c * 256, c * 256 + 256), KD, 256)
        n_front1 = len(chunks)
        moe1_at = n_front1
        front2_at = moe1_at + 3 * E
        n1 = len(chunks)
        IN2 = [("ka", 0, 0), ("ka", 1, 256), ("va", 0, 512), ("va", 1, 768), ("kvb", 0, 1024),
               ("qa", 0, 1280), ("qa", 1, 1536), ("qb", 0, 1792), ("qb", 1, 2048)]
        for n, c, at in IN2:
            chunk((n + "2", c), wcols("w_in_2", at, at + 256), KD, 256)
        for c in range(4):
            chunk(("ga2", c), wcols("w_in_2", 2304 + c * 256, 2560 + c * 256), KD, 256)
            chunk(("gb2", c), wcols("w_in_2", 3328 + c * 256, 3584 + c * 256), KD, 256)
            if c % 2 == 0:
                for x in "ab":
                    chunk(("oo" + x, c // 2), A["w_out_" + x + "_2"][:, c * 256:c * 256 + 512].rearrange("(k p) c -> p k c", p=P), 4, 512)
        for c in range(4):
            chunk(("w_o2", c), wcols("w_o_2", c * 256, c * 256 + 256), KD, 256)
        moe2_at = front2_at + len(chunks) - n1
        index = {}
        for i, (key, _, _) in enumerate(chunks):
            index[key] = i if i < n1 else front2_at + i - n1

        full = [sem(f"ring_full{s}") for s in range(RING)]
        freed = sem("ring_freed")

        def slot_ap(i, shape):
            v = ring[:, i % RING, 0:int(np.prod(shape))]
            return v.rearrange("p (a b) -> p a b", b=shape[1])

        def weights(eng, key):
            i = index[key]
            eng.wait_ge(full[i % RING], 16 * (i // RING + 1))
            return slot_ap(i, chunks[i if i < n1 else i - front2_at + n1][2])

        def load(sp, key, i, src, shape):
            if i >= RING:
                sp.wait_ge(freed, i - RING + 1)
            sp.dma_start(slot_ap(i, shape), src).then_inc(full[i % RING], 16)

        small_in = sem("small_in")
        ctx_in = sem("ctx_in")
        bias_in = [sem("bias_in0"), sem("bias_in1")]
        biasb_in = sem("expert_biases_in")
        xin = sem("x_in")
        filled = signal("psum_filled")
        emptied = signal("psum_emptied")
        vemptied = signal("psum_emptied_by_vector")
        madeV = signal("made_by_vector")
        madeA = signal("made_by_scalar")
        out_sem = sem("out_stored")
        STEPS = ("gather_onehot", "gathered", "xs", "spread_onehot", "spreadT", "spread", "hidden", "glu", "sig",
                 "act", "turned", "actT", "down", "ys", "scattered")
        S = {(n, kind): {x: sem(f"moe{n}_{kind}_{x}") for x in STEPS} for n in (1, 2) for kind in ("first", "more")}
        used2 = sem("moe2_rows_used")

        def run_experts(eng, n, further, first, begin=lambda *_: None):
            U = 4 if n == 1 else 2
            with eng.Fori(0, E // U) as it:
                for u in range(U):
                    e = it * U + u
                    more = eng.value_load(tabI[0:1, 0, bass.ds(e, 1)], min_val=0, max_val=MAXB - 1)
                    before = eng.value_load(tabI[0:1, 1, bass.ds(e, 1)], min_val=0, max_val=E * (MAXB - 1))
                    begin(it, u, e)
                    with eng.If(more > 0):
                        with eng.Fori(0, more) as b:
                            further(it, u, e, before + b, b + 1)
                    first(it, u, e)

        block = ctx.enter_context(nc.Block())
        pending = [0]

        def mm(*a, start, stop, **k):
            ins = nc.tensor.matmul(*a, start=start, stop=stop, **k)
            if pending[0] and start and not stop:
                ins.then_inc(freed, pending[0])
                pending[0] = 0
            return ins


        @block.sync
        def _(sp):
            sp.dma_start(K[:, :], const[:, :]).then_inc(xin, 16)
            sp.dma_start(hN[:, :, :], A["x"].rearrange("(a p) d -> p a d", p=P)).then_inc(xin, 16)
            for i in range(n1):
                key, src, shape = chunks[i]
                load(sp, key, i, src, shape)
            def load_moe1(e, u, wait):
                for j, nm in enumerate(("gate", "up", "down")):
                    i = moe1_at + 3 * u + j
                    wait(i, j)
                    src = A["moe_w_" + nm][bass.ds(e, 1)].rearrange("e (k p) c -> p (e k) c", p=P)
                    sp.dma_start(slot_ap(i, (KD, 256) if j < 2 else (2, D)), src).then_inc(full[i % RING], 16)

            s1, s2 = S[1, "first"], S[2, "first"]
            for u in range(4):
                load_moe1(u, u, lambda i, j: sp.wait_ge(freed, i - RING + 1))
            with sp.Fori(1, E // 4) as it:
                for u in range(4):
                    e = it * 4 + u
                    load_moe1(e, u, lambda i, j: sp.wait_ge(s1["hidden" if j < 2 else "down"], e - 3))
            for i in range(n1, len(chunks)):
                key, src, shape = chunks[i]
                at = index[key]
                if at - RING < front2_at:
                    e, j = divmod(at - RING - moe1_at, 3)
                    sp.wait_ge(s1["hidden" if j < 2 else "down"], e + 1)
                else:
                    sp.wait_ge(freed, n1 + at - RING - front2_at + 1)
                sp.dma_start(slot_ap(at, shape), src).then_inc(full[at % RING], 16)

            def load_moe2(e, wait):
                for j in range(12):
                    i = moe2_at + j
                    wait(i, j)
                    if j < 8:
                        src = A["w_gu_2"][bass.ds(e, 1), j * P:(j + 1) * P, :].rearrange("e p c -> p (e c)")
                        sp.dma_start(ring[:, i % RING, :], src).then_inc(full[i % RING], 16)
                    else:
                        src = A["w_dn_2"][bass.ds(e, 1), (j - 8) * 256:(j - 7) * 256, :].rearrange("e (k p) c -> p (e k) c", p=P)
                        sp.dma_start(slot_ap(i, (2, D)), src).then_inc(full[i % RING], 16)

            def free2(e, j):
                if j == 7:
                    sp.wait_ge(s2["hidden"], e)
                elif j == 11:
                    sp.wait_ge(s2["down"], e)
                else:
                    sp.wait_ge(used2, 10 * e - 10 + (j + 1 if j < 7 else j))

            load_moe2(0, lambda i, j: sp.wait_ge(freed, n1 + i - RING - front2_at + 1))
            with sp.Fori(1, E) as e:
                load_moe2(e, lambda i, j: free2(e, j))
            sp.wait_ge(madeA, nth(madeA, "out"))
            for a in range(TT):
                sp.dma_start(out.rearrange("(a p) d -> p a d", p=P)[:, a, :], hN[:, a, :]).then_inc(out_sem, 16)
            sp.wait_ge(out_sem, 16 * TT)

        smalls = []

        def rows(pk, at, src, n):
            smalls.append((packs[at:at + n, pk, :], src.rearrange("(r c) -> r c", c=P)))

        rows(0, 0, A["ada_b"], 48)
        rows(0, 48, A["norm1_g"], 8)
        rows(0, 56, A["norm2_g"], 8)
        rows(0, 64, A["final_g"], 8)
        rows(0, 72, A["nsa_cmp_pos"].rearrange("a l h -> (a l h)"), 32)
        rows(0, 104, A["c"].rearrange("a d -> (a d)"), 8)
        rows(0, 112, A["c_2"].rearrange("a d -> (a d)"), 8)
        rows(0, 120, A["c_ctx_2"], 8)
        rows(1, 0, A["b_mod_2"], 48)
        for n, k in enumerate(("g_pre_mix_2", "g_post_mix_2", "g_pre_ffn_2", "g_post_ffn_2")):
            rows(1, 48 + 8 * n, A[k], 8)
        rows(2, 0, A["ssm_lam_re"].rearrange("g p -> (g p)"), 16)
        rows(2, 16, A["ssm_lam_im"].rearrange("g p -> (g p)"), 16)
        ldt = A["ssm_log_dt"].rearrange("(j s) -> j s", s=2)
        smalls.append((dt2[32:48, :], ldt))
        rows(2, 48, A["ssm_d"].rearrange("g h -> (g h)"), 4)
        smalls.append((packs[80:128, 1, :], A["ada_b"].rearrange("(r c) -> r c", c=P)))
        smalls.append((packs[52:128, 2, :], const[0:76, 0:P]))
        for n, k in enumerate(("ssm_b_re", "ssm_b_im")):
            smalls.append((bR[:, n, :].rearrange("p (j h) -> p j h", h=16),
                           A[k].rearrange("g p h -> (g p) h").rearrange("(j q) h -> q j h", q=P)))
        for n, k in enumerate(("ssm_c_re", "ssm_c_im")):
            src = A[k].rearrange("g h p -> (g h) p").rearrange("(t q) p -> q t p", q=P)
            dst = cR[:, n, :].rearrange("p (t s c) -> p t s c", t=4, s=2)
            smalls += [(dst[:, :, 0, :], src), (dst[:, :, 1, :], src)]
        smalls.append((wr1[:, :, 0:4], A["moe_w_group"].rearrange("(k p) c -> p k c", p=P)))
        smalls.append((wr1[:, :, 4:36], A["moe_w_expert"].rearrange("(k p) c -> p k c", p=P)))
        smalls.append((wr2[:, :, :], A["w_router_2"].rearrange("(k p) c -> p k c", p=P)))
        smalls.append((rb[:, 0:4], A["moe_b_group"].rearrange("(a c) -> a c", a=1)))
        smalls.append((rb[:, 4:36], A["moe_b_expert"].rearrange("(a c) -> a c", a=1)))
        smalls.append((rb[:, 36:68], A["b_router_2"].rearrange("(a c) -> a c", a=1)))
        for kv in range(2):
            smalls.append((w2c[:, kv, :, :], A["nsa_cmp_w2"][kv].rearrange("(k p) c -> p k c", p=P)))
        for n, k in enumerate(("g_qnorm_2", "g_knorm_2")):
            smalls.append((gqk[:, n, :], A[k][None, :].broadcast_to([P, HD])))
        SMALL = 16 * len(smalls)

        @block.gpsimd
        def _(g):
            for dst, src in smalls:
                g.dma_start(dst, src).then_inc(small_in, 16)
            g.wait_ge(madeV, nth(madeV, "moe1 out"))
            g.dma_start(hN[:, :, :], A["ctx_2"].rearrange("(a p) d -> p a d", p=P)).then_inc(ctx_in, 16)
            for tt in range(TT):
                if tt == 1:
                    g.wait_ge(filled, nth(filled, ("S", 2, 3)))
                for h in range(8):
                    for r in range(2):
                        row = 2 * tt + r
                        src = bass.AP(tensor=A["rpb_2"].tensor, offset=h * 465 + (7 - row) * 31 + 15 - 63,
                                      ap=[[1, 64], [31, 4], [1, 64]])
                        g.dma_start(nab2[64 * r:64 * r + 64, h, :].rearrange("p (a b) -> p a b", b=64), src).then_inc(bias_in[tt], 16)
            g.wait_ge(madeV, nth(madeV, "biasB"))
            g.dma_start(biasB[0:E, 0:2048], A["b_gu_2"]).then_inc(biasb_in, 16)
            g.dma_start(biasB[0:E, 2048:3072], A["b_dn_2"]).then_inc(biasb_in, 16)

        units1 = [(g, tt, a) for g in range(4) for tt in range(TT) for a in ("cmp", "slc", "win")]
        units2 = [(a, hp, tt) for tt in range(TT) for a in ("na", "gqa") for hp in range(4)]

        @block.tensor
        def _(pe):
            ident = cst("ident")
            ones = cst("ones")

            def free_chunk(ins):
                ins.then_inc(freed, 1)

            def transpose(dst, src):
                return nc.tensor.transpose(dst, src, ident[0:src.shape[0], 0:src.shape[0]])

            pe.wait_ge(xin, 32)
            for tt in range(TT):
                for k in range(KD):
                    last = transpose(ps[:, 1 + tt * 2 + k // 4, (k % 4) * P:(k % 4 + 1) * P], hN[:, tt, k * P:(k + 1) * P])
            last.then_inc(filled, mark(filled, "x"))
            pe.wait_ge(small_in, SMALL)
            pe.wait_ge(madeV, nth(madeV, "dt rows"))
            for n in range(3):
                last = transpose(ps[:, 0, n * P:(n + 1) * P], packs[:, n, :])
            last.then_inc(filled, mark(filled, "cols"))

            def sumsq(key, bank, sq, n=T):
                pe.wait_ge(madeA, nth(madeA, ("sq", key)))
                for k in range(KD):
                    last = mm(ps[:, bank, 0:n], ones, sq[:, k, :], start=k == 0, stop=k == KD - 1)
                last.then_inc(filled, mark(filled, ("ss", key)))

            sumsq("n1", 5, hT[:, :, T:2 * T])
            def modulation(key, c, cpad, bank):
                w = weights(pe, (key, c))
                at = (c // 2 % 4) * P
                for k in range(KD):
                    for m in range(2):
                        r = 32 * (2 * (c % 2) + m)
                        last = mm(ps[r:r + 32, bank, at:at + P], cpad[:, k, :], w[:, k, m * P:(m + 1) * P],
                                  start=k == 0, stop=k == KD - 1)
                if c % 8 == 7:
                    last.then_inc(filled, mark(filled, (key, "rows", c // 8)))
                pending[0] += 1

            def turn_modulation(bank):
                for b in range(12):
                    last = transpose(ps[:, bank + b // 4, (b % 4) * P:(b % 4 + 1) * P],
                                     hT[:, b // 2, T + (b % 2) * P:T + (b % 2 + 1) * P])
                return last

            pe.wait_ge(madeV, nth(madeV, "csil"))
            for c in range(24):
                if c == 12:
                    pe.wait_ge(madeV, nth(madeV, "bd"))
                    for n in range(2):
                        for q in range(4):
                            last = transpose(ps[:, 4 + n, q * P:(q + 1) * P], bd[:, n, q * P:(q + 1) * P])
                    last.then_inc(filled, mark(filled, "bbT"))
                    for n in range(2):
                        for q in range(4):
                            last = transpose(ps[:, n, q * P:(q + 1) * P], cR[:, n, q * P:(q + 1) * P])
                    last.then_inc(filled, mark(filled, "cT"))
                modulation("mod1", c, cpad1, (2, 6, 7)[c // 8])
            pe.wait_ge(emptied, nth(emptied, ("mod1", 2)))
            turn_modulation(5).then_inc(filled, mark(filled, "mod1"))

            pe.wait_ge(madeV, nth(madeV, "h1"))
            turn = [0]

            def take_bank():
                b = turn[0] % 4
                g = turn[0]
                if g >= 4:
                    pe.wait_ge(emptied, nth(emptied, ("p1", g - 4)))
                else:
                    pe.wait_ge(emptied, nth(emptied, "cT"))
                turn[0] += 1
                return b, g

            def projT(key, c):
                w = weights(pe, (key, c))
                b, g = take_bank()
                for m in range(2):
                    for k in range(KD):
                        last = mm(ps[:, b, m * T:(m + 1) * T], w[:, k, m * P:(m + 1) * P], hT[:, k, 0:T],
                                  start=k == 0, stop=k == KD - 1)
                last.then_inc(filled, mark(filled, ("p1", g)))
                return last

            def projdup(key, half, last_half=True):
                w = weights(pe, (key, 0))
                b, g = take_bank()
                for m in range(2):
                    gg = 2 * half + m
                    for k in range(KD):
                        for s in range(2):
                            last = mm(ps[64 * s:64 * s + 64, b, m * T:(m + 1) * T], w[:, k, gg * 64:gg * 64 + 64],
                                      hT[:, k, 0:T], start=k == 0, stop=k == KD - 1)
                last.then_inc(filled, mark(filled, ("p1", g)))

            def projN(key, n):
                w = weights(pe, (key, 0))
                b, g = take_bank()
                for tt in range(TT):
                    for k in range(KD):
                        last = mm(ps[:, b, tt * n:(tt + 1) * n], hT[:, k, tt * P:(tt + 1) * P], w[:, k, :],
                                  start=k == 0, stop=k == KD - 1)
                last.then_inc(filled, mark(filled, ("p1", g)))

            def ssm_in(j):
                if j >= 2:
                    pe.wait_ge(vemptied, nth(vemptied, ("bu", j - 2)))
                elif j == 0:
                    pe.wait_ge(emptied, nth(emptied, ("p1", 1)))
                q, r = j // 4, 32 * (j % 4)
                for n in range(2):
                    last = mm(ps[:, 4 + j % 2, n * T:(n + 1) * T], bbT[r:r + 32, n, q, :], uT[r:r + 32, q, :],
                              start=True, stop=True)
                last.then_inc(filled, mark(filled, ("bu", j)))

            def ssm_out(j):
                pe.wait_ge(madeV, nth(madeV, ("s", j)))
                q, r = j // 4, 32 * (j % 4)
                for n in range(2):
                    last = mm(ps[r:r + 32, 6 + q // 2, (q % 2) * T:(q % 2 + 1) * T], cT[:, n, q, r:r + 32],
                              ss2[j % 2][:, n, :], start=n == 0, stop=n == 1)
                last.then_inc(filled, mark(filled, ("y", j)))

            done_j = [0, 0]

            def ssm_step():
                if done_j[0] < 16:
                    ssm_in(done_j[0])
                    done_j[0] += 1
                if done_j[0] >= 3 and done_j[1] < 16:
                    ssm_out(done_j[1])
                    done_j[1] += 1

            def freeing(n=1):
                pending[0] += n

            for n, c, _ in IN1:
                if n in ("u", "q"):
                    projT(n, c)
                elif n in ("kcmp", "vcmp", "kslc", "kwin"):
                    projdup(n, 0)
                    ssm_step()
                    projdup(n, 1)
                else:
                    projN(n, 256)
                freeing()
                if n != "u":
                    ssm_step()
            projN("ng", 48)
            freeing()
            pe.wait_ge(emptied, nth(emptied, ("p1", turn[0] - 1)))
            for kv in range(2):
                src = (kcmp, vcmp)[kv]
                w = [weights(pe, ("cw1", kv, c)) for c in range(2)]
                for m in range(2):
                    for c in range(16):
                        last = mm(ps[:, kv, m * 60:(m + 1) * 60], w[c // 8][:, c % 8, m * P:(m + 1) * P],
                                  src[:, :, 2 * c:2 * c + 16 * 14 + 1:16], start=c == 0, stop=c == 15)
                for m in range(2):
                    for c in range(16):
                        last = mm(ps[:, kv, 128 + m:129 + m], w[c // 8][:, c % 8, m * P:(m + 1) * P],
                                  cols[:, 0, 72 + 16 * kv + c:73 + 16 * kv + c], start=c == 0, stop=c == 15)
                last.then_inc(filled, mark(filled, ("hid", kv)))
                freeing(2)
            while done_j[1] < 16:
                ssm_step()
            pe.wait_ge(madeA, nth(madeA, "hid"))
            for s in range(2):
                for m in range(2):
                    last = mm(ps[64 * s:64 * s + 64, 2, 0:60], w2c[:, 0, m, :], hid[:, 0, m, :], start=m == 0, stop=m == 1)
            for g in range(4):
                for m in range(2):
                    last = mm(ps[0:NCMP, 3, g * HD:(g + 1) * HD], hid[:, 1, m, g * NCMP:(g + 1) * NCMP], w2c[:, 1, m, :],
                              start=m == 0, stop=m == 1)
            last.then_inc(filled, mark(filled, "kc"))
            pe.wait_ge(madeA, nth(madeA, "ygelu"))
            w = weights(pe, ("glu", 0))
            for m in range(4):
                for k in range(4):
                    last = mm(ps[:, 4 + m // 2, (m % 2) * T:(m % 2 + 1) * T], w[:, k, m * P:(m + 1) * P], yT[:, k, :],
                              start=k == 0, stop=k == 3)
            last.then_inc(filled, mark(filled, "z"))
            freeing()

            def seg(n, u):
                if n == 1:
                    g, tt, a = u
                    return (4, 16 if a == "cmp" else P * (tt + 1))
                return (2, 512)

            def scores(n, i, u):
                b = 2 * (i % 2)
                if i >= 2:
                    pe.wait_ge(madeA, nth(madeA, ("exp", n, i - 2)))
                if n == 1:
                    g, tt, a = u
                    nk = seg(1, u)[1]
                    for s in range(4):
                        par, half = s // 2, s % 2
                        hb = 64 * par
                        q = qT[hb:hb + 64, 2 * g + half, tt * P:(tt + 1) * P]
                        o = ps[:, b + par, half * nk:(half + 1) * nk]
                        if a == "cmp":
                            o = o[:, 0:NCMP]
                            mm(o, q, kcT[hb:hb + 64, g * NCMP:(g + 1) * NCMP], start=True, stop=False)
                            last = mm(o, ident, cst("cmpmask", tt * NCMP, (tt + 1) * NCMP), start=False, stop=True)
                        else:
                            kk = (kslc if a == "slc" else kwin)[hb:hb + 64, g, 0:nk]
                            mm(o, q, kk, start=True, stop=True)
                            last = mm(o[:, nk - P:nk], ident, cst("causal"), start=False, stop=True, skip_group_check=True)
                else:
                    a, hp, tt = u
                    for s in range(2):
                        q = (qaT if a == "na" else qbT)[64 * s:64 * s + 64, hp, tt * P:(tt + 1) * P]
                        kk = kaT[64 * s:64 * s + 64, hp, :] if a == "na" else kbT[64 * s:64 * s + 64, hp // 2, :]
                        o = ps[:, b + s, :]
                        last = mm(o, q, kk, start=True, stop=True)
                        if a == "na":
                            last = mm(o[:, 0:T], cst("mirror"), nab2[:, 2 * hp + s, :], start=False, stop=True, skip_group_check=True)
                last.then_inc(filled, mark(filled, ("S", n, i)))

            def turned(n, i, u):
                pe.wait_ge(madeV, nth(madeV, ("P", n, i)))
                if i >= 1:
                    pe.wait_ge(madeA, nth(madeA, ("PT", n, i - 1)))
                E_ = (Eb if n == 1 else E2)[i % 2]
                ns, nk = seg(n, u)
                if nk == 16:
                    for s in range(ns):
                        last = nc.tensor.transpose(ps[0:NCMP, 4, s * P:(s + 1) * P], E_[:, s * 16:s * 16 + NCMP], ident)
                else:
                    for kb in range(nk // P):
                        for s in range(ns):
                            x = kb * ns + s
                            last = transpose(ps[:, 4 + x // 4, (x % 4) * P:(x % 4 + 1) * P], E_[:, s * nk + kb * P:s * nk + (kb + 1) * P])
                last.then_inc(filled, mark(filled, ("T", n, i)))

            def values(n, i, u):
                pe.wait_ge(madeA, nth(madeA, ("PT", n, i)))
                ns, nk = seg(n, u)
                pt = (PT if n == 1 else PT2)[i % 2].rearrange("p (k s q) -> p k s q", s=ns, q=P)
                if n == 1:
                    g, tt, a = u
                    if a == "cmp" and i >= 3:
                        pe.wait_ge(emptied, nth(emptied, ("O", n, i - 1)))
                    for par in range(2):
                        o = ps[64 * par:64 * par + 64, 6, 0:2 * P]
                        if a == "cmp":
                            last = mm(o, vcN[0:NCMP, g, :], pt[0:NCMP, 0, 2 * par:2 * par + 2, :], start=True, stop=False, skip_group_check=True)
                        else:
                            v = vslc if a == "slc" else vwin
                            for kb in range(nk // P):
                                last = mm(o, v[:, kb, g * HD:(g + 1) * HD], pt[:, kb, 2 * par:2 * par + 2, :], start=False,
                                          stop=a == "win" and kb == nk // P - 1, skip_group_check=True)
                    last.then_inc(filled, mark(filled, ("O", n, i)))
                else:
                    a, hp, tt = u
                    if i >= 2:
                        pe.wait_ge(emptied, nth(emptied, ("O", n, i - 2)))
                    for par in range(2):
                        o = ps[64 * par:64 * par + 64, 6 + i % 2, 0:P]
                        for kb in range(4):
                            h = 2 * hp + par
                            v = vN[:, kb, h * HD:(h + 1) * HD] if a == "na" else vbN[:, kb, (hp // 2) * HD:(hp // 2 + 1) * HD]
                            last = mm(o, v, pt[:, kb, par, :], start=kb == 0, stop=kb == 3)
                    last.then_inc(filled, mark(filled, ("O", n, i)))

            def attention(n, units):
                scores(n, 0, units[0])
                scores(n, 1, units[1])
                turned(n, 0, units[0])
                for i, u in enumerate(units):
                    if i + 2 < len(units):
                        if n == 2 and units[i + 2] == ("na", 0, 1):
                            pe.wait_ge(madeV, nth(madeV, ("bias", 1)))
                        scores(n, i + 2, units[i + 2])
                    if n == 1:
                        if i % 8 == 0 and i > 0:
                            pe.wait_ge(emptied, nth(emptied, ("mod2", i // 8 - 1)))
                        modulation("mod2", i, cpad2, 7)
                    if i + 1 < len(units):
                        turned(n, i + 1, units[i + 1])
                    values(n, i, u)

            pe.wait_ge(madeA, nth(madeA, "kc"))
            pe.wait_ge(madeA, nth(madeA, "ysig"))
            attention(1, units1)

            pe.wait_ge(emptied, nth(emptied, ("O", 1, len(units1) - 1)))
            pe.wait_ge(emptied, nth(emptied, ("mod2", 2)))
            turn_modulation(4).then_inc(filled, mark(filled, "mod2"))
            pe.wait_ge(madeV, nth(madeV, "yS"))
            so = None
            for c in range(4):
                if c >= 1:
                    pe.wait_ge(madeV, nth(madeV, ("mgd", c - 1)))
                if c % 2 == 0:
                    so = weights(pe, ("so", c // 2))
                for n, key in enumerate(("mga", "mgs")):
                    w = weights(pe, (key, c))
                    for m in range(2):
                        for k in range(KD):
                            last = mm(ps[:, 2 + n, m * T:(m + 1) * T], w[:, k, m * P:(m + 1) * P], hT[:, k, 0:T],
                                      start=k == 0, stop=k == KD - 1)
                last.then_inc(filled, mark(filled, ("gates", c)))
                w = weights(pe, ("no", c))
                for m in range(2):
                    for k in range(KD):
                        last = mm(ps[:, 0, m * T:(m + 1) * T], w[:, k, m * P:(m + 1) * P], oT[:, k, :],
                                  start=k == 0, stop=k == KD - 1)
                for m in range(2):
                    mc = (c % 2) * 2 + m
                    for k in range(4):
                        last = mm(ps[:, 1, m * T:(m + 1) * T], so[:, k, mc * P:(mc + 1) * P], yS[:, k, :],
                                  start=k == 0, stop=k == 3)
                last.then_inc(filled, mark(filled, ("branch", c)))
                freeing(3 if c % 2 == 0 else 4)
            for c in range(4):
                if c == 0:
                    pe.wait_ge(madeV, nth(madeV, ("mgd", 3)))
                w = weights(pe, ("wo", c))
                for m in range(2):
                    for k in range(KD):
                        last = mm(ps[:, 4 + c, m * T:(m + 1) * T] if c < 4 else None, w[:, k, m * P:(m + 1) * P], mgd[:, k, :],
                                  start=k == 0, stop=k == KD - 1)
                last.then_inc(filled, mark(filled, ("tm", c)))
                freeing()

            def moe_front(n, wr, nr, rbias):
                key = f"f{n}"
                sumsq(key, 0, hT[:, :, T:2 * T])
                pe.wait_ge(madeV, nth(madeV, "h" + key))
                for tt in range(TT):
                    for k in range(KD):
                        last = transpose(ps[:, 1 + tt * 2 + k // 4, (k % 4) * P:(k % 4 + 1) * P], hT[:, k, tt * P:(tt + 1) * P])
                last.then_inc(filled, mark(filled, "hN" + key))
                for tt in range(TT):
                    for k in range(KD):
                        mm(ps[:, 5, tt * 64:tt * 64 + nr], hT[:, k, tt * P:(tt + 1) * P], wr[:, k, :], start=k == 0, stop=False)
                    last = mm(ps[:, 5, tt * 64:tt * 64 + nr], ones[0:1, :], rbias, start=False, stop=True)
                last.then_inc(filled, mark(filled, "logits" + key))
                pe.wait_ge(madeV, nth(madeV, "chosen" + key))
                for tt in range(TT):
                    mm(ps[:, 5, 128 + tt * E:128 + (tt + 1) * E], cst("before"), Am[:, tt, :], start=True, stop=tt == 0)
                    if tt == 1:
                        last = mm(ps[:, 5, 128 + E:128 + 2 * E], ones, Am[:, 0, :], start=False, stop=True)
                for tt in range(TT):
                    last = mm(ps[0:1, 5, 256:256 + E], ones[:, 0:1], Am[:, tt, :], start=tt == 0, stop=tt == 1)
                last.then_inc(filled, mark(filled, "places" + key))
                pe.wait_ge(madeV, nth(madeV, "tables" + key))
                for b in range(4):
                    last = mm(ps[:, 4 + b, :], zero[:, 0:P], zero, start=True, stop=True)
                last.then_inc(filled, mark(filled, "zeroed" + key))

            def gather(s, xs_onehot):
                for k in range(KD):
                    for tt in range(TT):
                        last = mm(ps[:, 0, k * SLOTS:(k + 1) * SLOTS], hN[:, tt, k * P:(k + 1) * P], xs_onehot[:, tt, :],
                                  start=tt == 0, stop=tt == 1)
                last.then_inc(s["gathered"], 1)

            def spread_turn(s, onehot):
                for tt in range(TT):
                    last = transpose(ps[:, 1, tt * P:(tt + 1) * P], onehot[:, tt, :])
                last.then_inc(s["spreadT"], 1)

            def scatter(s, ys, onehotT):
                for c in (0, 4, 1, 5, 2, 6, 3, 7):
                    r = 64 * (c // 4)
                    last = mm(ps[:, 4 + c // 2, (c % 2) * T:(c % 2 + 1) * T], ys[r:r + 64, (c % 4) * P:(c % 4 + 1) * P],
                              onehotT[r:r + 64, :], start=False, stop=False, skip_group_check=True)
                last.then_inc(s["scattered"], 1)

            def act_turn(n, s):
                for j in range(4 if n == 2 else 1):
                    last = transpose(ps[:, 3, j * P:(j + 1) * P], act[:, j * P:(j + 1) * P])
                last.then_inc(s["turned"], 1)

            def hidden1(it, u, s, xs):
                i = moe1_at + 3 * u
                for j in range(2):
                    pe.wait_ge(full[(i + j) % RING], it * 16 + 16 * ((i + j) // RING + 1))
                for k in range(KD):
                    for r in range(2):
                        for n in range(2):
                            w = slot_ap(i + n, (KD, 256))
                            last = mm(ps[64 * r:64 * r + 64, 1 + n, 0:P], xs[:, k, :], w[:, k, r * P:(r + 1) * P],
                                      start=k == 0, stop=k == KD - 1)
                last.then_inc(s["hidden"], 1)

            def down1(it, u, s):
                i = moe1_at + 3 * u + 2
                pe.wait_ge(full[i % RING], it * 16 + 16 * (i // RING + 1))
                w = slot_ap(i, (2, D))
                for f in range(2):
                    for r in range(2):
                        last = mm(ps[64 * r:64 * r + 64, 3, :], actT[:, 0, f * 64:(f + 1) * 64], w[:, f, r * 512:(r + 1) * 512],
                                  start=f == 0, stop=f == 1)
                last.then_inc(s["down"], 1)

            def rows2(e, j):
                i = moe2_at + j
                pe.wait_ge(full[i % RING], e * 16 + 16 * (i // RING + 1))
                return slot_ap(i, (2, D))

            def hidden2(e, u, s, xs, first):
                for n in range(2):
                    for r in range(2):
                        mm(ps[64 * r:64 * r + 64, 1 + n, :], esel[u], biasB[:, n * D + r * 512:n * D + (r + 1) * 512],
                           start=True, stop=False)
                for k in range(KD):
                    w = rows2(e, k)
                    for n in range(2):
                        for r in range(2):
                            last = mm(ps[64 * r:64 * r + 64, 1 + n, :], xs[:, k, :], w[:, n, r * 512:(r + 1) * 512],
                                      start=False, stop=k == KD - 1)
                    if k == KD - 1:
                        last.then_inc(s["hidden"], 1)
                    elif first:
                        last.then_inc(used2, 1)

            def down2(e, u, s, first):
                for r in range(2):
                    mm(ps[64 * r:64 * r + 64, 3, :], esel[u], biasB[:, 2048 + r * 512:2048 + (r + 1) * 512], start=True, stop=False)
                for f in range(8):
                    w = rows2(e, 8 + f // 2)
                    for r in range(2):
                        last = mm(ps[64 * r:64 * r + 64, 3, :], actT[:, f % 4, (f // 4) * 64:(f // 4 + 1) * 64],
                                  w[:, f % 2, r * 512:(r + 1) * 512], start=False, stop=f == 7)
                    if first and f % 2 == 1 and f < 7:
                        last.then_inc(used2, 1)
                last.then_inc(s["down"], 1)

            def moe(n):
                s, x = S[n, "first"], S[n, "more"]

                def further(it, u, e, q, b):
                    pe.wait_ge(s["ys"], e + 1)
                    pe.wait_ge(x["gather_onehot"], q + 1)
                    gather(x, ohgM)
                    pe.wait_ge(x["xs"], q + 1)
                    hidden1(it, u, x, xsM) if n == 1 else hidden2(e, u, x, xsM, False)
                    pe.wait_ge(x["act"], q + 1)
                    act_turn(n, x)
                    pe.wait_ge(x["spread_onehot"], q + 1)
                    spread_turn(x, ohsM)
                    pe.wait_ge(x["actT"], q + 1)
                    down1(it, u, x) if n == 1 else down2(e, u, x, False)
                    pe.wait_ge(x["ys"], q + 1)
                    pe.wait_ge(x["spread"], q + 1)
                    scatter(x, ysM, ohtM)

                def first(it, u, e):
                    hidden1(it, u, s, xsF) if n == 1 else hidden2(e, u, s, xsF, True)
                    pe.wait_ge(s["gather_onehot"], e + 2)
                    gather(s, ohgF)
                    pe.wait_ge(s["act"], e + 1)
                    pe.wait_ge(s["ys"], e + 1)
                    act_turn(n, s)
                    pe.wait_ge(s["spread_onehot"], e + 1)
                    spread_turn(s, ohsF)
                    scatter(s, ysF, ohtF[(u + 1) % 2])
                    pe.wait_ge(s["actT"], e + 1)
                    down1(it, u, s) if n == 1 else down2(e, u, s, True)

                def begin(it, u, e):
                    pe.wait_ge(s["xs"], e + 1)
                    pe.wait_ge(s["spread"], e + 1)

                pe.wait_ge(s["gather_onehot"], 1)
                gather(s, ohgF)
                run_experts(pe, n, further, first, begin)
                pe.wait_ge(s["ys"], E + 1)
                pe.wait_ge(s["spread"], E + 1)
                scatter(s, ysF, ohtF[(E - 1) % 2])

            moe_front(1, wr1, 36, rb[0:1, 0:36])
            moe(1)

            last = mm(ps[:, 0, 0:1], ones, csil[:, 0:1], start=True, stop=True)
            last.then_inc(filled, mark(filled, "moe1"))
            sumsq("fin", 0, hT[:, :, T:2 * T])
            sumsq("n2", 0, hT[:, :, T:2 * T])
            pe.wait_ge(ctx_in, 16)
            for tt in range(TT):
                for k in range(KD):
                    last = transpose(ps[:, 1 + tt * 2 + k // 4, (k % 4) * P:(k % 4 + 1) * P], hN[:, tt, k * P:(k + 1) * P])
            last.then_inc(filled, mark(filled, "ctx"))
            pe.wait_ge(madeA, nth(madeA, ("sq", "ctx")))
            for k in range(KD):
                last = mm(ps[:, 5, 0:T], ones, mgd[:, k, :], start=k == 0, stop=k == KD - 1)
            last.then_inc(filled, mark(filled, ("ss", "ctx")))
            pe.wait_ge(madeV, nth(madeV, "h2"))
            pe.wait_ge(madeV, nth(madeV, "hctx"))
            turn2 = [0]

            def bank2():
                g = turn2[0]
                if g >= 4:
                    pe.wait_ge(emptied, nth(emptied, ("p2", g - 4)))
                turn2[0] += 1
                return g % 4, g

            def fill2(outs):
                b, g = bank2()
                for o, lhs, rhs in outs:
                    for k in range(KD):
                        last = mm(o(b), lhs(k), rhs(k), start=k == 0, stop=k == KD - 1)
                last.then_inc(filled, mark(filled, ("p2", g)))

            for c in range(2):
                w = weights(pe, ("ka2", c))
                for m in range(2):
                    fill2([(lambda b: ps[:, b, :], lambda k, m=m: w[:, k, m * P:(m + 1) * P], lambda k: hT[:, k, :])])
                freeing()
            for c in range(2):
                w = weights(pe, ("va2", c))
                for h in range(2):
                    fill2([(lambda b, x=x: ps[:, b, x * 256:(x + 1) * 256],
                            lambda k, x=x, h=h: hT[:, k, (2 * h + x) * P:(2 * h + x + 1) * P], lambda k: w[:, k, :]) for x in range(2)])
                freeing()
            w = weights(pe, ("kvb2", 0))
            for h in range(2):
                fill2([(lambda b, x=x: ps[:, b, x * 256:(x + 1) * 256],
                        lambda k, x=x, h=h: hT[:, k, (2 * h + x) * P:(2 * h + x + 1) * P], lambda k: w[:, k, :]) for x in range(2)])
            freeing()
            for c in range(2):
                w = weights(pe, ("qa2", c))
                fill2([(lambda b, m=m: ps[:, b, m * T:(m + 1) * T], lambda k, m=m: w[:, k, m * P:(m + 1) * P],
                        lambda k: hT[:, k, 0:T]) for m in range(2)])
                freeing()
            for c in range(2):
                w = weights(pe, ("qb2", c))
                fill2([(lambda b, x=x: ps[:, b, x * 256:(x + 1) * 256],
                        lambda k, x=x: hT[:, k, x * P:(x + 1) * P], lambda k: w[:, k, :]) for x in range(2)])
                freeing()
            pe.wait_ge(madeV, nth(madeV, "rope"))
            for tt in range(TT):
                for m in range(4):
                    x = m * TT + tt
                    last = transpose(ps[:, 4 + x // 4, (x % 4) * P:(x % 4 + 1) * P], qbN[:, tt, m * P:(m + 1) * P])
            last.then_inc(filled, mark(filled, "qbT"))
            for kb in range(4):
                last = transpose(ps[:, 6, kb * P:(kb + 1) * P], kbN[:, kb, :])
            for kb in range(4):
                last = transpose(ps[:, 7, kb * P:(kb + 1) * P], kt1[:, kb, :])
            last.then_inc(filled, mark(filled, "kbT"))
            pe.wait_ge(emptied, nth(emptied, "kbT"))
            pe.wait_ge(emptied, nth(emptied, ("p2", turn2[0] - 1)))
            pe.wait_ge(madeV, nth(madeV, ("bias", 0)))
            attention(2, units2)
            pe.wait_ge(emptied, nth(emptied, ("O", 2, len(units2) - 1)))
            for c in range(4):
                if c >= 1:
                    pe.wait_ge(madeV, nth(madeV, ("mgd2", c - 1)))
                for n, key in enumerate(("ga2", "gb2")):
                    w = weights(pe, (key, c))
                    for m in range(2):
                        for k in range(KD):
                            last = mm(ps[:, 2 + n, m * T:(m + 1) * T], w[:, k, m * P:(m + 1) * P], hT[:, k, 0:T],
                                      start=k == 0, stop=k == KD - 1)
                last.then_inc(filled, mark(filled, ("gates2", c)))
                if c % 2 == 0:
                    oo = [weights(pe, ("oo" + x, c // 2)) for x in "ab"]
                for n in range(2):
                    for m in range(2):
                        mc = (c % 2) * 2 + m
                        for k in range(4):
                            last = mm(ps[:, n, m * T:(m + 1) * T], oo[n][:, k, mc * P:(mc + 1) * P], o2[:, 4 * n + k, :],
                                      start=k == 0, stop=k == 3)
                last.then_inc(filled, mark(filled, ("branch2", c)))
                freeing(2 if c % 2 == 0 else 4)
            for c in range(4):
                if c == 0:
                    pe.wait_ge(madeV, nth(madeV, ("mgd2", 3)))
                w = weights(pe, ("w_o2", c))
                for m in range(2):
                    for k in range(KD):
                        last = mm(ps[:, 4 + c, m * T:(m + 1) * T], w[:, k, m * P:(m + 1) * P], mgd[:, k, :],
                                  start=k == 0, stop=k == KD - 1)
                last.then_inc(filled, mark(filled, ("y2", c)))
                freeing()
            sumsq("post", 0, hT[:, :, T:2 * T])
            moe_front(2, wr2, 32, rb[0:1, 36:68])
            pe.wait_ge(biasb_in, 32)
            moe(2)
            last = mm(ps[:, 0, 0:1], ones, csil[:, 0:1], start=True, stop=True)
            last.then_inc(filled, mark(filled, "moe2"))
            sumsq("postf", 0, hT[:, :, T:2 * T])
            pe.wait_ge(madeV, nth(madeV, "xout"))
            for tt in range(TT):
                for k in range(KD):
                    last = transpose(ps[:, 1 + tt * 2 + k // 4, (k % 4) * P:(k % 4 + 1) * P], xT[:, k, tt * P:(tt + 1) * P])
            last.then_inc(filled, mark(filled, "out"))

        @block.scalar
        def _(act_):
            a = nc.scalar.activation

            def copy(dst, src, scale=1.0):
                return a(dst, src, ACT.Copy, scale=scale)

            def sqrt(key, dst):
                act_.wait_ge(madeV, nth(madeV, ("var", key)))
                a(dst, dst, ACT.Sqrt).then_inc(madeA, mark(madeA, ("std", key)))

            def square(key, src):
                a(hT[:, :, T:2 * T], src, ACT.Square).then_inc(madeA, mark(madeA, ("sq", key)))

            def four_banks(dst_of):
                for tt in range(TT):
                    for q in range(2):
                        src = ps[:, 1 + tt * 2 + q, :]
                        last = copy(dst_of(tt, q), src)
                return last

            act_.wait_ge(filled, nth(filled, "x"))
            for tt in range(TT):
                for q in range(2):
                    last = copy(xT[:, 4 * q:4 * q + 4, tt * P:(tt + 1) * P], ps[:, 1 + tt * 2 + q, :].rearrange("p (k t) -> p k t", t=P))
            act_.drain()
            square("n1", xT[:, :, :])
            act_.wait_ge(filled, nth(filled, "cols"))
            copy(cols[:, :, :].rearrange("p a b -> p (a b)"), ps[:, 0, 0:3 * P])
            act_.drain()
            a(csil[:, :], cols[:, 0, 104:128], ACT.Sigmoid).then_inc(madeA, mark(madeA, "cols"))
            a(small[:, 0, :], cols[:, 2, 32:48], ACT.Exp).then_inc(madeA, mark(madeA, "dt"))
            sqrt("n1", rstd[:, 0:T])
            act_.wait_ge(madeV, nth(madeV, "angle"))
            a(small[:, 4, :], small[:, 1, :], ACT.Exp)
            a(small[:, 5, :], small[:, 3, :], ACT.Sin, scale=SIN2PI)
            a(small[:, 6, :], small[:, 3, :], ACT.Sin, scale=SIN2PI / 2).then_inc(madeA, mark(madeA, "trig"))
            def mod_out(key, i, bank):
                act_.wait_ge(filled, nth(filled, (key, "rows", i)))
                copy(mod_rows[i], ps[:, bank, :].rearrange("p (a b) -> p a b", a=2)).then_inc(emptied, mark(emptied, (key, i)))

            mod_out("mod1", 0, 2)
            act_.wait_ge(filled, nth(filled, "bbT"))
            for n in range(2):
                last = copy(bbT[:, n, :, :].rearrange("p a b -> p (a b)"), ps[:, 4 + n, :])
            last.then_inc(emptied, mark(emptied, "bbT"))
            act_.wait_ge(filled, nth(filled, "cT"))
            for n in range(2):
                last = copy(cT[:, n, :, :].rearrange("p a b -> p (a b)"), ps[:, n, :])
            last.then_inc(emptied, mark(emptied, "cT"))
            mod_out("mod1", 1, 6)
            mod_out("mod1", 2, 7)

            turn = [0]
            nsin = [0]

            def take(fn):
                g = turn[0]
                act_.wait_ge(filled, nth(filled, ("p1", g)))
                fn(ps[:, g % 4, :]).then_inc(emptied, mark(emptied, ("p1", g)))
                turn[0] += 1

            def sines():
                j = nsin[0]
                if j >= 16:
                    return
                act_.wait_ge(madeV, nth(madeV, ("fr", j)))
                if j >= 2:
                    act_.wait_ge(madeV, nth(madeV, ("s", j - 2)))
                a(tabs[j % 2][:, 1, :], fr[j % 2], ACT.Sin, scale=SIN2PI)
                a(tabs[j % 2][:, 0, :], fr[j % 2], ACT.Sin, scale=SIN2PI / 2)
                act_.drain()
                a(tabs[j % 2][:, 0, :], tabs[j % 2][:, 0, :], ACT.Square).then_inc(madeA, mark(madeA, ("sin", j)))
                nsin[0] += 1

            two = lambda v: v.rearrange("p (a b) -> p a b", a=2)
            for n, c, _ in IN1:
                if n in ("u", "q"):
                    dst = (uT if n == "u" else qT)[:, 2 * c:2 * c + 2, :]
                    take(lambda b: copy(dst, two(b), 0.125 if n == "q" else 1.0))
                    sines()
                elif n in ("kslc", "kwin"):
                    for h in range(2):
                        take(lambda b: copy((kslc if n == "kslc" else kwin)[:, 2 * h:2 * h + 2, :], two(b)))
                        sines()
                elif n in ("kcmp", "vcmp"):
                    kv = kcmp if n == "kcmp" else vcmp

                    def shifted(b, h):
                        copy(kv[0:64, 2 * h:2 * h + 2, :], two(b)[0:64])
                        return copy(kv[64:128, 2 * h:2 * h + 2, 0:T - 1], two(b)[64:128, :, 1:T])
                    for h in range(2):
                        take(lambda b: shifted(b, h))
                        sines()
                else:
                    take(lambda b: copy((vslc if n == "vslc" else vwin)[:, :, :], two(b)))
                    sines()
            take(lambda b: a(gates[:, :, :], b[:, 0:96].rearrange("p (a b) -> p a b", a=2), ACT.Sigmoid))
            for kv in range(2):
                act_.wait_ge(filled, nth(filled, ("hid", kv)))
                copy(cbias[:, 2 * kv:2 * kv + 2], ps[:, kv, 128:130])
                act_.drain()
                for m in range(2):
                    last = a(hid[:, kv, m, :], ps[:, kv, m * 60:(m + 1) * 60], ACT.Gelu_apprx_tanh, bias=cbias[:, 2 * kv + m:2 * kv + m + 1])
            last.then_inc(madeA, mark(madeA, "hid"))
            while nsin[0] < 16:
                sines()
            act_.wait_ge(filled, nth(filled, "kc"))
            copy(kcT, ps[:, 2, 0:60])
            copy(vcN[0:NCMP, :, :].rearrange("p a b -> p (a b)"), ps[0:NCMP, 3, 0:256]).then_inc(madeA, mark(madeA, "kc"))
            act_.wait_ge(madeV, nth(madeV, "yD"))
            a(yT, yT, ACT.Gelu_apprx_tanh).then_inc(madeA, mark(madeA, "ygelu"))
            act_.wait_ge(filled, nth(filled, "z"))
            for m in range(2):
                last = a(yS[:, 2 * m:2 * m + 2, :].rearrange("p a b -> p (a b)"), ps[:, 4 + m, :], ACT.Sigmoid)
            last.then_inc(madeA, mark(madeA, "ysig"))
            act_.wait_ge(madeV, nth(madeV, "yS"))

            def seg(n, u):
                if n == 1:
                    g, tt, x = u
                    return (4, 16 if x == "cmp" else P * (tt + 1))
                return (2, 512)

            def exp(n, i, u):
                act_.wait_ge(madeV, nth(madeV, ("mx", n, i)))
                if i >= 2:
                    act_.wait_ge(filled, nth(filled, ("T", n, i - 2)))
                ns, nk = seg(n, u)
                e_ = (Eb if n == 1 else E2)[i % 2]
                m = NCMP if nk == 16 else nk
                for s in range(ns):
                    bank, at = (2 * (i % 2) + s // 2, (s % 2) * nk) if n == 1 else (2 * (i % 2) + s, 0)
                    last = a(e_[:, s * nk:s * nk + m], ps[:, bank, at:at + m], ACT.Exp,
                             bias=stat[:, i % 2, s:s + 1], accum_out=stat[:, i % 2, 4 + s:5 + s])
                last.then_inc(madeA, mark(madeA, ("exp", n, i)))

            def turned(n, i, u):
                act_.wait_ge(filled, nth(filled, ("T", n, i)))
                ns, nk = seg(n, u)
                pt = (PT if n == 1 else PT2)[i % 2]
                if nk == 16:
                    last = copy(pt[0:NCMP, 0:4 * P], ps[0:NCMP, 4, :])
                else:
                    w = ns * nk
                    last = copy(pt[:, 0:w], ps[:, 4:6, :].rearrange("p a b -> p (a b)")[:, 0:w])
                last.then_inc(madeA, mark(madeA, ("PT", n, i)))

            def outs(n, i, u):
                if n == 1:
                    g, tt, x = u
                    if x != "win":
                        return
                    act_.wait_ge(filled, nth(filled, ("O", n, i)))
                    last = copy(oT[:, 2 * g:2 * g + 2, tt * P:(tt + 1) * P], ps[:, 6, 0:2 * P].rearrange("p (a b) -> p a b", a=2))
                else:
                    x, hp, tt = u
                    act_.wait_ge(filled, nth(filled, ("O", n, i)))
                    last = copy(o2[:, (0 if x == "na" else 4) + hp, tt * P:(tt + 1) * P], ps[:, 6 + i % 2, 0:P])
                last.then_inc(emptied, mark(emptied, ("O", n, i)))

            def attention(n, units):
                exp(n, 0, units[0])
                exp(n, 1, units[1])
                turned(n, 0, units[0])
                for i, u in enumerate(units):
                    if i + 2 < len(units):
                        exp(n, i + 2, units[i + 2])
                    if i + 1 < len(units):
                        turned(n, i + 1, units[i + 1])
                    outs(n, i, u)
                    if n == 1 and i % 8 == 7:
                        mod_out("mod2", i // 8, 7)

            def sigmoids(key, c, prev):
                act_.wait_ge(filled, nth(filled, (key, c)))
                if c >= 1:
                    act_.wait_ge(madeV, nth(madeV, (prev, c - 1)))
                for n in range(2):
                    last = a(sgl[:, n, :, :].rearrange("p a b -> p (a b)"), ps[:, 2 + n, :], ACT.Sigmoid)
                last.then_inc(madeA, mark(madeA, ("sgl", key, c)))

            def moe_front(key, do_square=True):
                if do_square:
                    act_.wait_ge(madeV, nth(madeV, "x" + key))
                    square(key, xT[:, :, :])
                sqrt(key, rstd[:, 0:T])
                act_.wait_ge(filled, nth(filled, "hN" + key))
                for tt in range(TT):
                    for q in range(2):
                        last = copy(hN[:, tt, q * 512:(q + 1) * 512], ps[:, 1 + tt * 2 + q, :])
                last.then_inc(madeA, mark(madeA, "hN" + key))
                act_.wait_ge(madeV, nth(madeV, "shifted" + key))
                last = a(Wt[:, :, 0:E], lg[:, :, 0:E], ACT.Exp)
                if key == "f1":
                    last = a(rt[:, :, 0:4], gx[:, :, 0:4], ACT.Exp)
                last.then_inc(madeA, mark(madeA, "exp" + key))
                act_.wait_ge(madeV, nth(madeV, "ready" + key))

            def moe(n):
                s, x = S[n, "first"], S[n, "more"]
                w = 512 if n == 2 else P

                def block_of(s, q, onehotT, turned_first):
                    act_.wait_ge(s["glu"], q)
                    a(sg[:, 0:w], glu[:, 0:w], ACT.Sigmoid, scale=1.702 if n == 2 else 1.0).then_inc(s["sig"], 1)
                    act_.wait_ge(s["turned"], q)
                    copy(actT.rearrange("p a b -> p (a b)")[:, 0:w], ps[:, 3, 0:w]).then_inc(s["actT"], 1)
                    act_.wait_ge(s["spreadT"], q)
                    copy(onehotT, ps[:, 1, 0:T]).then_inc(s["spread"], 1)

                run_experts(act_, n, lambda it, u, e, q, b: block_of(x, q + 1, ohtM, False),
                            lambda it, u, e: block_of(s, e + 1, ohtF[u % 2], True))

            attention(1, units1)
            for c in range(4):
                sigmoids("gates", c, "mgd")
            moe_front("f1")
            moe(1)
            act_.wait_ge(madeV, nth(madeV, "moe1 out"))
            square("fin", xT[:, :, :])
            sqrt("fin", rstd[:, 0:T])
            act_.wait_ge(madeV, nth(madeV, "x2"))
            square("n2", xT[:, :, :])
            sqrt("n2", rstd[:, 0:T])
            act_.wait_ge(filled, nth(filled, "ctx"))
            for tt in range(TT):
                for q in range(2):
                    last = copy(hT[:, 4 * q:4 * q + 4, T + tt * P:T + (tt + 1) * P], ps[:, 1 + tt * 2 + q, :].rearrange("p (k t) -> p k t", t=P))
            act_.drain()
            a(mgd, hT[:, :, T:2 * T], ACT.Square).then_inc(madeA, mark(madeA, ("sq", "ctx")))
            sqrt("ctx", rstd[:, T:2 * T])
            turn2 = [0]

            def take2(fn):
                g = turn2[0]
                act_.wait_ge(filled, nth(filled, ("p2", g)))
                fn(ps[:, g % 4, :]).then_inc(emptied, mark(emptied, ("p2", g)))
                turn2[0] += 1

            for m in range(4):
                take2(lambda b: copy(kaT[:, m, :], b))
            for c in range(2):
                for h in range(2):
                    take2(lambda b: copy(vN[:, 2 * h:2 * h + 2, c * 256:(c + 1) * 256], two(b)))
            for h in range(2):
                def kv_b(b):
                    copy(kbN[:, 2 * h:2 * h + 2, :], two(b)[:, :, 0:P])
                    return copy(vbN[:, 2 * h:2 * h + 2, :], two(b)[:, :, P:2 * P])
                take2(kv_b)
            for c in range(2):
                take2(lambda b: copy(qaT[:, 2 * c:2 * c + 2, :], two(b), 0.125))
            for c in range(2):
                take2(lambda b: copy(qbN[:, :, c * 256:(c + 1) * 256], two(b)))
            sqrt("heads", rn[:, 0:24])
            act_.wait_ge(filled, nth(filled, "qbT"))
            for n in range(2):
                last = copy(qbT[:, 2 * n:2 * n + 2, :], two(ps[:, 4 + n, :]), 0.125)
            act_.wait_ge(filled, nth(filled, "kbT"))
            copy(kbT[0:64, 0, :], ps[0:64, 6, :])
            copy(kbT[64:128, 1, :], ps[64:128, 6, :])
            copy(kbT[64:128, 0, :], ps[64:128, 7, :])
            copy(kbT[0:64, 1, :], ps[0:64, 7, :]).then_inc(emptied, mark(emptied, "kbT"))
            attention(2, units2)
            for c in range(4):
                sigmoids("gates2", c, "mgd2")
            for c in range(4):
                act_.wait_ge(filled, nth(filled, ("y2", c)))
                copy(o2[:, 2 * c:2 * c + 2, :], two(ps[:, 4 + c, :]))
                last = a(hT[:, 2 * c:2 * c + 2, T:2 * T], two(ps[:, 4 + c, :]), ACT.Square)
            last.then_inc(madeA, mark(madeA, ("sq", "post")))
            sqrt("post", rstd[:, 0:T])
            moe_front("f2")
            moe(2)
            act_.wait_ge(filled, nth(filled, "moe2"))
            for c in range(4):
                copy(o2[:, 2 * c:2 * c + 2, :], two(ps[:, 4 + c, :]))
                last = a(hT[:, 2 * c:2 * c + 2, T:2 * T], two(ps[:, 4 + c, :]), ACT.Square)
            last.then_inc(madeA, mark(madeA, ("sq", "postf")))
            sqrt("postf", rstd[:, 0:T])
            act_.wait_ge(filled, nth(filled, "out"))
            for tt in range(TT):
                for q in range(2):
                    last = copy(hN[:, tt, q * 512:(q + 1) * 512], ps[:, 1 + tt * 2 + q, :])
            last.then_inc(madeA, mark(madeA, "out"))

        @block.vector
        def _(v):
            V = nc.vector
            tt_, ts, stt = V.tensor_tensor, V.tensor_scalar, V.scalar_tensor_tensor

            def B(x, n):
                return x[:, :, None].broadcast_to([P, x.shape[1], n])

            def over(x, n):
                return x[:, None, :].broadcast_to([P, n, x.shape[1]])

            def rms(key, bank, dst, n=D):
                v.wait_ge(filled, nth(filled, ("ss", key)))
                ts(dst, ps[:, bank, 0:T], 1.0 / n, EPS, ALU.mult, ALU.add).then_inc(madeV, mark(madeV, ("var", key)))
                v.wait_ge(madeA, nth(madeA, ("std", key)))
                V.reciprocal(dst, dst)
                v.drain()

            def modulate(dst, src, r, gs, sh, key):
                tt_(dst, src, over(r, KD), ALU.mult)
                v.drain()
                for k in range(KD):
                    last = ts(dst[:, k, :], dst[:, k, :], gs[:, k:k + 1], sh[:, k:k + 1] if sh is not None else None,
                              ALU.mult, ALU.add if sh is not None else None) if sh is not None else \
                        ts(dst[:, k, :], dst[:, k, :], gs[:, k:k + 1], None, ALU.mult)
                last.then_inc(madeV, mark(madeV, key))

            V.memset(cpad2, 0.0)
            v.wait_ge(small_in, SMALL)
            V.tensor_copy(packs[32:48, 2, :].rearrange("p (s c) -> p s c", s=2),
                                     dt2[32:48, :, None].broadcast_to([16, 2, 64])).then_inc(madeV, mark(madeV, "dt rows"))
            v.wait_ge(madeA, nth(madeA, "cols"))
            tt_(csil[:, :], csil[:, :], cols[:, 0, 104:128], ALU.mult)
            V.memset(cpad1, 0.0)
            v.drain()
            V.tensor_copy(cpad2[:, :, 0], csil[:, 8:16])
            V.tensor_copy(cpad2[:, :, 1], csil[:, 16:24])
            V.tensor_copy(cpad1[:, :, 0], csil[:, 0:8]).then_inc(madeV, mark(madeV, "csil"))
            rms("n1", 5, rstd[:, 0:T])
            lr, li = cols[:, 2, 0:16], cols[:, 2, 16:32]
            sm = lambda i: small[:, i, :]
            v.wait_ge(madeA, nth(madeA, "dt"))

            def step(ins):
                v.drain()
            step(tt_(sm(1), lr, sm(0), ALU.mult))
            step(tt_(sm(2), li, sm(0), ALU.mult))
            step(ts(sm(2), sm(2), 1.0 / TWO_PI, None, ALU.mult))
            step(ts(sm(3), sm(2), MAGIC, None, ALU.add))
            step(ts(sm(3), sm(3), -MAGIC, None, ALU.add))
            tt_(sm(3), sm(2), sm(3), ALU.subtract).then_inc(madeV, mark(madeV, "angle"))
            v.wait_ge(madeA, nth(madeA, "trig"))
            step(tt_(sm(7), sm(6), sm(6), ALU.mult))
            step(ts(sm(7), sm(7), -2.0, 1.0, ALU.mult, ALU.add))
            tt_(sm(8), sm(4), sm(7), ALU.mult)
            tt_(sm(9), sm(4), sm(5), ALU.mult)
            tt_(sm(10), lr, lr, ALU.mult)
            step(tt_(sm(11), li, li, ALU.mult))
            tt_(sm(10), sm(10), sm(11), ALU.add)
            step(ts(sm(8), sm(8), -1.0, None, ALU.add))
            V.reciprocal(sm(10), sm(10))
            tt_(sm(12), sm(8), lr, ALU.mult)
            tt_(sm(13), sm(9), li, ALU.mult)
            tt_(sm(14), sm(9), lr, ALU.mult)
            step(tt_(sm(15), sm(8), li, ALU.mult))
            tt_(sm(12), sm(12), sm(13), ALU.add)
            step(tt_(sm(14), sm(14), sm(15), ALU.subtract))
            tt_(sm(12), sm(12), sm(10), ALU.mult)
            step(tt_(sm(13), sm(14), sm(10), ALU.mult))
            b3 = lambda x: x.rearrange("p (j h) -> p j h", h=16)
            v.wait_ge(small_in, SMALL)
            cr_, ci_ = B(sm(12), 16), B(sm(13), 16)
            tmp = b3(sa[:, 0, :])
            tmp2 = b3(sa[:, 1, :])
            tt_(b3(bbuf[:, 0, :]), cr_, b3(bR[:, 0, :]), ALU.mult)
            tt_(tmp, ci_, b3(bR[:, 1, :]), ALU.mult)
            tt_(b3(bbuf[:, 1, :]), cr_, b3(bR[:, 1, :]), ALU.mult)
            step(tt_(tmp2, ci_, b3(bR[:, 0, :]), ALU.mult))
            tt_(b3(bbuf[:, 0, :]), b3(bbuf[:, 0, :]), tmp, ALU.subtract)
            step(tt_(b3(bbuf[:, 1, :]), b3(bbuf[:, 1, :]), tmp2, ALU.add))
            for n in range(2):
                d_ = bd[:, n, :].rearrange("p (j s h) -> p j s h", s=2, h=16)
                for s in range(2):
                    ts(d_[:, :, s, :], b3(bbuf[:, n, :]), cst("half", s, s + 1), None, ALU.mult)
                c3 = cR[:, n, :].rearrange("p (t c) -> p t c", c=P)
                last = stt(c3, c3, 1.0 if n == 0 else -1.0, over(cst("parity"), 4), ALU.mult, ALU.mult)
            last.then_inc(madeV, mark(madeV, "bd"))
            v.wait_ge(filled, nth(filled, "mod1"))
            mod_cols = lambda bank: ps[:, bank:bank + 3, :].rearrange("p a b -> p (a b)").rearrange("p (i c) -> p i c", c=32)
            tt_(mod1[:, :], mod_cols(5)[:, :, 0], cols[:, 0, 0:48], ALU.add)
            v.drain()
            stt(gain[:, 0, :], mod1[:, 8:16], 1.0, cols[:, 0, 48:56], ALU.add, ALU.mult)
            stt(gain[:, 1, :], mod1[:, 32:40], 1.0, cols[:, 0, 56:64], ALU.add, ALU.mult)
            v.drain()
            modulate(hT[:, :, 0:T], xT[:, :, :], rstd[:, 0:T], gain[:, 0, :], mod1[:, 0:8], "h1")

            def fraction(j):
                if j >= 2:
                    v.wait_ge(madeA, nth(madeA, ("sin", j - 2)))
                f, th = fr[j % 2], small[:, 2, j:j + 1]
                step(ts(f, cst("time"), th, MAGIC, ALU.mult, ALU.add))
                step(ts(f, f, -MAGIC, None, ALU.add))
                stt(f, cst("time"), th, f, ALU.mult, ALU.subtract).then_inc(madeV, mark(madeV, ("fr", j)))

            fraction(0)
            fraction(1)
            for j in range(16):
                tb = tabs[j % 2]
                v.wait_ge(madeA, nth(madeA, ("sin", j)))
                step(ts(tb[:, 0, :], tb[:, 0, :], -2.0, 1.0, ALU.mult, ALU.add))
                if j + 2 < 16:
                    fraction(j + 2)
                v.wait_ge(filled, nth(filled, ("bu", j)))
                bu = ps[:, 4 + j % 2, :].rearrange("p (a b) -> p a b", a=2)
                C, S_ = over(tb[:, 0, :], 2), over(tb[:, 1, :], 2)
                tt_(sa, bu, C, ALU.mult)
                tt_(sb_, bu, S_, ALU.mult).then_inc(vemptied, mark(vemptied, ("bu", j)))
                v.drain()
                tt_(sw[:, 0, :], sa[:, 0, :], sb_[:, 1, :], ALU.add)
                step(tt_(sw[:, 1, :], sa[:, 1, :], sb_[:, 0, :], ALU.subtract))
                r = small[:, 4, j:j + 1].broadcast_to([P, T])
                V.tensor_tensor_scan(sz[:, 0, :], r, sw[:, 0, :], 0.0, ALU.mult, ALU.add)
                step(V.tensor_tensor_scan(sz[:, 1, :], r, sw[:, 1, :], 0.0, ALU.mult, ALU.add))
                tt_(sa, sz, C, ALU.mult)
                step(tt_(sb_, sz, S_, ALU.mult))
                if j >= 2:
                    v.wait_ge(filled, nth(filled, ("y", j - 2)))
                tt_(ss2[j % 2][:, 0, :], sa[:, 0, :], sb_[:, 1, :], ALU.subtract)
                tt_(ss2[j % 2][:, 1, :], sa[:, 1, :], sb_[:, 0, :], ALU.add).then_inc(madeV, mark(madeV, ("s", j)))
            v.wait_ge(filled, nth(filled, ("y", 15)))
            for k in range(4):
                last = stt(yT[:, k, :], uT[:, k, :], cols[:, 2, 48 + k:49 + k], ps[:, 6 + k // 2, (k % 2) * T:(k % 2 + 1) * T],
                           ALU.mult, ALU.add)
            last.then_inc(madeV, mark(madeV, "yD"))
            v.wait_ge(madeA, nth(madeA, "ysig"))
            tt_(yS, yS, yT, ALU.mult).then_inc(madeV, mark(madeV, "yS"))

            def seg(n, u):
                if n == 1:
                    g, tt, x = u
                    return (4, 16 if x == "cmp" else P * (tt + 1))
                return (2, 512)

            def view(x, ns, nk):
                w = x[:, 0:ns * nk].rearrange("p (s k) -> p s k", s=ns)
                return w[:, :, 0:NCMP] if nk == 16 else w

            def maxima(n, i, u):
                v.wait_ge(filled, nth(filled, ("S", n, i)))
                ns, nk = seg(n, u)
                sc = ps[:, 2 * (i % 2):2 * (i % 2) + 2, 0:ns * nk // 2].rearrange("p a (s k) -> p a s k", k=nk)
                m = NCMP if nk == 16 else nk
                dst = stat[:, i % 2, 0:ns].rearrange("p (a s) -> p a s", a=2)
                V.tensor_reduce(dst, sc[:, :, :, 0:m], AX.X, ALU.max, negate=True).then_inc(madeV, mark(madeV, ("mx", n, i)))

            def normalise(n, i, u):
                v.wait_ge(madeA, nth(madeA, ("exp", n, i)))
                ns, nk = seg(n, u)
                st = stat[:, i % 2, :]
                c = st[:, 8:8 + ns]
                step(V.reciprocal(c, st[:, 4:4 + ns]))
                if n == 1:
                    g, tt, x = u
                    at = ("cmp", "slc", "win").index(x) * 16 + 4 * g
                    c2 = c.rearrange("p (par half) -> p par half", par=2)
                    step(tt_(c2, c2, gates[:, tt, at:at + 4].rearrange("p (half par) -> p par half", par=2), ALU.mult))
                    if x == "cmp":
                        step(ts(c, c, cst("cmprow", tt, tt + 1), None, ALU.mult))
                e_ = view((Eb if n == 1 else E2)[i % 2], ns, nk)
                m = NCMP if nk == 16 else nk
                tt_(e_, e_, B(c, m), ALU.mult).then_inc(madeV, mark(madeV, ("P", n, i)))

            def bias(tt):
                v.wait_ge(bias_in[tt], 256)
                x = nab2[:, :, :].rearrange("p h (r c) -> p (h r) c", c=64)
                tt_(x, x, over(cst("namask"), 32), ALU.add).then_inc(madeV, mark(madeV, ("bias", tt)))

            def attention(n, units):
                maxima(n, 0, units[0])
                maxima(n, 1, units[1])
                normalise(n, 0, units[0])
                for i, u in enumerate(units):
                    if i + 1 < len(units):
                        normalise(n, i + 1, units[i + 1])
                    if n == 2 and i == 6:
                        bias(1)
                    if i + 2 < len(units):
                        maxima(n, i + 2, units[i + 2])

            v.wait_ge(emptied, nth(emptied, ("p1", 16)))
            attention(1, units1)

            def merge(key, gkey, out_key, tmpb):
                for c in range(4):
                    v.wait_ge(madeA, nth(madeA, ("sgl", gkey, c)))
                    v.wait_ge(filled, nth(filled, (key, c)))
                    for n in range(2):
                        s_ = sgl[:, n, :, :].rearrange("p a b -> p (a b)")
                        tt_(s_, ps[:, n, :], s_, ALU.mult)
                    v.drain()
                    tt_(mgd[:, 2 * c:2 * c + 2, :], sgl[:, 0, :, :], sgl[:, 1, :, :], ALU.add).then_inc(madeV, mark(madeV, (out_key, c)))

            v.wait_ge(filled, nth(filled, "mod2"))
            tt_(mod2[:, :, :], mod_cols(4)[:, :, 0:2], B(cols[:, 1, 0:48], 2), ALU.add)
            merge("branch", "gates", "mgd", None)
            for c in range(4):
                v.wait_ge(filled, nth(filled, ("tm", c)))
                for m in range(2):
                    k = 2 * c + m
                    last = stt(xT[:, k, :], ps[:, 4 + c, m * T:(m + 1) * T], mod1[:, 16 + k:17 + k], xT[:, k, :], ALU.mult, ALU.add)
            last.then_inc(madeV, mark(madeV, "xf1"))

            def top(scores, n, kth, chosen, a1, a2):
                x = a1[:, 0:n * n].rearrange("p (i j) -> p i j", j=n)
                y = a2[:, 0:n * n].rearrange("p (i j) -> p i j", j=n)
                mine, other = B(scores, n), over(scores, n)
                idx = cst("time", 0, n)
                tt_(x, B(idx, n), over(idx, n), ALU.is_gt)
                step(tt_(y, other, mine, ALU.is_equal))
                step(tt_(y, y, x, ALU.mult))
                step(tt_(x, other, mine, ALU.is_gt))
                step(tt_(x, x, y, ALU.add))
                step(V.tensor_reduce(chosen, x, AX.X, ALU.add))
                step(ts(chosen, chosen, kth - 0.5, None, ALU.is_lt))

            def moe_front(key, gs, sh, nr):
                rms(key, 0, rstd[:, 0:T])
                modulate(hT[:, :, 0:T], xT[:, :, :], rstd[:, 0:T], gs, sh, "h" + key)
                v.wait_ge(filled, nth(filled, "logits" + key))
                for tt in range(TT):
                    last = V.tensor_copy(lg[:, tt, 0:nr], ps[:, 5, tt * 64:tt * 64 + nr])
                step(last)
                if key == "f1":
                    step(V.tensor_copy(gx[:, :, 0:4], lg[:, :, 0:4]))
                    step(V.tensor_reduce(rt[:, :, 8], gx[:, :, 0:4], AX.X, ALU.max))
                    for tt in range(TT):
                        top(gx[:, tt, 0:4], 4, 1, gx[:, tt, 4:8], t1, t2)
                    for tt in range(TT):
                        e4 = t1[:, 0:E].rearrange("p (g e) -> p g e", e=8)
                        step(ts(gx[:, tt, 4:8], gx[:, tt, 4:8], -1.0, -NEG, ALU.add, ALU.mult))
                        step(tt_(e4, lg[:, tt, 4:36].rearrange("p (g e) -> p g e", e=8), B(gx[:, tt, 4:8], 8), ALU.add))
                        step(V.tensor_copy(lg[:, tt, 0:E], t1[:, 0:E]))
                        step(ts(gx[:, tt, 0:4], gx[:, tt, 0:4], rt[:, tt, 8:9], None, ALU.subtract))
                for tt in range(TT):
                    top(lg[:, tt, 0:E], E, 2 if key == "f1" else 4, Am[:, tt, :], t1, t2)
                ts(zero, hT[:, 0:2, 0:T], 0.0, None, ALU.mult) if False else V.memset(zero, 0.0).then_inc(madeV, mark(madeV, "chosen" + key))
                step(V.tensor_reduce(rt[:, :, 9], lg[:, :, 0:E], AX.X, ALU.max))
                for tt in range(TT):
                    last = ts(lg[:, tt, 0:E], lg[:, tt, 0:E], rt[:, tt, 9:10], None, ALU.subtract)
                last.then_inc(madeV, mark(madeV, "shifted" + key))
                v.wait_ge(filled, nth(filled, "places" + key))
                cnt = ps[0:1, 5, 256:256 + E]
                c0, c1, c2 = crow[0:1, 0, :], crow[0:1, 1, :], crow[0:1, 2, :]
                step(ts(c0, cnt, SLOTS + 0.5, None, ALU.is_gt))
                for b in range(2, MAXB):
                    step(stt(c0, cnt, SLOTS * b + 0.5, c0, ALU.is_gt, ALU.add))
                step(V.memset(c2, 1.0))
                step(V.tensor_tensor_scan(c1, c2, c0, 0.0, ALU.mult, ALU.add))
                step(tt_(c1, c1, c0, ALU.subtract))
                V.tensor_copy(tabI[0:1, 0, :], c0)
                V.tensor_copy(tabI[0:1, 1, :], c1)
                V.memset(sel[:, :, E:E + 2], 0.0)
                V.memset(Wt[:, :, E:E + 2], 0.0)
                for tt in range(TT):
                    step(stt(sel[:, tt, 0:E], ps[:, 5, 128 + tt * E:128 + (tt + 1) * E], 1.0, Am[:, tt, :], ALU.add, ALU.mult))
                step(ts(sel[:, :, :], sel[:, :, :], -1.0, None, ALU.add))
                v.wait_ge(madeA, nth(madeA, "exp" + key))
                step(tt_(Wt[:, :, 0:E], Wt[:, :, 0:E], Am[:, :, :], ALU.mult))
                step(V.tensor_reduce(rt[:, :, 10], Wt[:, :, 0:E], AX.X, ALU.add))
                if key == "f1":
                    step(V.tensor_reduce(rt[:, :, 11], rt[:, :, 0:4], AX.X, ALU.add))
                    step(tt_(rt[:, :, 10], rt[:, :, 10], rt[:, :, 11], ALU.mult))
                step(V.reciprocal(rt[:, :, 10], rt[:, :, 10]))
                for tt in range(TT):
                    last = ts(Wt[:, tt, 0:E], Wt[:, tt, 0:E], rt[:, tt, 10:11], None, ALU.mult)
                step(last)
                if key == "f2":
                    V.memset(biasB, 0.0).then_inc(madeV, mark(madeV, "biasB"))
                V.memset(t1, 0.0).then_inc(madeV, mark(madeV, "ready" + key))
                V.memset(t2, 0.0).then_inc(madeV, mark(madeV, "tables" + key))

            def moe(n):
                s, x = S[n, "first"], S[n, "more"]
                w = 512 if n == 2 else P

                def gather_onehot(s, dst, e, slots):
                    for tt in range(TT):
                        last = ts(dst[:, tt, :], slots, sel[:, tt, bass.ds(e, 1)], None, ALU.is_equal)
                    last.then_inc(s["gather_onehot"], 1)

                def spread_onehot(s, dst, e, slots):
                    for tt in range(TT):
                        for half in range(2):
                            last = ts(dst[:, tt, half * SLOTS:(half + 1) * SLOTS], slots, sel[:, tt, bass.ds(e, 1)],
                                      Wt[:, tt, bass.ds(e, 1)], ALU.is_equal, ALU.mult)
                    last.then_inc(s["spread_onehot"], 1)

                def xs_out(s, dst):
                    V.tensor_copy(dst.rearrange("p a b -> p (a b)"), ps[:, 0, :]).then_inc(s["xs"], 1)

                def select(dst, e):
                    V.tensor_copy(dst, cst("ident")[:, bass.ds(e, 1)].broadcast_to([P, SLOTS]))

                def units(s, q):
                    v.wait_ge(s["hidden"], q)
                    if n == 1:
                        V.tensor_copy(glu[:, 0:w], ps[:, 1, 0:w]).then_inc(s["glu"], 1)
                        v.drain()
                        tt_(lin[:, 0:w], ps[:, 2, 0:w], glu[:, 0:w], ALU.mult)
                    else:
                        ts(glu, ps[:, 1, :], 7.0, None, ALU.min).then_inc(s["glu"], 1)
                        ts(lin, ps[:, 2, :], 7.0, -7.0, ALU.min, ALU.max)
                        v.drain()
                        stt(lin, lin, 1.0, glu, ALU.add, ALU.mult)
                    v.drain()
                    v.wait_ge(s["sig"], q)
                    tt_(act[:, 0:w], lin[:, 0:w], sg[:, 0:w], ALU.mult).then_inc(s["act"], 1)

                slots0 = cst("time", 0, SLOTS)

                def further(it, u, e, q, b):
                    slots = cst("time")[:, bass.ds(b * SLOTS, SLOTS)]
                    gather_onehot(x, ohgM, e, slots)
                    spread_onehot(x, ohsM, e, slots)
                    v.wait_ge(x["gathered"], q + 1)
                    xs_out(x, xsM)
                    units(x, q + 1)
                    v.wait_ge(x["down"], q + 1)
                    V.tensor_copy(ysM, ps[:, 3, :]).then_inc(x["ys"], 1)

                def first(it, u, e):
                    units(s, e + 1)
                    if n == 2:
                        select(esel[(u + 1) % 2], e + 1)
                    v.wait_ge(s["gathered"], e + 2)
                    xs_out(s, xsF)
                    gather_onehot(s, ohgF, e + 2, slots0)
                    v.wait_ge(s["spreadT"], e + 1)
                    spread_onehot(s, ohsF, e + 1, slots0)
                    v.wait_ge(s["down"], e + 1)
                    V.tensor_copy(ysF, ps[:, 3, :]).then_inc(s["ys"], 1)

                V.memset(ysF, 0.0).then_inc(s["ys"], 1)
                V.memset(ohtF[1], 0.0).then_inc(s["spread"], 1)
                if n == 2:
                    select(esel[0], 0)
                gather_onehot(s, ohgF, 0, slots0)
                spread_onehot(s, ohsF, 0, slots0)
                v.wait_ge(s["gathered"], 1)
                xs_out(s, xsF)
                gather_onehot(s, ohgF, 1, slots0)
                run_experts(v, n, further, first)

            moe_front("f1", gain[:, 1, :], mod1[:, 24:32], 36)
            moe(1)
            v.wait_ge(filled, nth(filled, "moe1"))
            for k in range(KD):
                last = stt(xT[:, k, :], ps[:, 4 + k // 2, (k % 2) * T:(k % 2 + 1) * T], mod1[:, 40 + k:41 + k], xT[:, k, :], ALU.mult, ALU.add)
            last.then_inc(madeV, mark(madeV, "moe1 out"))
            rms("fin", 0, rstd[:, 0:T])
            modulate(xT[:, :, :], xT[:, :, :], rstd[:, 0:T], cols[:, 0, 64:72], None, "x2")
            stt(gain[:, 2, :], mod2[:, 8:16, 0], 1.0, cols[:, 1, 48:56], ALU.add, ALU.mult)
            stt(gain[:, 3, :], mod2[:, 8:16, 1], 1.0, cols[:, 1, 48:56], ALU.add, ALU.mult)
            tt_(gain[:, 4, :], mod2[:, 16:24, 0], cols[:, 1, 56:64], ALU.mult)
            stt(gain[:, 5, :], mod2[:, 32:40, 0], 1.0, cols[:, 1, 64:72], ALU.add, ALU.mult)
            tt_(gain[:, 0, :], mod2[:, 40:48, 0], cols[:, 1, 72:80], ALU.mult)
            v.drain()
            rms("n2", 0, rstd[:, 0:T])
            modulate(hT[:, :, 0:T], xT[:, :, :], rstd[:, 0:T], gain[:, 2, :], mod2[:, 0:8, 0], "h2")
            rms("ctx", 5, rstd[:, T:2 * T])
            modulate(hT[:, :, T:2 * T], hT[:, :, T:2 * T], rstd[:, T:2 * T], gain[:, 3, :], mod2[:, 0:8, 1], "hctx")
            v.wait_ge(emptied, nth(emptied, ("p2", 13)))
            q3 = lambda x: x.rearrange("p t (h d) -> p (t h) d", d=HD)
            tt_(q3(qt1), q3(qbN), q3(qbN), ALU.mult)
            step(tt_(q3(kt1), q3(kbN), q3(kbN), ALU.mult))
            V.tensor_reduce(rn[:, 0:16], q3(qt1), AX.X, ALU.add)
            step(V.tensor_reduce(rn[:, 16:24], q3(kt1), AX.X, ALU.add))
            ts(rn[:, 0:24], rn[:, 0:24], 1.0 / HD, EPS, ALU.mult, ALU.add).then_inc(madeV, mark(madeV, ("var", "heads")))
            bias(0)
            v.wait_ge(madeA, nth(madeA, ("std", "heads")))
            step(V.reciprocal(rn[:, 0:24], rn[:, 0:24]))
            tt_(q3(qbN), q3(qbN), B(rn[:, 0:16], HD), ALU.mult)
            step(tt_(q3(kbN), q3(kbN), B(rn[:, 16:24], HD), ALU.mult))
            tt_(q3(qbN), q3(qbN), over(gqk[:, 0, :], 16), ALU.mult)
            step(tt_(q3(kbN), q3(kbN), over(gqk[:, 1, :], 8), ALU.mult))
            for x, x1, x2, nh in ((qbN, qt1, qt2, 8), (kbN, kt1, qt2, 2)):
                for tt in range(TT):
                    h3 = lambda y: y[:, tt, 0:nh * HD].rearrange("p (h d) -> p h d", d=HD)
                    h5 = lambda y: y[:, tt, 0:nh * HD].rearrange("p (h a b c) -> p h a b c", a=2, b=2, c=16)
                    tt_(h3(x1), h3(x), over(cst("ropecos", tt * HD, (tt + 1) * HD), nh), ALU.mult)
                    sn = cst("ropesin", tt * HD, (tt + 1) * HD).rearrange("p (a b c) -> p a b c", a=2, b=2)
                    for b in range(2):
                        tt_(h5(x2)[:, :, :, b, :], h5(x)[:, :, :, 1 - b, :],
                            sn[:, None, :, b, :].broadcast_to([P, nh, 2, 16]), ALU.mult)
                    v.drain()
                    step(tt_(h3(x), h3(x1), h3(x2), ALU.add))
            V.tensor_copy(kt1[:, :, 0:HD], kbN[:, :, HD:2 * HD])
            V.tensor_copy(kt1[:, :, HD:2 * HD], kbN[:, :, 0:HD]).then_inc(madeV, mark(madeV, "rope"))
            attention(2, units2)
            merge("branch2", "gates2", "mgd2", None)

            def residual(key, g_, out_key):
                rms(key, 0, rstd[:, 0:T])
                step(tt_(o2[:, :, :], o2[:, :, :], over(rstd[:, 0:T], KD), ALU.mult))
                for k in range(KD):
                    last = stt(xT[:, k, :], o2[:, k, :], g_[:, k:k + 1], xT[:, k, :], ALU.mult, ALU.add)
                last.then_inc(madeV, mark(madeV, out_key))

            residual("post", gain[:, 4, :], "xf2")
            moe_front("f2", gain[:, 5, :], mod2[:, 24:32, 0], 32)
            moe(2)
            residual("postf", gain[:, 0, :], "xout")
    return counts.values


_SQUEEZE = ["ada_w", "ada_b", "norm1_g", "w_in", "ssm_lam_re", "ssm_lam_im", "ssm_log_dt", "ssm_b_re", "ssm_b_im",
            "ssm_c_re", "ssm_c_im", "ssm_d", "ssm_w_glu", "ssm_w_o", "nsa_cmp_pos", "nsa_cmp_w1", "nsa_cmp_w2",
            "nsa_w_o", "w_out", "norm2_g", "moe_w_group", "moe_b_group", "moe_w_expert", "moe_b_expert",
            "moe_w_gate", "moe_w_up", "moe_w_down", "w_mod_2", "b_mod_2", "g_pre_mix_2", "g_post_mix_2",
            "g_pre_ffn_2", "g_post_ffn_2", "w_in_2", "rpb_2", "g_qnorm_2", "g_knorm_2", "w_out_a_2", "w_out_b_2",
            "w_o_2", "w_router_2", "b_router_2", "w_gu_2", "b_gu_2", "w_dn_2", "b_dn_2"]
_SMALLER = ["x", "ctx_2"]
_PLAIN = ["c", "final_g", "c_2", "c_ctx_2"]


def kernel(**inputs):
    import concourse.bacc as _bacc
    from concourse.bass_utils import run_bass_kernel_spmd as _run

    arrays, shapes = {}, {}
    for name in _SQUEEZE + _SMALLER + _PLAIN:
        a = np.ascontiguousarray(inputs[name])
        if name not in _PLAIN:
            a = a.reshape(a.shape[1:])
        arrays[f"in_{name}_dram"] = a
        shapes[name] = a.shape
    arrays["constants_dram"] = CONST_ARRAY
    known = None
    for _ in range(2):
        nc = _bacc.Bacc("TRN2", target_bir_lowering=False, num_devices=1)
        A = {name: nc.dram_tensor(f"in_{name}_dram", shape, F32, kind="ExternalInput").ap()
             for name, shape in shapes.items()}
        const = nc.dram_tensor("constants_dram", CONST_ARRAY.shape, F32, kind="ExternalInput").ap()
        out = nc.dram_tensor("out_0_dram", (T, D), F32, kind="ExternalOutput").ap()
        known = program(nc, A, const, out, known)
    r = _run(nc, [arrays], core_ids=[0])
    return r.results[0]["out_0_dram"].reshape(1, T, D)
```

```python
from contextlib import ExitStack

import numpy as np
import concourse.bass as bass
from concourse import mybir

F32 = mybir.dt.float32
I32 = mybir.dt.int32
ALU = mybir.AluOpType
ACT = mybir.ActivationFunctionType
AX = mybir.AxisListType

P = 128
T = 256
D = 1024
KD = D // P
TT = T // P
HD = 64
NCMP = 15
EPS = 1e-6
NEG = -1e30
E = 32
SLOTS = 64
MAXB = T // SLOTS
RING = 12
SLOT = 2048
TWO_PI = 2 * np.pi
SIN2PI = 6.283185
MAGIC = 1.5 * 2.0 ** 23

CONST = {}


def constants():
    p = np.arange(P)
    parts = {}
    parts["ident"] = np.eye(P)
    parts["ones"] = np.ones((P, P))
    parts["causal"] = np.where(p[None, :] > p[:, None], NEG, 0.0)
    t = (np.arange(TT)[None, :] * P + p[:, None])
    end = np.arange(NCMP) * 16 + 31
    parts["cmpmask"] = np.where(end[None, None, :] <= t[:, :, None], 0.0, NEG).reshape(P, -1)
    parts["cmprow"] = (t >= 31).astype(np.float64)
    parts["before"] = (p[:, None] < p[None, :]).astype(np.float64)
    mirror = np.zeros((P, P))
    mirror[p, (p // 64) * 64 + 63 - p % 64] = 1.0
    parts["mirror"] = mirror
    parts["time"] = np.broadcast_to(np.arange(T)[None, :], (P, T))
    col = 63 - p % 64
    c0 = np.clip(col - 8, 0, 48)
    kc = np.arange(64)
    parts["namask"] = np.where((kc[None, :] >= c0[:, None]) & (kc[None, :] < c0[:, None] + 16), 0.0, NEG)
    nf = 16
    freqs = 10000.0 ** (-np.arange(nf) / nf)
    row, cl = t // 64, t % 64
    angr, angc = row[:, :, None] * freqs, cl[:, :, None] * freqs
    parts["ropecos"] = np.concatenate([np.cos(angr), np.cos(angr), np.cos(angc), np.cos(angc)], -1).reshape(P, -1)
    parts["ropesin"] = np.concatenate([-np.sin(angr), np.sin(angr), -np.sin(angc), np.sin(angc)], -1).reshape(P, -1)
    parts["parity"] = ((p[:, None] // 16) % 2 == (p[None, :] // 64)).astype(np.float64)
    parts["half"] = (p[:, None] // 64 == np.arange(2)[None, :]).astype(np.float64)
    at, cols = 0, []
    for name, a in parts.items():
        CONST[name] = (at, a.shape[1])
        at += a.shape[1]
        cols.append(a)
    return np.ascontiguousarray(np.concatenate(cols, 1).astype(np.float32))


CONST_ARRAY = constants()
NCONST = CONST_ARRAY.shape[1]


class Counts:

    def __init__(self, known):
        self.known, self.names, self.values, self.n = known, {}, {}, {}

    def mark(self, sem, key):
        name = self.names[id(sem)]
        assert (name, key) not in self.values, (name, key)
        self.n[name] = self.values[name, key] = self.n.get(name, 0) + 1
        return 1

    def nth(self, sem, key):
        return 1 if self.known is None else self.known[self.names[id(sem)], key]


def program(nc, A, const, out, known):
    counts = Counts(known)
    mark, nth = counts.mark, counts.nth
    with ExitStack() as ctx:
        def sb(name, shape, dt=F32):
            return ctx.enter_context(nc.sbuf_tensor(name, shape, dt))

        def sem(name):
            return ctx.enter_context(nc.semaphore(name))

        def signal(name):
            s = sem(name)
            counts.names[id(s)] = name
            return s

        K = sb("consts", [P, NCONST])

        def cst(name, a=None, b=None):
            at, n = CONST[name]
            return K[:, at + (a or 0):at + (n if b is None else b)]

        ring = sb("ring", [P, RING, SLOT])
        xT = sb("xT", [P, KD, T])
        hT = sb("hT", [P, KD, 2 * T])
        hN = sb("hN", [P, TT, D])
        packs = sb("packs", [P, 3, P])
        cols = sb("cols", [P, 3, P])
        csil = sb("csil", [P, 24])
        mod1 = sb("mod1", [P, 48])
        mod2 = sb("mod2", [P, 48, 2])
        gain = sb("gain", [P, 6, KD])
        wr1 = sb("wr1", [P, KD, 36])
        wr2 = sb("wr2", [P, KD, 32])
        rb = sb("rb", [1, 68])
        w2c = sb("w2c", [P, 2, 2, HD])
        gqk = sb("gqk", [P, 2, HD])
        rstd = sb("rstd", [P, 2 * T])
        ARENA = 16100
        arena = sb("arena", [P, ARENA])
        ps = ctx.enter_context(nc.psum_tensor("ps", [P, 8, 512], F32))

        def carve(at, *shape):
            n = int(np.prod(shape))
            assert at + n <= ARENA, (at, n)
            v = arena[:, at:at + n]
            if len(shape) == 2:
                v = v.rearrange("p (a b) -> p a b", b=shape[1])
            if len(shape) == 3:
                v = v.rearrange("p (a b c) -> p a b c", b=shape[1], c=shape[2])
            return v

        class Lay:
            def __init__(self, at=0):
                self.at = at

            def __call__(self, *shape):
                v = carve(self.at, *shape)
                self.at += int(np.prod(shape))
                return v

        L = Lay()
        qT = L(KD, T)
        kslc = L(4, T)
        kwin = L(4, T)
        vslc = L(TT, 256)
        vwin = L(TT, 256)
        gates = L(TT, 48)
        uT = L(4, T)
        kcT = L(60)
        vcN = L(4, HD)
        s_at = L.at
        kcmp = hN[:, 0, :].rearrange("p (g t) -> p g t", t=T)
        vcmp = hN[:, 1, :].rearrange("p (g t) -> p g t", t=T)
        bbT = L(2, 4, P)
        cT = L(2, 4, P)
        yT = L(4, T)
        fr = [L(T), L(T)]
        tabs = [L(2, T), L(2, T)]
        sa = L(2, T)
        sb_ = L(2, T)
        sw = L(2, T)
        sz = L(2, T)
        ss2 = [L(2, T), L(2, T)]
        hid = L(TT, P)
        small = L(24, 16)
        assert L.at <= ARENA, L.at
        cpad1 = hN[:, 0, 0:KD * 32].rearrange("p (k c) -> p k c", c=32)
        cpad2 = L(KD, 32)
        hidR = L(256)
        blocks = [[hT[:, 4 * kv + c // 4, T + (c % 4) * 64:T + (c % 4 + 1) * 64] for c in range(16)] for kv in range(2)]
        mod_rows = [hT[:, 2 * i:2 * i + 2, T:2 * T] for i in range(3)]
        bd = carve(0, 2, 4 * P)
        cR = carve(1024, 2, 4 * P)
        bR = carve(2048, 2, 256)
        bbuf = carve(2560, 2, 256)
        LA = Lay(s_at)
        Eb = [LA(1024), LA(1024)]
        PT = [LA(1024), LA(1024)]
        sgl = LA(2, 2, T)
        mgd = hN[:, :, :].rearrange("p a b -> p (a b)").rearrange("p (k t) -> p k t", t=T)
        yS = LA(4, T)
        oT = LA(KD, T)
        stat = sb("stat", [P, 2, 16])
        rn = sb("rn", [P, 24])
        dt2 = sb("dt2", [P, 2])
        L2 = Lay()
        kaT = L2(4, 2 * T)
        qaT = L2(4, T)
        qbT = L2(4, T)
        kbT = L2(2, 2 * T)
        vN = L2(4, 512)
        vbN = L2(4, P)
        o2 = L2(KD, T)
        at2 = L2.at
        E2 = [L2(1024), L2(1024)]
        PT2 = [L2(1024), L2(1024)]
        nab2 = L2(8, T)
        L3 = Lay(at2)
        qbN = L3(TT, 512)
        qt1 = L3(TT, 512)
        qt2 = L3(TT, 512)
        kbN = L3(4, P)
        kt1 = L3(4, P)
        M = Lay()
        biasB = M(3072)
        xsP, xsM = M(KD, P), M(KD, SLOTS)
        xsF = xsP.rearrange("p a b -> p (a b)")[:, 0:KD * SLOTS].rearrange("p (k s) -> p k s", s=SLOTS)
        ohgF, ohgM = M(TT, P), M(TT, P)
        ohsF, ohsM = M(TT, P), M(TT, P)
        ohtF, ohtM = [M(T), M(T)], M(T)
        ysF, ysM = M(512), M(512)
        xsM1 = biasB[:, 0:1024].rearrange("p (k s) -> p k s", s=P)
        ysF1, ysM1 = biasB[:, 1024:2048], biasB[:, 2048:3072]
        glu = M(512)
        lin = M(512)
        sg = M(512)
        act = M(512)
        actT = M(4, P)
        esel = [M(SLOTS), M(SLOTS)]
        zero = M(512)
        lg = M(TT, 36)
        Am = M(TT, E)
        Wt = M(TT, E + 4)
        sel = M(TT, E + 4)
        t1 = M(E * E)
        t2 = M(E * E)
        gx = M(TT, 8)
        m8 = M(TT, 8)
        rt = M(TT, 16)
        crow = M(4, E)
        tabI = sb("tabI", [1, 2, E], I32)

        def wcols(name, a, b):
            w = A[name][:, a:b].rearrange("(k p) c -> p k c", p=P)
            return w

        chunks = []

        def chunk(key, src, *shape):
            chunks.append((key, src, shape))

        for c in range(24):
            chunk(("mod1", c), wcols("ada_w", c * 256, c * 256 + 256), KD, 256)
        IN1 = [("u", 0, 2608), ("u", 1, 2864)] + [("q", c, c * 256) for c in range(4)] + \
              [("kcmp", 0, 1024), ("vcmp", 0, 1280), ("kslc", 0, 1536), ("kwin", 0, 2048),
               ("vslc", 0, 1792), ("vwin", 0, 2304)]
        for n, c, at in IN1:
            chunk((n, c), wcols("w_in", at, at + 256), KD, 256)
        chunk(("ng", 0), wcols("w_in", 2560, 2608), KD, 48)
        for kv in range(2):
            w = A["nsa_cmp_w1"][kv].rearrange("(c p) h -> p c h", p=P)
            for c in range(2):
                chunk(("cw1", kv, c), w[:, 8 * c:8 * c + 8, :], 8, 256)
        for c in range(24):
            chunk(("mod2", c), wcols("w_mod_2", c * 256, c * 256 + 256), KD, 256)
        chunk(("glu", 0), A["ssm_w_glu"].rearrange("(k p) c -> p k c", p=P), 4, 512)
        for c in range(4):
            chunk(("mga", c), wcols("w_in", 3120 + c * 256, 3376 + c * 256), KD, 256)
            chunk(("mgs", c), wcols("w_in", 4144 + c * 256, 4400 + c * 256), KD, 256)
            chunk(("no", c), wcols("nsa_w_o", c * 256, c * 256 + 256), KD, 256)
            if c % 2 == 0:
                chunk(("so", c // 2), A["ssm_w_o"][:, c * 256:c * 256 + 512].rearrange("(k p) c -> p k c", p=P), 4, 512)
        for c in range(4):
            chunk(("wo", c), wcols("w_out", c * 256, c * 256 + 256), KD, 256)
        n_front1 = len(chunks)
        moe1_at = n_front1
        front2_at = moe1_at + 3 * E
        n1 = len(chunks)
        IN2 = [("kvb", 0, 1024), ("qb", 0, 1792), ("qb", 1, 2048), ("ka", 0, 0), ("ka", 1, 256),
               ("va", 0, 512), ("va", 1, 768), ("qa", 0, 1280), ("qa", 1, 1536)]
        for n, c, at in IN2:
            chunk((n + "2", c), wcols("w_in_2", at, at + 256), KD, 256)
        for c in range(4):
            chunk(("ga2", c), wcols("w_in_2", 2304 + c * 256, 2560 + c * 256), KD, 256)
            chunk(("gb2", c), wcols("w_in_2", 3328 + c * 256, 3584 + c * 256), KD, 256)
            if c % 2 == 0:
                for x in "ab":
                    chunk(("oo" + x, c // 2), A["w_out_" + x + "_2"][:, c * 256:c * 256 + 512].rearrange("(k p) c -> p k c", p=P), 4, 512)
        for c in range(4):
            chunk(("w_o2", c), wcols("w_o_2", c * 256, c * 256 + 256), KD, 256)
        moe2_at = front2_at + len(chunks) - n1
        index = {}
        for i, (key, _, _) in enumerate(chunks):
            index[key] = i if i < n1 else front2_at + i - n1

        full = [sem(f"ring_full{s}") for s in range(RING)]
        freed = sem("ring_freed")

        def slot_ap(i, shape):
            v = ring[:, i % RING, 0:int(np.prod(shape))]
            return v.rearrange("p (a b) -> p a b", b=shape[1])

        def weights(eng, key):
            i = index[key]
            eng.wait_ge(full[i % RING], 16 * (i // RING + 1))
            return slot_ap(i, chunks[i if i < n1 else i - front2_at + n1][2])

        def load(sp, key, i, src, shape):
            if i >= RING:
                sp.wait_ge(freed, i - RING + 1)
            sp.dma_start(slot_ap(i, shape), src).then_inc(full[i % RING], 16)

        small_in = sem("vectors_in")
        tables_in = sem("tables_in")
        ctx_in = sem("ctx_in")
        bias_in = [sem("bias_in0"), sem("bias_in1")]
        biasb_in = sem("expert_biases_in")
        xin = sem("x_in")
        filled = signal("psum_filled")
        emptied = signal("psum_emptied")
        vemptied = signal("psum_emptied_by_vector")
        madeV = signal("made_by_vector")
        madeA = signal("made_by_scalar")
        blocks_made = sem("blocks_made")
        out_sem = sem("out_stored")
        STEPS = ("gather_onehot", "gathered", "xs", "spread_onehot", "spreadT", "spread", "hidden", "glu", "sig",
                 "act", "turned", "actT", "down", "ys", "scattered")
        S = {(n, kind): {x: sem(f"moe{n}_{kind}_{x}") for x in STEPS} for n in (1, 2) for kind in ("first", "more")}
        used2 = sem("moe2_rows_used")

        def run_experts(eng, n, further, first, begin=lambda *_: None):
            with eng.Fori(0, E // 4 if n == 1 else E // 2) as it:
                for u in range(2):
                    g = it * 2 + u
                    more = eng.value_load(tabI[0:1, 0, bass.ds(g, 1)], min_val=0, max_val=MAXB - 1)
                    before = eng.value_load(tabI[0:1, 1, bass.ds(g, 1)], min_val=0, max_val=E * (MAXB - 1))
                    begin(it, u, g)
                    with eng.If(more > 0):
                        with eng.Fori(0, more) as b:
                            further(it, u, g, before + b, b + 1)
                    first(it, u, g)

        block = ctx.enter_context(nc.Block())
        pending = [0]

        def mm(*a, start, stop, **k):
            ins = nc.tensor.matmul(*a, start=start, stop=stop, **k)
            if pending[0] and start and not stop:
                ins.then_inc(freed, pending[0])
                pending[0] = 0
            return ins


        smalls = []

        def rows(pk, at, src, n):
            smalls.append((packs[at:at + n, pk, :], src.rearrange("(r c) -> r c", c=P)))

        rows(0, 0, A["ada_b"], 48)
        rows(0, 48, A["norm1_g"], 8)
        rows(0, 56, A["norm2_g"], 8)
        rows(0, 64, A["final_g"], 8)
        rows(0, 72, A["nsa_cmp_pos"].rearrange("a l h -> (a l h)"), 32)
        rows(0, 104, A["c"].rearrange("a d -> (a d)"), 8)
        rows(0, 112, A["c_2"].rearrange("a d -> (a d)"), 8)
        rows(0, 120, A["c_ctx_2"], 8)
        rows(1, 0, A["b_mod_2"], 48)
        for n, k in enumerate(("g_pre_mix_2", "g_post_mix_2", "g_pre_ffn_2", "g_post_ffn_2")):
            rows(1, 48 + 8 * n, A[k], 8)
        rows(2, 0, A["ssm_lam_re"].rearrange("g p -> (g p)"), 16)
        rows(2, 16, A["ssm_lam_im"].rearrange("g p -> (g p)"), 16)
        ldt = A["ssm_log_dt"].rearrange("(j s) -> j s", s=2)
        smalls.append((dt2[32:48, :], ldt))
        rows(2, 48, A["ssm_d"].rearrange("g h -> (g h)"), 4)
        smalls.append((packs[80:128, 1, :], A["ada_b"].rearrange("(r c) -> r c", c=P)))
        smalls.append((packs[52:128, 2, :], const[0:76, 0:P]))
        SMALL = 16 * len(smalls)
        vectors, smalls = smalls, []
        for n, k in enumerate(("ssm_b_re", "ssm_b_im")):
            smalls.append((bR[:, n, :].rearrange("p (j h) -> p j h", h=16),
                           A[k].rearrange("g p h -> (g p) h").rearrange("(j q) h -> q j h", q=P)))
        for n, k in enumerate(("ssm_c_re", "ssm_c_im")):
            src = A[k].rearrange("g h p -> (g h) p").rearrange("(t q) p -> q t p", q=P)
            dst = cR[:, n, :].rearrange("p (t s c) -> p t s c", t=4, s=2)
            smalls += [(dst[:, :, 0, :], src), (dst[:, :, 1, :], src)]
        smalls.append((wr1[:, :, 0:4], A["moe_w_group"].rearrange("(k p) c -> p k c", p=P)))
        smalls.append((wr1[:, :, 4:36], A["moe_w_expert"].rearrange("(k p) c -> p k c", p=P)))
        smalls.append((wr2[:, :, :], A["w_router_2"].rearrange("(k p) c -> p k c", p=P)))
        smalls.append((rb[:, 0:4], A["moe_b_group"].rearrange("(a c) -> a c", a=1)))
        smalls.append((rb[:, 4:36], A["moe_b_expert"].rearrange("(a c) -> a c", a=1)))
        smalls.append((rb[:, 36:68], A["b_router_2"].rearrange("(a c) -> a c", a=1)))
        for kv in range(2):
            smalls.append((w2c[:, kv, :, :], A["nsa_cmp_w2"][kv].rearrange("(k p) c -> p k c", p=P)))
        for n, k in enumerate(("g_qnorm_2", "g_knorm_2")):
            smalls.append((gqk[:, n, :], A[k][None, :].broadcast_to([P, HD])))
        TABLES = 16 * len(smalls)

        @block.sync
        def _(sp):
            sp.dma_start(K[:, :], const[:, :]).then_inc(xin, 16)
            sp.dma_start(hN[:, :, :], A["x"].rearrange("(a p) d -> p a d", p=P)).then_inc(xin, 16)
            sp.wait_ge(small_in, SMALL)
            for i in range(n1):
                key, src, shape = chunks[i]
                load(sp, key, i, src, shape)
            def load_moe1(it, u, wait):
                for j in range(6):
                    i = moe1_at + 6 * u + j
                    wait(i, j)
                    e = it * 4 + u * 2 + j % 2
                    src = A["moe_w_" + ("gate", "up", "down")[j // 2]][bass.ds(e, 1)].rearrange("e (k p) c -> p (e k) c", p=P)
                    sp.dma_start(slot_ap(i, (KD, 256) if j < 4 else (2, D)), src).then_inc(full[i % RING], 16)

            s1, s2 = S[1, "first"], S[2, "first"]
            for u in range(2):
                load_moe1(0, u, lambda i, j: sp.wait_ge(freed, i - RING + 1))
            with sp.Fori(1, E // 4) as it:
                for u in range(2):
                    load_moe1(it, u, lambda i, j: sp.wait_ge(s1["hidden" if j < 4 else "down"], it * 2 + u - 1))
            for i in range(n1, len(chunks)):
                key, src, shape = chunks[i]
                at = index[key]
                if at - RING < front2_at:
                    pair, j = divmod(at - RING - moe1_at, 6)
                    sp.wait_ge(s1["hidden" if j < 4 else "down"], pair + 1)
                else:
                    sp.wait_ge(freed, n1 + at - RING - front2_at + 1)
                sp.dma_start(slot_ap(at, shape), src).then_inc(full[at % RING], 16)

            def load_moe2(e, wait):
                for j in range(12):
                    i = moe2_at + j
                    wait(i, j)
                    if j < 8:
                        src = A["w_gu_2"][bass.ds(e, 1), j * P:(j + 1) * P, :].rearrange("e p c -> p (e c)")
                        sp.dma_start(ring[:, i % RING, :], src).then_inc(full[i % RING], 16)
                    else:
                        src = A["w_dn_2"][bass.ds(e, 1), (j - 8) * 256:(j - 7) * 256, :].rearrange("e (k p) c -> p (e k) c", p=P)
                        sp.dma_start(slot_ap(i, (2, D)), src).then_inc(full[i % RING], 16)

            def free2(e, j):
                if j == 7:
                    sp.wait_ge(s2["hidden"], e)
                elif j == 11:
                    sp.wait_ge(s2["down"], e)
                else:
                    sp.wait_ge(used2, 10 * e - 10 + (j + 1 if j < 7 else j))

            load_moe2(0, lambda i, j: sp.wait_ge(freed, n1 + i - RING - front2_at + 1))
            with sp.Fori(1, E) as e:
                load_moe2(e, lambda i, j: free2(e, j))
            sp.wait_ge(madeA, nth(madeA, "out"))
            for a in range(TT):
                sp.dma_start(out.rearrange("(a p) d -> p a d", p=P)[:, a, :], hN[:, a, :]).then_inc(out_sem, 16)
            sp.wait_ge(out_sem, 16 * TT)

        @block.gpsimd
        def _(g):
            for dst, src in smalls:
                g.dma_start(dst, src).then_inc(tables_in, 16)
            g.wait_ge(madeA, nth(madeA, "cols"))
            for kv in range(2):
                g.wait_ge(emptied, nth(emptied, ("p1", 6 + kv)))
                for c in range(16):
                    b = blocks[kv][c]
                    src = (kcmp, vcmp)[kv][:, :, 2 * c:2 * c + 16 * 14 + 1:16]
                    nc.gpsimd.memset(b[:, 60:64], 0.0)
                    last = nc.gpsimd.tensor_scalar(b[:, 0:60].rearrange("p (g n) -> p g n", n=NCMP), src,
                                                   cols[:, 0, 72 + 16 * kv + c:73 + 16 * kv + c], None, ALU.add)
                last.then_inc(blocks_made, 1)
            g.wait_ge(madeV, nth(madeV, "moe1 out"))
            g.dma_start(hN[:, :, :], A["ctx_2"].rearrange("(a p) d -> p a d", p=P)).then_inc(ctx_in, 16)
            for tt in range(TT):
                if tt == 1:
                    g.wait_ge(filled, nth(filled, ("S", 2, 3)))
                for h in range(8):
                    for r in range(2):
                        row = 2 * tt + r
                        src = bass.AP(tensor=A["rpb_2"].tensor, offset=h * 465 + (7 - row) * 31 + 15 - 63,
                                      ap=[[1, 64], [31, 4], [1, 64]])
                        g.dma_start(nab2[64 * r:64 * r + 64, h, :].rearrange("p (a b) -> p a b", b=64), src).then_inc(bias_in[tt], 16)
            g.wait_ge(madeV, nth(madeV, "biasB"))
            g.dma_start(biasB[0:E, 0:2048], A["b_gu_2"]).then_inc(biasb_in, 16)
            g.dma_start(biasB[0:E, 2048:3072], A["b_dn_2"]).then_inc(biasb_in, 16)

        units1 = [(g, tt, a) for g in range(4) for tt in range(TT) for a in ("cmp", "slc", "win")]
        units2 = [(a, hp, tt) for tt in range(TT) for a in ("na", "gqa") for hp in range(4)]

        @block.tensor
        def _(pe):
            ident = cst("ident")
            ones = cst("ones")

            def free_chunk(ins):
                ins.then_inc(freed, 1)

            def transpose(dst, src):
                return nc.tensor.transpose(dst, src, ident[0:src.shape[0], 0:src.shape[0]])

            pe.wait_ge(xin, 32)
            for tt in range(TT):
                for k in range(KD):
                    last = transpose(ps[:, 1 + tt * 2 + k // 4, (k % 4) * P:(k % 4 + 1) * P], hN[:, tt, k * P:(k + 1) * P])
            last.then_inc(filled, mark(filled, "x"))
            pe.wait_ge(small_in, SMALL)
            pe.wait_ge(madeV, nth(madeV, "dt rows"))
            for n in range(3):
                last = transpose(ps[:, 0, n * P:(n + 1) * P], packs[:, n, :])
            last.then_inc(filled, mark(filled, "cols"))

            def sumsq(key, bank, sq, n=T):
                pe.wait_ge(madeA, nth(madeA, ("sq", key)))
                for k in range(KD):
                    last = mm(ps[:, bank, 0:n], ones, sq[:, k, :], start=k == 0, stop=k == KD - 1)
                last.then_inc(filled, mark(filled, ("ss", key)))

            sumsq("n1", 5, hT[:, :, T:2 * T])
            def modulation(key, c, cpad, bank):
                w = weights(pe, (key, c))
                at = (c // 2 % 4) * P
                for k in range(KD):
                    for m in range(2):
                        r = 32 * (2 * (c % 2) + m)
                        last = mm(ps[r:r + 32, bank, at:at + P], cpad[:, k, :], w[:, k, m * P:(m + 1) * P],
                                  start=k == 0, stop=k == KD - 1)
                if c % 8 == 7:
                    last.then_inc(filled, mark(filled, (key, "rows", c // 8)))
                pending[0] += 1

            def turn_modulation(bank):
                for b in range(12):
                    last = transpose(ps[:, bank + b // 4, (b % 4) * P:(b % 4 + 1) * P],
                                     hT[:, b // 2, T + (b % 2) * P:T + (b % 2 + 1) * P])
                return last

            pe.wait_ge(madeV, nth(madeV, "csil"))
            for c in range(24):
                if c == 12:
                    pe.wait_ge(madeV, nth(madeV, "bd"))
                    pe.wait_ge(tables_in, TABLES)
                    for n in range(2):
                        for q in range(4):
                            last = transpose(ps[:, 4 + n, q * P:(q + 1) * P], bd[:, n, q * P:(q + 1) * P])
                    last.then_inc(filled, mark(filled, "bbT"))
                    for n in range(2):
                        for q in range(4):
                            last = transpose(ps[:, n, q * P:(q + 1) * P], cR[:, n, q * P:(q + 1) * P])
                    last.then_inc(filled, mark(filled, "cT"))
                modulation("mod1", c, cpad1, (2, 6, 7)[c // 8])
            pe.wait_ge(emptied, nth(emptied, ("mod1", 2)))
            turn_modulation(5).then_inc(filled, mark(filled, "mod1"))

            pe.wait_ge(madeV, nth(madeV, "h1"))
            turn = [0]

            def take_bank():
                b = turn[0] % 4
                g = turn[0]
                if g >= 4:
                    pe.wait_ge(emptied, nth(emptied, ("p1", g - 4)))
                else:
                    pe.wait_ge(emptied, nth(emptied, "cT"))
                turn[0] += 1
                return b, g

            def projT(key, c):
                w = weights(pe, (key, c))
                b, g = take_bank()
                for m in range(2):
                    for k in range(KD):
                        last = mm(ps[:, b, m * T:(m + 1) * T], w[:, k, m * P:(m + 1) * P], hT[:, k, 0:T],
                                  start=k == 0, stop=k == KD - 1)
                last.then_inc(filled, mark(filled, ("p1", g)))
                return last

            def projN(key, n):
                w = weights(pe, (key, 0))
                b, g = take_bank()
                for tt in range(TT):
                    for k in range(KD):
                        last = mm(ps[:, b, tt * n:(tt + 1) * n], hT[:, k, tt * P:(tt + 1) * P], w[:, k, :],
                                  start=k == 0, stop=k == KD - 1)
                last.then_inc(filled, mark(filled, ("p1", g)))

            def ssm_in(j):
                if j >= 2:
                    pe.wait_ge(vemptied, nth(vemptied, ("bu", j - 2)))
                elif j == 0:
                    pe.wait_ge(emptied, nth(emptied, ("p1", 1)))
                q, r = j // 4, 32 * (j % 4)
                for n in range(2):
                    last = mm(ps[:, 4 + j % 2, n * T:(n + 1) * T], bbT[r:r + 32, n, q, :], uT[r:r + 32, q, :],
                              start=True, stop=True)
                last.then_inc(filled, mark(filled, ("bu", j)))

            def ssm_out(j):
                pe.wait_ge(madeV, nth(madeV, ("s", j)))
                q, r = j // 4, 32 * (j % 4)
                for n in range(2):
                    last = mm(ps[r:r + 32, 6 + q // 2, (q % 2) * T:(q % 2 + 1) * T], cT[:, n, q, r:r + 32],
                              ss2[j % 2][:, n, :], start=n == 0, stop=n == 1)
                last.then_inc(filled, mark(filled, ("y", j)))

            done_j = [0, 0]

            def ssm_step():
                if done_j[0] < 16:
                    ssm_in(done_j[0])
                    done_j[0] += 1
                if done_j[0] >= 3 and done_j[1] < 16:
                    ssm_out(done_j[1])
                    done_j[1] += 1

            def freeing(n=1):
                pending[0] += n

            for n, c, _ in IN1:
                if n in ("u", "q"):
                    projT(n, c)
                elif n in ("kcmp", "vcmp", "kslc", "kwin"):
                    projT(n, 0)
                else:
                    projN(n, 256)
                freeing()
                if n != "u":
                    ssm_step()
            projN("ng", 48)
            freeing()
            pe.wait_ge(emptied, nth(emptied, ("p1", turn[0] - 1)))
            pe.wait_ge(blocks_made, 2)
            w = [[weights(pe, ("cw1", kv, c)) for c in range(2)] for kv in range(2)]
            for c in range(16):
                for kv in range(2):
                    last = mm(ps[64 * kv:64 * kv + 64, 0, 0:256], blocks[kv][c], w[kv][c // 8][:, c % 8, :],
                              start=c == 0, stop=c == 15)
            last.then_inc(filled, mark(filled, "hidR"))
            freeing(4)
            ssm_step()
            pe.wait_ge(madeA, nth(madeA, "hidR"))
            for m in range(2):
                last = transpose(ps[:, 1, m * P:(m + 1) * P], hidR[:, m * P:(m + 1) * P])
            last.then_inc(filled, mark(filled, "hidT"))
            ssm_step()
            pe.wait_ge(madeA, nth(madeA, "hid"))
            for s in range(2):
                for m in range(2):
                    last = mm(ps[64 * s:64 * s + 64, 2, 0:60], w2c[:, 0, m, :], hid[:, m, 0:60], start=m == 0, stop=m == 1)
            for g in range(4):
                for m in range(2):
                    last = mm(ps[0:NCMP, 3, g * HD:(g + 1) * HD], hid[:, m, 64 + g * NCMP:64 + (g + 1) * NCMP], w2c[:, 1, m, :],
                              start=m == 0, stop=m == 1)
            last.then_inc(filled, mark(filled, "kc"))
            while done_j[1] < 16:
                ssm_step()

            def seg(n, u):
                if n == 1:
                    g, tt, a = u
                    return (4, 16 if a == "cmp" else P * (tt + 1))
                return (2, 512)

            def scores(n, i, u):
                b = 2 * (i % 2)
                if i >= 2:
                    pe.wait_ge(madeA, nth(madeA, ("exp", n, i - 2)))
                if n == 1:
                    g, tt, a = u
                    nk = seg(1, u)[1]
                    for s in range(4):
                        par, half = s // 2, s % 2
                        hb = 64 * par
                        q = qT[hb:hb + 64, 2 * g + half, tt * P:(tt + 1) * P]
                        o = ps[:, b + par, half * nk:(half + 1) * nk]
                        if a == "cmp":
                            o = o[:, 0:NCMP]
                            mm(o, q, kcT[hb:hb + 64, g * NCMP:(g + 1) * NCMP], start=True, stop=False)
                            last = mm(o, ident, cst("cmpmask", tt * NCMP, (tt + 1) * NCMP), start=False, stop=True)
                        else:
                            kk = (kslc if a == "slc" else kwin)[hb:hb + 64, g, 0:nk]
                            mm(o, q, kk, start=True, stop=True)
                            last = mm(o[:, nk - P:nk], ident, cst("causal"), start=False, stop=True, skip_group_check=True)
                else:
                    a, hp, tt = u
                    for s in range(2):
                        q = (qaT if a == "na" else qbT)[64 * s:64 * s + 64, hp, tt * P:(tt + 1) * P]
                        kk = kaT[64 * s:64 * s + 64, hp, :] if a == "na" else kbT[64 * s:64 * s + 64, hp // 2, :]
                        o = ps[:, b + s, :]
                        last = mm(o, q, kk, start=True, stop=True)
                        if a == "na":
                            last = mm(o[:, 0:T], cst("mirror"), nab2[:, 2 * hp + s, :], start=False, stop=True, skip_group_check=True)
                last.then_inc(filled, mark(filled, ("S", n, i)))

            def turned(n, i, u):
                pe.wait_ge(madeV, nth(madeV, ("P", n, i)))
                if i >= 1:
                    pe.wait_ge(madeA, nth(madeA, ("PT", n, i - 1)))
                E_ = (Eb if n == 1 else E2)[i % 2]
                ns, nk = seg(n, u)
                if nk == 16:
                    for s in range(ns):
                        last = nc.tensor.transpose(ps[0:NCMP, 4, s * P:(s + 1) * P], E_[:, s * 16:s * 16 + NCMP], ident)
                else:
                    for kb in range(nk // P):
                        for s in range(ns):
                            x = kb * ns + s
                            last = transpose(ps[:, 4 + x // 4, (x % 4) * P:(x % 4 + 1) * P], E_[:, s * nk + kb * P:s * nk + (kb + 1) * P])
                last.then_inc(filled, mark(filled, ("T", n, i)))

            def values(n, i, u):
                pe.wait_ge(madeA, nth(madeA, ("PT", n, i)))
                ns, nk = seg(n, u)
                pt = (PT if n == 1 else PT2)[i % 2].rearrange("p (k s q) -> p k s q", s=ns, q=P)
                if n == 1:
                    g, tt, a = u
                    if a == "cmp" and i >= 3:
                        pe.wait_ge(emptied, nth(emptied, ("O", n, i - 1)))
                    for par in range(2):
                        o = ps[64 * par:64 * par + 64, 6, 0:2 * P]
                        if a == "cmp":
                            last = mm(o, vcN[0:NCMP, g, :], pt[0:NCMP, 0, 2 * par:2 * par + 2, :], start=True, stop=False, skip_group_check=True)
                        else:
                            v = vslc if a == "slc" else vwin
                            for kb in range(nk // P):
                                last = mm(o, v[:, kb, g * HD:(g + 1) * HD], pt[:, kb, 2 * par:2 * par + 2, :], start=False,
                                          stop=a == "win" and kb == nk // P - 1, skip_group_check=True)
                    last.then_inc(filled, mark(filled, ("O", n, i)))
                else:
                    a, hp, tt = u
                    if i >= 2:
                        pe.wait_ge(emptied, nth(emptied, ("O", n, i - 2)))
                    for par in range(2):
                        o = ps[64 * par:64 * par + 64, 6 + i % 2, 0:P]
                        for kb in range(4):
                            h = 2 * hp + par
                            v = vN[:, kb, h * HD:(h + 1) * HD] if a == "na" else vbN[:, kb, (hp // 2) * HD:(hp // 2 + 1) * HD]
                            last = mm(o, v, pt[:, kb, par, :], start=kb == 0, stop=kb == 3)
                    last.then_inc(filled, mark(filled, ("O", n, i)))

            def attention(n, units):
                scores(n, 0, units[0])
                scores(n, 1, units[1])
                turned(n, 0, units[0])
                for i, u in enumerate(units):
                    if i + 2 < len(units):
                        if n == 2 and units[i + 2] == ("na", 0, 1):
                            pe.wait_ge(madeV, nth(madeV, ("bias", 1)))
                        scores(n, i + 2, units[i + 2])
                    if n == 1:
                        if i % 8 == 0 and i > 0:
                            pe.wait_ge(emptied, nth(emptied, ("mod2", i // 8 - 1)))
                        modulation("mod2", i, cpad2, 7)
                    if i + 1 < len(units):
                        turned(n, i + 1, units[i + 1])
                    values(n, i, u)

            pe.wait_ge(madeA, nth(madeA, "kc"))
            pe.wait_ge(madeV, nth(madeV, "yD"))
            attention(1, units1)
            w = weights(pe, ("glu", 0))
            for m in range(4):
                for k in range(4):
                    last = mm(ps[:, m // 2, (m % 2) * T:(m % 2 + 1) * T], w[:, k, m * P:(m + 1) * P], yS[:, k, :],
                              start=k == 0, stop=k == 3)
            last.then_inc(filled, mark(filled, "z"))
            freeing()

            pe.wait_ge(emptied, nth(emptied, ("O", 1, len(units1) - 1)))
            pe.wait_ge(emptied, nth(emptied, ("mod2", 2)))
            turn_modulation(4).then_inc(filled, mark(filled, "mod2"))
            so = None
            for c in range(4):
                if c >= 1:
                    pe.wait_ge(madeV, nth(madeV, ("mgd", c - 1)))
                if c % 2 == 0:
                    so = weights(pe, ("so", c // 2))
                for n, key in enumerate(("mga", "mgs")):
                    w = weights(pe, (key, c))
                    for m in range(2):
                        for k in range(KD):
                            last = mm(ps[:, 2 + n, m * T:(m + 1) * T], w[:, k, m * P:(m + 1) * P], hT[:, k, 0:T],
                                      start=k == 0, stop=k == KD - 1)
                last.then_inc(filled, mark(filled, ("gates", c)))
                if c == 0:
                    pe.wait_ge(madeV, nth(madeV, "yS"))
                w = weights(pe, ("no", c))
                for m in range(2):
                    for k in range(KD):
                        last = mm(ps[:, 0, m * T:(m + 1) * T], w[:, k, m * P:(m + 1) * P], oT[:, k, :],
                                  start=k == 0, stop=k == KD - 1)
                for m in range(2):
                    mc = (c % 2) * 2 + m
                    for k in range(4):
                        last = mm(ps[:, 1, m * T:(m + 1) * T], so[:, k, mc * P:(mc + 1) * P], yS[:, k, :],
                                  start=k == 0, stop=k == 3)
                last.then_inc(filled, mark(filled, ("branch", c)))
                freeing(3 if c % 2 == 0 else 4)
            for c in range(4):
                if c == 0:
                    pe.wait_ge(madeV, nth(madeV, ("mgd", 3)))
                w = weights(pe, ("wo", c))
                for m in range(2):
                    for k in range(KD):
                        last = mm(ps[:, 4 + c, m * T:(m + 1) * T], w[:, k, m * P:(m + 1) * P], mgd[:, k, :],
                                  start=k == 0, stop=k == KD - 1)
                last.then_inc(filled, mark(filled, ("tm", c)))
                freeing()

            def moe_front(n, wr, nr, rbias):
                key = f"f{n}"
                sumsq(key, 0, hT[:, :, T:2 * T])
                pe.wait_ge(madeV, nth(madeV, "h" + key))
                for tt in range(TT):
                    for k in range(KD):
                        mm(ps[:, 5, tt * 64:tt * 64 + nr], hT[:, k, tt * P:(tt + 1) * P], wr[:, k, :], start=k == 0, stop=False)
                    last = mm(ps[:, 5, tt * 64:tt * 64 + nr], ones[0:1, :], rbias, start=False, stop=True)
                last.then_inc(filled, mark(filled, "logits" + key))
                for tt in range(TT):
                    for k in range(KD):
                        last = transpose(ps[:, 1 + tt * 2 + k // 4, (k % 4) * P:(k % 4 + 1) * P], hT[:, k, tt * P:(tt + 1) * P])
                last.then_inc(filled, mark(filled, "hN" + key))
                pe.wait_ge(madeV, nth(madeV, "chosen" + key))
                for tt in range(TT):
                    mm(ps[:, 5, 128 + tt * E:128 + (tt + 1) * E], cst("before"), Am[:, tt, :], start=True, stop=tt == 0)
                    if tt == 1:
                        last = mm(ps[:, 5, 128 + E:128 + 2 * E], ones, Am[:, 0, :], start=False, stop=True)
                for tt in range(TT):
                    last = mm(ps[0:1, 5, 256:256 + E], ones[:, 0:1], Am[:, tt, :], start=tt == 0, stop=tt == 1)
                last.then_inc(filled, mark(filled, "places" + key))
                pe.wait_ge(madeV, nth(madeV, "tables" + key))
                for b in range(4):
                    last = mm(ps[:, 4 + b, :], zero[:, 0:P], zero, start=True, stop=True)
                last.then_inc(filled, mark(filled, "zeroed" + key))

            def gather_pair(s, onehot):
                for k in range(KD):
                    for tt in range(TT):
                        last = mm(ps[:, 2 * (k // 4), (k % 4) * P:(k % 4 + 1) * P], hN[:, tt, k * P:(k + 1) * P], onehot[:, tt, :],
                                  start=tt == 0, stop=tt == 1)
                last.then_inc(s["gathered"], 1)

            def gather(s, xs_onehot):
                for k in range(KD):
                    for tt in range(TT):
                        last = mm(ps[:, 0, k * SLOTS:(k + 1) * SLOTS], hN[:, tt, k * P:(k + 1) * P], xs_onehot[:, tt, :],
                                  start=tt == 0, stop=tt == 1)
                last.then_inc(s["gathered"], 1)

            def spread_turn(s, onehot, bank, at):
                for tt in range(TT):
                    last = transpose(ps[:, bank, at + tt * P:at + (tt + 1) * P], onehot[:, tt, :])
                last.then_inc(s["spreadT"], 1)

            def scatter_pair(s, ys, onehotT):
                for k in range(KD):
                    last = mm(ps[:, 4 + k // 2, (k % 2) * T:(k % 2 + 1) * T], ys[:, k * P:(k + 1) * P], onehotT,
                              start=False, stop=False, skip_group_check=True)
                last.then_inc(s["scattered"], 1)

            def scatter(s, ys, onehotT):
                for c in (0, 4, 1, 5, 2, 6, 3, 7):
                    r = 64 * (c // 4)
                    last = mm(ps[:, 4 + c // 2, (c % 2) * T:(c % 2 + 1) * T], ys[r:r + 64, (c % 4) * P:(c % 4 + 1) * P],
                              onehotT[r:r + 64, :], start=False, stop=False, skip_group_check=True)
                last.then_inc(s["scattered"], 1)

            def act_turn(n, s):
                for j in range(4 if n == 2 else 2):
                    last = transpose(ps[:, 3, j * P:(j + 1) * P], act[:, j * P:(j + 1) * P])
                last.then_inc(s["turned"], 1)

            def pair_tile(it, u, j, shape):
                i = moe1_at + 6 * u + j
                pe.wait_ge(full[i % RING], it * 16 + 16 * (i // RING + 1))
                return slot_ap(i, shape)

            def hidden_pair(it, u, s, xs):
                for n in range(2):
                    w = [pair_tile(it, u, 2 * n + x, (KD, 256)) for x in range(2)]
                    for k in range(KD):
                        for x in range(2):
                            last = mm(ps[64 * x:64 * x + 64, 1, n * 256:(n + 1) * 256], xs[:, k, x * SLOTS:(x + 1) * SLOTS],
                                      w[x][:, k, :], start=k == 0, stop=k == KD - 1)
                last.then_inc(s["hidden"], 1)

            def down_pair(it, u, s):
                w = [pair_tile(it, u, 4 + x, (2, D)) for x in range(2)]
                for half in range(2):
                    for f in range(2):
                        for x in range(2):
                            last = mm(ps[64 * x:64 * x + 64, 3 * half, :], actT[:, f, x * SLOTS:(x + 1) * SLOTS],
                                      w[x][:, f, half * 512:(half + 1) * 512], start=f == 0, stop=f == 1)
                last.then_inc(s["down"], 1)

            def rows2(e, j):
                i = moe2_at + j
                pe.wait_ge(full[i % RING], e * 16 + 16 * (i // RING + 1))
                return slot_ap(i, (2, D))

            def hidden2(e, u, s, xs, first):
                for n in range(2):
                    for r in range(2):
                        mm(ps[64 * r:64 * r + 64, 1 + n, :], esel[u], biasB[:, n * D + r * 512:n * D + (r + 1) * 512],
                           start=True, stop=False)
                for k in range(KD):
                    w = rows2(e, k)
                    for n in range(2):
                        for r in range(2):
                            last = mm(ps[64 * r:64 * r + 64, 1 + n, :], xs[:, k, :], w[:, n, r * 512:(r + 1) * 512],
                                      start=False, stop=k == KD - 1)
                    if k == KD - 1:
                        last.then_inc(s["hidden"], 1)
                    elif first:
                        last.then_inc(used2, 1)

            def down2(e, u, s, first):
                for r in range(2):
                    mm(ps[64 * r:64 * r + 64, 3, :], esel[u], biasB[:, 2048 + r * 512:2048 + (r + 1) * 512], start=True, stop=False)
                for f in range(8):
                    w = rows2(e, 8 + f // 2)
                    for r in range(2):
                        last = mm(ps[64 * r:64 * r + 64, 3, :], actT[:, f % 4, (f // 4) * 64:(f // 4 + 1) * 64],
                                  w[:, f % 2, r * 512:(r + 1) * 512], start=False, stop=f == 7)
                    if first and f % 2 == 1 and f < 7:
                        last.then_inc(used2, 1)
                last.then_inc(s["down"], 1)

            def moe1():
                s, x = S[1, "first"], S[1, "more"]

                def further(it, u, p, q, b):
                    pe.wait_ge(s["ys"], p + 1)
                    pe.wait_ge(x["gather_onehot"], q + 1)
                    gather_pair(x, ohgM)
                    pe.wait_ge(x["xs"], q + 1)
                    hidden_pair(it, u, x, xsM1)
                    pe.wait_ge(x["spread_onehot"], q + 1)
                    spread_turn(x, ohsM, 3, T)
                    pe.wait_ge(x["act"], q + 1)
                    act_turn(1, x)
                    pe.wait_ge(x["actT"], q + 1)
                    pe.wait_ge(x["spread"], q + 1)
                    down_pair(it, u, x)
                    pe.wait_ge(x["ys"], q + 1)
                    scatter_pair(x, ysM1, ohtM)

                def first(it, u, p):
                    hidden_pair(it, u, s, xsP)
                    pe.wait_ge(s["gather_onehot"], p + 2)
                    pe.wait_ge(s["ys"], p + 1)
                    gather_pair(s, ohgF)
                    pe.wait_ge(s["spread_onehot"], p + 1)
                    spread_turn(s, ohsF, 3, T)
                    pe.wait_ge(s["act"], p + 1)
                    act_turn(1, s)
                    scatter_pair(s, ysF1, ohtF[(u + 1) % 2])
                    pe.wait_ge(s["actT"], p + 1)
                    pe.wait_ge(s["spread"], p + 2)
                    pe.wait_ge(s["xs"], p + 2)
                    down_pair(it, u, s)

                def begin(it, u, p):
                    pe.wait_ge(s["xs"], p + 1)
                    pe.wait_ge(s["spread"], p + 1)

                pe.wait_ge(s["gather_onehot"], 1)
                gather_pair(s, ohgF)
                run_experts(pe, 1, further, first, begin)
                pe.wait_ge(s["ys"], E // 2 + 1)
                pe.wait_ge(s["spread"], E // 2 + 1)
                scatter_pair(s, ysF1, ohtF[1])

            def moe2():
                s, x = S[2, "first"], S[2, "more"]

                def further(it, u, e, q, b):
                    pe.wait_ge(s["ys"], e + 1)
                    pe.wait_ge(x["gather_onehot"], q + 1)
                    gather(x, ohgM[:, :, 0:SLOTS])
                    pe.wait_ge(x["xs"], q + 1)
                    hidden2(e, u, x, xsM, False)
                    pe.wait_ge(x["act"], q + 1)
                    act_turn(2, x)
                    pe.wait_ge(x["spread_onehot"], q + 1)
                    spread_turn(x, ohsM, 1, 0)
                    pe.wait_ge(x["actT"], q + 1)
                    down2(e, u, x, False)
                    pe.wait_ge(x["ys"], q + 1)
                    pe.wait_ge(x["spread"], q + 1)
                    scatter(x, ysM, ohtM)

                def first(it, u, e):
                    hidden2(e, u, s, xsF, True)
                    pe.wait_ge(s["gather_onehot"], e + 2)
                    gather(s, ohgF[:, :, 0:SLOTS])
                    pe.wait_ge(s["act"], e + 1)
                    pe.wait_ge(s["ys"], e + 1)
                    act_turn(2, s)
                    pe.wait_ge(s["spread_onehot"], e + 1)
                    spread_turn(s, ohsF, 1, 0)
                    scatter(s, ysF, ohtF[(u + 1) % 2])
                    pe.wait_ge(s["actT"], e + 1)
                    down2(e, u, s, True)

                def begin(it, u, e):
                    pe.wait_ge(s["xs"], e + 1)
                    pe.wait_ge(s["spread"], e + 1)

                pe.wait_ge(s["gather_onehot"], 1)
                gather(s, ohgF[:, :, 0:SLOTS])
                run_experts(pe, 2, further, first, begin)
                pe.wait_ge(s["ys"], E + 1)
                pe.wait_ge(s["spread"], E + 1)
                scatter(s, ysF, ohtF[1])

            moe_front(1, wr1, 36, rb[0:1, 0:36])
            moe1()

            last = mm(ps[:, 0, 0:1], ones, csil[:, 0:1], start=True, stop=True)
            last.then_inc(filled, mark(filled, "moe1"))
            sumsq("fin", 0, hT[:, :, T:2 * T])
            sumsq("n2", 0, hT[:, :, T:2 * T])
            pe.wait_ge(ctx_in, 16)
            for tt in range(TT):
                for k in range(KD):
                    last = transpose(ps[:, 1 + tt * 2 + k // 4, (k % 4) * P:(k % 4 + 1) * P], hN[:, tt, k * P:(k + 1) * P])
            last.then_inc(filled, mark(filled, "ctx"))
            pe.wait_ge(madeA, nth(madeA, ("sq", "ctx")))
            for k in range(KD):
                last = mm(ps[:, 5, 0:T], ones, mgd[:, k, :], start=k == 0, stop=k == KD - 1)
            last.then_inc(filled, mark(filled, ("ss", "ctx")))
            pe.wait_ge(madeV, nth(madeV, "h2"))
            pe.wait_ge(madeV, nth(madeV, "hctx"))
            turn2 = [0]

            def bank2():
                g = turn2[0]
                if g >= 4:
                    pe.wait_ge(emptied, nth(emptied, ("p2", g - 4)))
                turn2[0] += 1
                return g % 4, g

            def fill2(outs):
                b, g = bank2()
                for o, lhs, rhs in outs:
                    for k in range(KD):
                        last = mm(o(b), lhs(k), rhs(k), start=k == 0, stop=k == KD - 1)
                last.then_inc(filled, mark(filled, ("p2", g)))

            w = weights(pe, ("kvb2", 0))
            for h in range(2):
                fill2([(lambda b, x=x: ps[:, b, x * 256:(x + 1) * 256],
                        lambda k, x=x, h=h: hT[:, k, (2 * h + x) * P:(2 * h + x + 1) * P], lambda k: w[:, k, :]) for x in range(2)])
            freeing()
            for c in range(2):
                w = weights(pe, ("qb2", c))
                fill2([(lambda b, x=x: ps[:, b, x * 256:(x + 1) * 256],
                        lambda k, x=x: hT[:, k, x * P:(x + 1) * P], lambda k: w[:, k, :]) for x in range(2)])
                freeing()
            for c in range(2):
                w = weights(pe, ("ka2", c))
                for m in range(2):
                    fill2([(lambda b: ps[:, b, :], lambda k, m=m: w[:, k, m * P:(m + 1) * P], lambda k: hT[:, k, :])])
                freeing()
            for c in range(2):
                w = weights(pe, ("va2", c))
                for h in range(2):
                    fill2([(lambda b, x=x: ps[:, b, x * 256:(x + 1) * 256],
                            lambda k, x=x, h=h: hT[:, k, (2 * h + x) * P:(2 * h + x + 1) * P], lambda k: w[:, k, :]) for x in range(2)])
                freeing()
            for c in range(2):
                w = weights(pe, ("qa2", c))
                fill2([(lambda b, m=m: ps[:, b, m * T:(m + 1) * T], lambda k, m=m: w[:, k, m * P:(m + 1) * P],
                        lambda k: hT[:, k, 0:T]) for m in range(2)])
                freeing()
            pe.wait_ge(madeV, nth(madeV, "rope"))
            for tt in range(TT):
                for m in range(4):
                    x = m * TT + tt
                    last = transpose(ps[:, 4 + x // 4, (x % 4) * P:(x % 4 + 1) * P], qbN[:, tt, m * P:(m + 1) * P])
            last.then_inc(filled, mark(filled, "qbT"))
            for kb in range(4):
                last = transpose(ps[:, 6, kb * P:(kb + 1) * P], kbN[:, kb, :])
            for kb in range(4):
                last = transpose(ps[:, 7, kb * P:(kb + 1) * P], kt1[:, kb, :])
            last.then_inc(filled, mark(filled, "kbT"))
            pe.wait_ge(emptied, nth(emptied, "kbT"))
            pe.wait_ge(emptied, nth(emptied, ("p2", turn2[0] - 1)))
            pe.wait_ge(madeV, nth(madeV, ("bias", 0)))
            attention(2, units2)
            pe.wait_ge(emptied, nth(emptied, ("O", 2, len(units2) - 1)))
            for c in range(4):
                if c >= 1:
                    pe.wait_ge(madeV, nth(madeV, ("mgd2", c - 1)))
                for n, key in enumerate(("ga2", "gb2")):
                    w = weights(pe, (key, c))
                    for m in range(2):
                        for k in range(KD):
                            last = mm(ps[:, 2 + n, m * T:(m + 1) * T], w[:, k, m * P:(m + 1) * P], hT[:, k, 0:T],
                                      start=k == 0, stop=k == KD - 1)
                last.then_inc(filled, mark(filled, ("gates2", c)))
                if c % 2 == 0:
                    oo = [weights(pe, ("oo" + x, c // 2)) for x in "ab"]
                for n in range(2):
                    for m in range(2):
                        mc = (c % 2) * 2 + m
                        for k in range(4):
                            last = mm(ps[:, n, m * T:(m + 1) * T], oo[n][:, k, mc * P:(mc + 1) * P], o2[:, 4 * n + k, :],
                                      start=k == 0, stop=k == 3)
                last.then_inc(filled, mark(filled, ("branch2", c)))
                freeing(2 if c % 2 == 0 else 4)
            for c in range(4):
                if c == 0:
                    pe.wait_ge(madeV, nth(madeV, ("mgd2", 3)))
                w = weights(pe, ("w_o2", c))
                for m in range(2):
                    for k in range(KD):
                        last = mm(ps[:, 4 + c, m * T:(m + 1) * T], w[:, k, m * P:(m + 1) * P], mgd[:, k, :],
                                  start=k == 0, stop=k == KD - 1)
                last.then_inc(filled, mark(filled, ("y2", c)))
                freeing()
            sumsq("post", 0, hT[:, :, T:2 * T])
            moe_front(2, wr2, 32, rb[0:1, 36:68])
            pe.wait_ge(biasb_in, 32)
            moe2()
            last = mm(ps[:, 0, 0:1], ones, csil[:, 0:1], start=True, stop=True)
            last.then_inc(filled, mark(filled, "moe2"))
            sumsq("postf", 0, hT[:, :, T:2 * T])
            pe.wait_ge(madeV, nth(madeV, "xout"))
            for tt in range(TT):
                for k in range(KD):
                    last = transpose(ps[:, 1 + tt * 2 + k // 4, (k % 4) * P:(k % 4 + 1) * P], xT[:, k, tt * P:(tt + 1) * P])
            last.then_inc(filled, mark(filled, "out"))

        @block.scalar
        def _(act_):
            a = nc.scalar.activation
            for dst, src in vectors:
                act_.dma_start(dst, src).then_inc(small_in, 16)

            def copy(dst, src, scale=1.0):
                return a(dst, src, ACT.Copy, scale=scale)

            def sqrt(key, dst):
                act_.wait_ge(madeV, nth(madeV, ("var", key)))
                a(dst, dst, ACT.Sqrt).then_inc(madeA, mark(madeA, ("std", key)))

            def square(key, src):
                a(hT[:, :, T:2 * T], src, ACT.Square).then_inc(madeA, mark(madeA, ("sq", key)))

            def four_banks(dst_of):
                for tt in range(TT):
                    for q in range(2):
                        src = ps[:, 1 + tt * 2 + q, :]
                        last = copy(dst_of(tt, q), src)
                return last

            act_.wait_ge(filled, nth(filled, "x"))
            for tt in range(TT):
                for q in range(2):
                    last = copy(xT[:, 4 * q:4 * q + 4, tt * P:(tt + 1) * P], ps[:, 1 + tt * 2 + q, :].rearrange("p (k t) -> p k t", t=P))
            act_.drain()
            square("n1", xT[:, :, :])
            act_.wait_ge(filled, nth(filled, "cols"))
            copy(cols[:, :, :].rearrange("p a b -> p (a b)"), ps[:, 0, 0:3 * P])
            act_.drain()
            a(csil[:, :], cols[:, 0, 104:128], ACT.Sigmoid).then_inc(madeA, mark(madeA, "cols"))
            a(small[:, 0, :], cols[:, 2, 32:48], ACT.Exp).then_inc(madeA, mark(madeA, "dt"))
            sqrt("n1", rstd[:, 0:T])
            act_.wait_ge(madeV, nth(madeV, "angle"))
            a(small[:, 4, :], small[:, 1, :], ACT.Exp)
            a(small[:, 5, :], small[:, 3, :], ACT.Sin, scale=SIN2PI)
            a(small[:, 6, :], small[:, 3, :], ACT.Sin, scale=SIN2PI / 2).then_inc(madeA, mark(madeA, "trig"))
            def mod_out(key, i, bank):
                act_.wait_ge(filled, nth(filled, (key, "rows", i)))
                copy(mod_rows[i], ps[:, bank, :].rearrange("p (a b) -> p a b", a=2)).then_inc(emptied, mark(emptied, (key, i)))

            mod_out("mod1", 0, 2)
            act_.wait_ge(filled, nth(filled, "bbT"))
            for n in range(2):
                last = copy(bbT[:, n, :, :].rearrange("p a b -> p (a b)"), ps[:, 4 + n, :])
            last.then_inc(emptied, mark(emptied, "bbT"))
            act_.wait_ge(filled, nth(filled, "cT"))
            for n in range(2):
                last = copy(cT[:, n, :, :].rearrange("p a b -> p (a b)"), ps[:, n, :])
            last.then_inc(emptied, mark(emptied, "cT"))
            mod_out("mod1", 1, 6)
            mod_out("mod1", 2, 7)

            turn = [0]
            nsin = [0]

            def take(fn):
                g = turn[0]
                act_.wait_ge(filled, nth(filled, ("p1", g)))
                fn(ps[:, g % 4, :]).then_inc(emptied, mark(emptied, ("p1", g)))
                turn[0] += 1

            def sines():
                j = nsin[0]
                if j >= 16:
                    return
                act_.wait_ge(madeV, nth(madeV, ("fr", j)))
                if j >= 2:
                    act_.wait_ge(madeV, nth(madeV, ("s", j - 2)))
                a(tabs[j % 2][:, 1, :], fr[j % 2], ACT.Sin, scale=SIN2PI)
                a(tabs[j % 2][:, 0, :], fr[j % 2], ACT.Sin, scale=SIN2PI / 2)
                act_.drain()
                a(tabs[j % 2][:, 0, :], tabs[j % 2][:, 0, :], ACT.Square).then_inc(madeA, mark(madeA, ("sin", j)))
                nsin[0] += 1

            two = lambda v: v.rearrange("p (a b) -> p a b", a=2)
            for n, c, _ in IN1:
                if n in ("u", "q"):
                    dst = (uT if n == "u" else qT)[:, 2 * c:2 * c + 2, :]
                    take(lambda b: copy(dst, two(b), 0.125 if n == "q" else 1.0))
                    sines()
                elif n in ("kslc", "kwin"):
                    dst = kslc if n == "kslc" else kwin

                    def both(b):
                        for s in range(2):
                            for h in range(2):
                                last = copy(dst[64 * h:64 * h + 64, s::2, :], two(b)[64 * s:64 * s + 64])
                        return last
                    take(both)
                    sines()
                elif n in ("kcmp", "vcmp"):
                    kv = kcmp if n == "kcmp" else vcmp

                    def shifted(b):
                        for s in range(2):
                            copy(kv[0:64, s::2, :], two(b)[64 * s:64 * s + 64])
                            last = copy(kv[64:128, s::2, 0:T - 1], two(b)[64 * s:64 * s + 64, :, 1:T])
                        return last
                    take(shifted)
                    sines()
                else:
                    take(lambda b: copy((vslc if n == "vslc" else vwin)[:, :, :], two(b)))
                    sines()
            take(lambda b: a(gates[:, :, :], b[:, 0:96].rearrange("p (a b) -> p a b", a=2), ACT.Sigmoid))
            act_.wait_ge(filled, nth(filled, "hidR"))
            a(hidR, ps[:, 0, 0:256], ACT.Gelu_apprx_tanh).then_inc(madeA, mark(madeA, "hidR"))
            sines()
            act_.wait_ge(filled, nth(filled, "hidT"))
            copy(hid.rearrange("p a b -> p (a b)"), ps[:, 1, 0:256]).then_inc(madeA, mark(madeA, "hid"))
            sines()
            act_.wait_ge(filled, nth(filled, "kc"))
            copy(kcT, ps[:, 2, 0:60])
            copy(vcN[0:NCMP, :, :].rearrange("p a b -> p (a b)"), ps[0:NCMP, 3, 0:256]).then_inc(madeA, mark(madeA, "kc"))
            while nsin[0] < 16:
                sines()
            act_.wait_ge(madeV, nth(madeV, "yD"))
            a(yS, yT, ACT.Gelu_apprx_tanh)

            def seg(n, u):
                if n == 1:
                    g, tt, x = u
                    return (4, 16 if x == "cmp" else P * (tt + 1))
                return (2, 512)

            def exp(n, i, u):
                act_.wait_ge(madeV, nth(madeV, ("mx", n, i)))
                if i >= 2:
                    act_.wait_ge(filled, nth(filled, ("T", n, i - 2)))
                ns, nk = seg(n, u)
                e_ = (Eb if n == 1 else E2)[i % 2]
                m = NCMP if nk == 16 else nk
                for s in range(ns):
                    bank, at = (2 * (i % 2) + s // 2, (s % 2) * nk) if n == 1 else (2 * (i % 2) + s, 0)
                    last = a(e_[:, s * nk:s * nk + m], ps[:, bank, at:at + m], ACT.Exp,
                             bias=stat[:, i % 2, s:s + 1], accum_out=stat[:, i % 2, 4 + s:5 + s])
                last.then_inc(madeA, mark(madeA, ("exp", n, i)))

            def turned(n, i, u):
                act_.wait_ge(filled, nth(filled, ("T", n, i)))
                ns, nk = seg(n, u)
                pt = (PT if n == 1 else PT2)[i % 2]
                if nk == 16:
                    last = copy(pt[0:NCMP, 0:4 * P], ps[0:NCMP, 4, :])
                else:
                    w = ns * nk
                    last = copy(pt[:, 0:w], ps[:, 4:6, :].rearrange("p a b -> p (a b)")[:, 0:w])
                last.then_inc(madeA, mark(madeA, ("PT", n, i)))

            def outs(n, i, u):
                if n == 1:
                    g, tt, x = u
                    if x != "win":
                        return
                    act_.wait_ge(filled, nth(filled, ("O", n, i)))
                    last = copy(oT[:, 2 * g:2 * g + 2, tt * P:(tt + 1) * P], ps[:, 6, 0:2 * P].rearrange("p (a b) -> p a b", a=2))
                else:
                    x, hp, tt = u
                    act_.wait_ge(filled, nth(filled, ("O", n, i)))
                    last = copy(o2[:, (0 if x == "na" else 4) + hp, tt * P:(tt + 1) * P], ps[:, 6 + i % 2, 0:P])
                last.then_inc(emptied, mark(emptied, ("O", n, i)))

            def attention(n, units):
                exp(n, 0, units[0])
                exp(n, 1, units[1])
                turned(n, 0, units[0])
                for i, u in enumerate(units):
                    if i + 2 < len(units):
                        exp(n, i + 2, units[i + 2])
                    if i + 1 < len(units):
                        turned(n, i + 1, units[i + 1])
                    outs(n, i, u)
                    if n == 1 and i % 8 == 7:
                        mod_out("mod2", i // 8, 7)

            def sigmoids(key, c, prev):
                act_.wait_ge(filled, nth(filled, (key, c)))
                if c >= 1:
                    act_.wait_ge(madeV, nth(madeV, (prev, c - 1)))
                for n in range(2):
                    last = a(sgl[:, n, :, :].rearrange("p a b -> p (a b)"), ps[:, 2 + n, :], ACT.Sigmoid)
                last.then_inc(madeA, mark(madeA, ("sgl", key, c)))

            def moe_front(key, do_square=True):
                if do_square:
                    act_.wait_ge(madeV, nth(madeV, "x" + key))
                    square(key, xT[:, :, :])
                sqrt(key, rstd[:, 0:T])
                act_.wait_ge(filled, nth(filled, "hN" + key))
                for tt in range(TT):
                    for q in range(2):
                        last = copy(hN[:, tt, q * 512:(q + 1) * 512], ps[:, 1 + tt * 2 + q, :])
                last.then_inc(madeA, mark(madeA, "hN" + key))
                act_.wait_ge(madeV, nth(madeV, "shifted" + key))
                last = a(Wt[:, :, 0:E], lg[:, :, 0:E], ACT.Exp)
                if key == "f1":
                    last = a(rt[:, :, 0:4], gx[:, :, 0:4], ACT.Exp)
                last.then_inc(madeA, mark(madeA, "exp" + key))
                act_.wait_ge(madeV, nth(madeV, "ready" + key))

            def moe(n):
                s, x = S[n, "first"], S[n, "more"]
                w = 512 if n == 2 else 256

                def block_of(s, q, onehotT):
                    act_.wait_ge(s["glu"], q)
                    a(sg[:, 0:w], glu[:, 0:w], ACT.Sigmoid, scale=1.702 if n == 2 else 1.0).then_inc(s["sig"], 1)
                    act_.wait_ge(s["turned"], q)
                    copy(actT.rearrange("p a b -> p (a b)")[:, 0:w], ps[:, 3, 0:w]).then_inc(s["actT"], 1)
                    act_.wait_ge(s["spreadT"], q)
                    copy(onehotT, ps[:, 3, T:2 * T] if n == 1 else ps[:, 1, 0:T]).then_inc(s["spread"], 1)

                run_experts(act_, n, lambda it, u, e, q, b: block_of(x, q + 1, ohtM),
                            lambda it, u, e: block_of(s, e + 1, ohtF[u % 2]))

            attention(1, units1)
            act_.wait_ge(filled, nth(filled, "z"))
            for m in range(2):
                last = a(mgd[:, 2 * m:2 * m + 2, :].rearrange("p a b -> p (a b)"), ps[:, m, :], ACT.Sigmoid)
            last.then_inc(madeA, mark(madeA, "ysig"))
            for c in range(4):
                sigmoids("gates", c, "mgd")
            moe_front("f1")
            moe(1)
            act_.wait_ge(madeV, nth(madeV, "moe1 out"))
            square("fin", xT[:, :, :])
            sqrt("fin", rstd[:, 0:T])
            act_.wait_ge(madeV, nth(madeV, "x2"))
            square("n2", xT[:, :, :])
            sqrt("n2", rstd[:, 0:T])
            act_.wait_ge(filled, nth(filled, "ctx"))
            for tt in range(TT):
                for q in range(2):
                    last = copy(hT[:, 4 * q:4 * q + 4, T + tt * P:T + (tt + 1) * P], ps[:, 1 + tt * 2 + q, :].rearrange("p (k t) -> p k t", t=P))
            act_.drain()
            a(mgd, hT[:, :, T:2 * T], ACT.Square).then_inc(madeA, mark(madeA, ("sq", "ctx")))
            sqrt("ctx", rstd[:, T:2 * T])
            turn2 = [0]

            def take2(fn):
                g = turn2[0]
                act_.wait_ge(filled, nth(filled, ("p2", g)))
                fn(ps[:, g % 4, :]).then_inc(emptied, mark(emptied, ("p2", g)))
                turn2[0] += 1

            for h in range(2):
                def kv_b(b):
                    copy(kbN[:, 2 * h:2 * h + 2, :], two(b)[:, :, 0:P])
                    return copy(vbN[:, 2 * h:2 * h + 2, :], two(b)[:, :, P:2 * P])
                take2(kv_b)
            for c in range(2):
                take2(lambda b: copy(qbN[:, :, c * 256:(c + 1) * 256], two(b)))
            sqrt("heads", rn[:, 0:24])
            for m in range(4):
                take2(lambda b: copy(kaT[:, m, :], b))
            for c in range(2):
                for h in range(2):
                    take2(lambda b: copy(vN[:, 2 * h:2 * h + 2, c * 256:(c + 1) * 256], two(b)))
            for c in range(2):
                take2(lambda b: copy(qaT[:, 2 * c:2 * c + 2, :], two(b), 0.125))
            act_.wait_ge(filled, nth(filled, "qbT"))
            for n in range(2):
                last = copy(qbT[:, 2 * n:2 * n + 2, :], two(ps[:, 4 + n, :]), 0.125)
            act_.wait_ge(filled, nth(filled, "kbT"))
            copy(kbT[0:64, 0, :], ps[0:64, 6, :])
            copy(kbT[64:128, 1, :], ps[64:128, 6, :])
            copy(kbT[64:128, 0, :], ps[64:128, 7, :])
            copy(kbT[0:64, 1, :], ps[0:64, 7, :]).then_inc(emptied, mark(emptied, "kbT"))
            attention(2, units2)
            for c in range(4):
                sigmoids("gates2", c, "mgd2")
            for c in range(4):
                act_.wait_ge(filled, nth(filled, ("y2", c)))
                copy(o2[:, 2 * c:2 * c + 2, :], two(ps[:, 4 + c, :]))
                last = a(hT[:, 2 * c:2 * c + 2, T:2 * T], two(ps[:, 4 + c, :]), ACT.Square)
            last.then_inc(madeA, mark(madeA, ("sq", "post")))
            sqrt("post", rstd[:, 0:T])
            moe_front("f2")
            moe(2)
            act_.wait_ge(filled, nth(filled, "moe2"))
            for c in range(4):
                copy(o2[:, 2 * c:2 * c + 2, :], two(ps[:, 4 + c, :]))
                last = a(hT[:, 2 * c:2 * c + 2, T:2 * T], two(ps[:, 4 + c, :]), ACT.Square)
            last.then_inc(madeA, mark(madeA, ("sq", "postf")))
            sqrt("postf", rstd[:, 0:T])
            act_.wait_ge(filled, nth(filled, "out"))
            for tt in range(TT):
                for q in range(2):
                    last = copy(hN[:, tt, q * 512:(q + 1) * 512], ps[:, 1 + tt * 2 + q, :])
            last.then_inc(madeA, mark(madeA, "out"))

        @block.vector
        def _(v):
            V = nc.vector
            tt_, ts, stt = V.tensor_tensor, V.tensor_scalar, V.scalar_tensor_tensor

            def B(x, n):
                return x[:, :, None].broadcast_to([P, x.shape[1], n])

            def over(x, n):
                return x[:, None, :].broadcast_to([P, n, x.shape[1]])

            def rms(key, bank, dst, n=D):
                v.wait_ge(filled, nth(filled, ("ss", key)))
                ts(dst, ps[:, bank, 0:T], 1.0 / n, EPS, ALU.mult, ALU.add).then_inc(madeV, mark(madeV, ("var", key)))
                v.wait_ge(madeA, nth(madeA, ("std", key)))
                V.reciprocal(dst, dst)
                v.drain()

            def modulate(dst, src, r, gs, sh, key):
                for k in range(KD):
                    last = stt(dst[:, k, :], src[:, k, :], gs[:, k:k + 1], r, ALU.mult, ALU.mult)
                if sh is not None:
                    v.drain()
                    for k in range(KD):
                        last = ts(dst[:, k, :], dst[:, k, :], sh[:, k:k + 1], None, ALU.add)
                last.then_inc(madeV, mark(madeV, key))

            V.memset(cpad2, 0.0)
            v.wait_ge(small_in, SMALL)
            V.tensor_copy(packs[32:48, 2, :].rearrange("p (s c) -> p s c", s=2),
                                     dt2[32:48, :, None].broadcast_to([16, 2, 64])).then_inc(madeV, mark(madeV, "dt rows"))
            v.wait_ge(madeA, nth(madeA, "cols"))
            tt_(csil[:, :], csil[:, :], cols[:, 0, 104:128], ALU.mult)
            V.memset(cpad1, 0.0)
            v.drain()
            V.tensor_copy(cpad2[:, :, 0], csil[:, 8:16])
            V.tensor_copy(cpad2[:, :, 1], csil[:, 16:24])
            V.tensor_copy(cpad1[:, :, 0], csil[:, 0:8]).then_inc(madeV, mark(madeV, "csil"))
            rms("n1", 5, rstd[:, 0:T])
            lr, li = cols[:, 2, 0:16], cols[:, 2, 16:32]
            sm = lambda i: small[:, i, :]
            v.wait_ge(madeA, nth(madeA, "dt"))

            def step(ins):
                v.drain()
            step(tt_(sm(1), lr, sm(0), ALU.mult))
            step(tt_(sm(2), li, sm(0), ALU.mult))
            step(ts(sm(2), sm(2), 1.0 / TWO_PI, None, ALU.mult))
            step(ts(sm(3), sm(2), MAGIC, None, ALU.add))
            step(ts(sm(3), sm(3), -MAGIC, None, ALU.add))
            tt_(sm(3), sm(2), sm(3), ALU.subtract).then_inc(madeV, mark(madeV, "angle"))
            v.wait_ge(madeA, nth(madeA, "trig"))
            step(tt_(sm(7), sm(6), sm(6), ALU.mult))
            step(ts(sm(7), sm(7), -2.0, 1.0, ALU.mult, ALU.add))
            tt_(sm(8), sm(4), sm(7), ALU.mult)
            tt_(sm(9), sm(4), sm(5), ALU.mult)
            tt_(sm(10), lr, lr, ALU.mult)
            step(tt_(sm(11), li, li, ALU.mult))
            tt_(sm(10), sm(10), sm(11), ALU.add)
            step(ts(sm(8), sm(8), -1.0, None, ALU.add))
            V.reciprocal(sm(10), sm(10))
            tt_(sm(12), sm(8), lr, ALU.mult)
            tt_(sm(13), sm(9), li, ALU.mult)
            tt_(sm(14), sm(9), lr, ALU.mult)
            step(tt_(sm(15), sm(8), li, ALU.mult))
            tt_(sm(12), sm(12), sm(13), ALU.add)
            step(tt_(sm(14), sm(14), sm(15), ALU.subtract))
            tt_(sm(12), sm(12), sm(10), ALU.mult)
            step(tt_(sm(13), sm(14), sm(10), ALU.mult))
            b3 = lambda x: x.rearrange("p (j h) -> p j h", h=16)
            v.wait_ge(tables_in, TABLES)
            cr_, ci_ = B(sm(12), 16), B(sm(13), 16)
            tmp = b3(sa[:, 0, :])
            tmp2 = b3(sa[:, 1, :])
            tt_(b3(bbuf[:, 0, :]), cr_, b3(bR[:, 0, :]), ALU.mult)
            tt_(tmp, ci_, b3(bR[:, 1, :]), ALU.mult)
            tt_(b3(bbuf[:, 1, :]), cr_, b3(bR[:, 1, :]), ALU.mult)
            step(tt_(tmp2, ci_, b3(bR[:, 0, :]), ALU.mult))
            tt_(b3(bbuf[:, 0, :]), b3(bbuf[:, 0, :]), tmp, ALU.subtract)
            step(tt_(b3(bbuf[:, 1, :]), b3(bbuf[:, 1, :]), tmp2, ALU.add))
            for n in range(2):
                d_ = bd[:, n, :].rearrange("p (j s h) -> p j s h", s=2, h=16)
                for s in range(2):
                    ts(d_[:, :, s, :], b3(bbuf[:, n, :]), cst("half", s, s + 1), None, ALU.mult)
                c3 = cR[:, n, :].rearrange("p (t c) -> p t c", c=P)
                last = stt(c3, c3, 1.0 if n == 0 else -1.0, over(cst("parity"), 4), ALU.mult, ALU.mult)
            last.then_inc(madeV, mark(madeV, "bd"))
            v.wait_ge(filled, nth(filled, "mod1"))
            mod_cols = lambda bank: ps[:, bank:bank + 3, :].rearrange("p a b -> p (a b)").rearrange("p (i c) -> p i c", c=32)
            tt_(mod1[:, :], mod_cols(5)[:, :, 0], cols[:, 0, 0:48], ALU.add)
            v.drain()
            stt(gain[:, 0, :], mod1[:, 8:16], 1.0, cols[:, 0, 48:56], ALU.add, ALU.mult)
            stt(gain[:, 1, :], mod1[:, 32:40], 1.0, cols[:, 0, 56:64], ALU.add, ALU.mult)
            v.drain()
            modulate(hT[:, :, 0:T], xT[:, :, :], rstd[:, 0:T], gain[:, 0, :], mod1[:, 0:8], "h1")

            def fraction(j):
                if j >= 2:
                    v.wait_ge(madeA, nth(madeA, ("sin", j - 2)))
                f, th = fr[j % 2], small[:, 2, j:j + 1]
                step(ts(f, cst("time"), th, MAGIC, ALU.mult, ALU.add))
                step(ts(f, f, -MAGIC, None, ALU.add))
                stt(f, cst("time"), th, f, ALU.mult, ALU.subtract).then_inc(madeV, mark(madeV, ("fr", j)))

            fraction(0)
            fraction(1)
            for j in range(16):
                tb = tabs[j % 2]
                v.wait_ge(madeA, nth(madeA, ("sin", j)))
                step(ts(tb[:, 0, :], tb[:, 0, :], -2.0, 1.0, ALU.mult, ALU.add))
                if j + 2 < 16:
                    fraction(j + 2)
                v.wait_ge(filled, nth(filled, ("bu", j)))
                bu = ps[:, 4 + j % 2, :].rearrange("p (a b) -> p a b", a=2)
                C, S_ = over(tb[:, 0, :], 2), over(tb[:, 1, :], 2)
                tt_(sa, bu, C, ALU.mult)
                tt_(sb_, bu, S_, ALU.mult).then_inc(vemptied, mark(vemptied, ("bu", j)))
                v.drain()
                tt_(sw[:, 0, :], sa[:, 0, :], sb_[:, 1, :], ALU.add)
                step(tt_(sw[:, 1, :], sa[:, 1, :], sb_[:, 0, :], ALU.subtract))
                r = small[:, 4, j:j + 1].broadcast_to([P, T])
                V.tensor_tensor_scan(sz[:, 0, :], r, sw[:, 0, :], 0.0, ALU.mult, ALU.add)
                step(V.tensor_tensor_scan(sz[:, 1, :], r, sw[:, 1, :], 0.0, ALU.mult, ALU.add))
                tt_(sa, sz, C, ALU.mult)
                step(tt_(sb_, sz, S_, ALU.mult))
                if j >= 2:
                    v.wait_ge(filled, nth(filled, ("y", j - 2)))
                tt_(ss2[j % 2][:, 0, :], sa[:, 0, :], sb_[:, 1, :], ALU.subtract)
                tt_(ss2[j % 2][:, 1, :], sa[:, 1, :], sb_[:, 0, :], ALU.add).then_inc(madeV, mark(madeV, ("s", j)))
            v.wait_ge(filled, nth(filled, ("y", 15)))
            for k in range(4):
                last = stt(yT[:, k, :], uT[:, k, :], cols[:, 2, 48 + k:49 + k], ps[:, 6 + k // 2, (k % 2) * T:(k % 2 + 1) * T],
                           ALU.mult, ALU.add)
            last.then_inc(madeV, mark(madeV, "yD"))

            def seg(n, u):
                if n == 1:
                    g, tt, x = u
                    return (4, 16 if x == "cmp" else P * (tt + 1))
                return (2, 512)

            def view(x, ns, nk):
                w = x[:, 0:ns * nk].rearrange("p (s k) -> p s k", s=ns)
                return w[:, :, 0:NCMP] if nk == 16 else w

            def maxima(n, i, u):
                v.wait_ge(filled, nth(filled, ("S", n, i)))
                ns, nk = seg(n, u)
                sc = ps[:, 2 * (i % 2):2 * (i % 2) + 2, 0:ns * nk // 2].rearrange("p a (s k) -> p a s k", k=nk)
                m = NCMP if nk == 16 else nk
                dst = stat[:, i % 2, 0:ns].rearrange("p (a s) -> p a s", a=2)
                V.tensor_reduce(dst, sc[:, :, :, 0:m], AX.X, ALU.max, negate=True).then_inc(madeV, mark(madeV, ("mx", n, i)))

            def normalise(n, i, u):
                v.wait_ge(madeA, nth(madeA, ("exp", n, i)))
                ns, nk = seg(n, u)
                st = stat[:, i % 2, :]
                c = st[:, 8:8 + ns]
                step(V.reciprocal(c, st[:, 4:4 + ns]))
                if n == 1:
                    g, tt, x = u
                    at = ("cmp", "slc", "win").index(x) * 16 + 4 * g
                    c2 = c.rearrange("p (par half) -> p par half", par=2)
                    step(tt_(c2, c2, gates[:, tt, at:at + 4].rearrange("p (half par) -> p par half", par=2), ALU.mult))
                    if x == "cmp":
                        step(ts(c, c, cst("cmprow", tt, tt + 1), None, ALU.mult))
                e_ = view((Eb if n == 1 else E2)[i % 2], ns, nk)
                m = NCMP if nk == 16 else nk
                tt_(e_, e_, B(c, m), ALU.mult).then_inc(madeV, mark(madeV, ("P", n, i)))

            def bias(tt):
                v.wait_ge(bias_in[tt], 256)
                x = nab2[:, :, :].rearrange("p h (r c) -> p (h r) c", c=64)
                tt_(x, x, over(cst("namask"), 32), ALU.add).then_inc(madeV, mark(madeV, ("bias", tt)))

            def attention(n, units):
                maxima(n, 0, units[0])
                maxima(n, 1, units[1])
                normalise(n, 0, units[0])
                for i, u in enumerate(units):
                    if i + 1 < len(units):
                        normalise(n, i + 1, units[i + 1])
                    if n == 2 and i == 6:
                        bias(1)
                    if i + 2 < len(units):
                        maxima(n, i + 2, units[i + 2])

            v.wait_ge(emptied, nth(emptied, ("p1", 12)))
            attention(1, units1)

            def merge(key, gkey, out_key):
                for c in range(4):
                    v.wait_ge(madeA, nth(madeA, ("sgl", gkey, c)))
                    v.wait_ge(filled, nth(filled, (key, c)))
                    for n in range(2):
                        s_ = sgl[:, n, :, :].rearrange("p a b -> p (a b)")
                        tt_(s_, ps[:, n, :], s_, ALU.mult)
                    v.drain()
                    tt_(mgd[:, 2 * c:2 * c + 2, :], sgl[:, 0, :, :], sgl[:, 1, :, :], ALU.add).then_inc(madeV, mark(madeV, (out_key, c)))

            v.wait_ge(filled, nth(filled, "mod2"))
            v.wait_ge(madeA, nth(madeA, "ysig"))
            tt_(yS, yS, mgd[:, 0:4, :], ALU.mult).then_inc(madeV, mark(madeV, "yS"))
            tt_(mod2[:, :, :], mod_cols(4)[:, :, 0:2], B(cols[:, 1, 0:48], 2), ALU.add)
            v.drain()
            merge("branch", "gates", "mgd")
            for c in range(4):
                v.wait_ge(filled, nth(filled, ("tm", c)))
                for m in range(2):
                    k = 2 * c + m
                    last = stt(xT[:, k, :], ps[:, 4 + c, m * T:(m + 1) * T], mod1[:, 16 + k:17 + k], xT[:, k, :], ALU.mult, ALU.add)
            last.then_inc(madeV, mark(madeV, "xf1"))

            def top(scores, n, kth, chosen, a1, a2):
                x = a1[:, 0:n * n].rearrange("p (i j) -> p i j", j=n)
                y = a2[:, 0:n * n].rearrange("p (i j) -> p i j", j=n)
                mine, other = B(scores, n), over(scores, n)
                idx = cst("time", 0, n)
                tt_(x, B(idx, n), over(idx, n), ALU.is_gt)
                step(tt_(y, other, mine, ALU.is_equal))
                step(tt_(y, y, x, ALU.mult))
                step(tt_(x, other, mine, ALU.is_gt))
                step(tt_(x, x, y, ALU.add))
                step(V.tensor_reduce(chosen, x, AX.X, ALU.add))
                step(ts(chosen, chosen, kth - 0.5, None, ALU.is_lt))

            def top_experts(scores, kth, chosen, tt):
                best, gt, eq, cum = m8[:, tt, :], t1[:, 0:E], t1[:, E:2 * E], t1[:, 2 * E:3 * E]
                left = rt[:, tt, 12:13]
                step(V.max(best, scores))
                t_ = best[:, kth - 1:kth]
                ts(gt, scores, t_, None, ALU.is_gt)
                step(ts(eq, scores, t_, None, ALU.is_equal))
                V.tensor_reduce(left, gt, AX.X, ALU.add)
                step(V.tensor_tensor_scan(cum, cst("ones", 0, E), eq, 0.0, ALU.mult, ALU.add))
                step(ts(left, left, -1.0, kth + 0.5, ALU.mult, ALU.add))
                step(stt(eq, cum, left, eq, ALU.is_lt, ALU.mult))
                step(tt_(chosen, gt, eq, ALU.add))

            def moe_front(key, gs, sh, nr):
                rms(key, 0, rstd[:, 0:T])
                modulate(hT[:, :, 0:T], xT[:, :, :], rstd[:, 0:T], gs, sh, "h" + key)
                V.memset(zero, 0.0)
                V.memset(sel[:, :, E:E + 4], 0.0)
                V.memset(Wt[:, :, E:E + 4], 0.0)
                V.memset(ohtF[1], 0.0)
                V.memset(ysF1 if key == "f1" else ysF, 0.0)
                if key == "f2":
                    V.memset(biasB, 0.0).then_inc(madeV, mark(madeV, "biasB"))
                v.wait_ge(filled, nth(filled, "logits" + key))
                for tt in range(TT):
                    last = V.tensor_copy(lg[:, tt, 0:nr], ps[:, 5, tt * 64:tt * 64 + nr])
                step(last)
                if key == "f1":
                    step(V.tensor_copy(gx[:, :, 0:4], lg[:, :, 0:4]))
                    step(V.tensor_reduce(rt[:, :, 8], gx[:, :, 0:4], AX.X, ALU.max))
                    for tt in range(TT):
                        top(gx[:, tt, 0:4], 4, 1, gx[:, tt, 4:8], t1, t2)
                    for tt in range(TT):
                        e4 = t1[:, 0:E].rearrange("p (g e) -> p g e", e=8)
                        step(ts(gx[:, tt, 4:8], gx[:, tt, 4:8], -1.0, -NEG, ALU.add, ALU.mult))
                        step(tt_(e4, lg[:, tt, 4:36].rearrange("p (g e) -> p g e", e=8), B(gx[:, tt, 4:8], 8), ALU.add))
                        step(V.tensor_copy(lg[:, tt, 0:E], t1[:, 0:E]))
                        step(ts(gx[:, tt, 0:4], gx[:, tt, 0:4], rt[:, tt, 8:9], None, ALU.subtract))
                for tt in range(TT):
                    top_experts(lg[:, tt, 0:E], 2 if key == "f1" else 4, Am[:, tt, :], tt)
                V.memset(crow[:, 3, 1:2], 0.0).then_inc(madeV, mark(madeV, "chosen" + key))
                step(V.tensor_reduce(rt[:, :, 9], lg[:, :, 0:E], AX.X, ALU.max))
                for tt in range(TT):
                    last = ts(lg[:, tt, 0:E], lg[:, tt, 0:E], rt[:, tt, 9:10], None, ALU.subtract)
                last.then_inc(madeV, mark(madeV, "shifted" + key))
                v.wait_ge(filled, nth(filled, "places" + key))
                cnt = ps[0:1, 5, 256:256 + E]
                c0, c1, c2 = crow[0:1, 0, :], crow[0:1, 1, :], crow[0:1, 2, :]
                step(ts(c0, cnt, SLOTS + 0.5, None, ALU.is_gt))
                for b in range(2, MAXB):
                    step(stt(c0, cnt, SLOTS * b + 0.5, c0, ALU.is_gt, ALU.add))
                if key == "f1":
                    step(V.tensor_reduce(c2[:, 0:E // 2], c0.rearrange("o (p x) -> o p x", x=2), AX.X, ALU.max))
                    step(V.tensor_copy(c0[:, 0:E // 2], c2[:, 0:E // 2]))
                step(V.memset(c2, 1.0))
                step(V.tensor_tensor_scan(c1, c2, c0, 0.0, ALU.mult, ALU.add))
                step(tt_(c1, c1, c0, ALU.subtract))
                V.tensor_copy(tabI[0:1, 0, :], c0)
                V.tensor_copy(tabI[0:1, 1, :], c1)
                for tt in range(TT):
                    step(stt(sel[:, tt, 0:E], ps[:, 5, 128 + tt * E:128 + (tt + 1) * E], 1.0, Am[:, tt, :], ALU.add, ALU.mult))
                step(ts(sel[:, :, :], sel[:, :, :], -1.0, None, ALU.add))
                v.wait_ge(madeA, nth(madeA, "exp" + key))
                step(tt_(Wt[:, :, 0:E], Wt[:, :, 0:E], Am[:, :, :], ALU.mult))
                step(V.tensor_reduce(rt[:, :, 10], Wt[:, :, 0:E], AX.X, ALU.add))
                if key == "f1":
                    step(V.tensor_reduce(rt[:, :, 11], rt[:, :, 0:4], AX.X, ALU.add))
                    step(tt_(rt[:, :, 10], rt[:, :, 10], rt[:, :, 11], ALU.mult))
                step(V.reciprocal(rt[:, :, 10], rt[:, :, 10]))
                for tt in range(TT):
                    last = ts(Wt[:, tt, 0:E], Wt[:, tt, 0:E], rt[:, tt, 10:11], None, ALU.mult)
                step(last)
                V.memset(rt[:, :, 14:15], 0.0).then_inc(madeV, mark(madeV, "ready" + key))
                V.memset(rt[:, :, 15:16], 0.0).then_inc(madeV, mark(madeV, "tables" + key))

            def moe(n):
                s, x = S[n, "first"], S[n, "more"]
                w = 512 if n == 2 else 256

                def gather_onehot(s, dst, g, slots):
                    for tt in range(TT):
                        for x in range(3 - n):
                            e = bass.ds(g * (3 - n) + x, 1)
                            last = ts(dst[:, tt, x * SLOTS:(x + 1) * SLOTS], slots, sel[:, tt, e], None, ALU.is_equal)
                    last.then_inc(s["gather_onehot"], 1)

                def spread_onehot(s, dst, g, slots):
                    for tt in range(TT):
                        for x in range(2):
                            e = bass.ds(g * 2 + x if n == 1 else g, 1)
                            last = ts(dst[:, tt, x * SLOTS:(x + 1) * SLOTS], slots, sel[:, tt, e], Wt[:, tt, e],
                                      ALU.is_equal, ALU.mult)
                    last.then_inc(s["spread_onehot"], 1)

                def xs_out(s, dst):
                    V.tensor_copy(dst.rearrange("p a b -> p (a b)"), ps[:, 0, :]).then_inc(s["xs"], 1)

                def pair_out(s, dst):
                    for x in range(2):
                        last = V.tensor_copy(dst[:, 4 * x:4 * x + 4, :].rearrange("p a b -> p (a b)"), ps[:, 2 * x, :])
                    last.then_inc(s["xs"], 1)

                def ys_out(s, dst, dst1):
                    if n == 1:
                        V.tensor_copy(dst1[:, 0:512], ps[:, 0, :])
                        V.tensor_copy(dst1[:, 512:1024], ps[:, 3, :]).then_inc(s["ys"], 1)
                    else:
                        V.tensor_copy(dst, ps[:, 3, :]).then_inc(s["ys"], 1)

                def select(dst, e):
                    V.tensor_copy(dst, cst("ident")[:, bass.ds(e, 1)].broadcast_to([P, SLOTS]))

                def units(s, q):
                    v.wait_ge(s["hidden"], q)
                    if n == 1:
                        V.tensor_copy(glu[:, 0:w], ps[:, 1, 0:w]).then_inc(s["glu"], 1)
                        v.drain()
                        tt_(lin[:, 0:w], ps[:, 1, w:2 * w], glu[:, 0:w], ALU.mult)
                    else:
                        ts(glu, ps[:, 1, :], 7.0, None, ALU.min).then_inc(s["glu"], 1)
                        ts(lin, ps[:, 2, :], 7.0, -7.0, ALU.min, ALU.max)
                        v.drain()
                        stt(lin, lin, 1.0, glu, ALU.add, ALU.mult)
                    v.drain()
                    v.wait_ge(s["sig"], q)
                    tt_(act[:, 0:w], lin[:, 0:w], sg[:, 0:w], ALU.mult).then_inc(s["act"], 1)

                slots0 = cst("time", 0, SLOTS)

                def further(it, u, e, q, b):
                    slots = cst("time")[:, bass.ds(b * SLOTS, SLOTS)]
                    gather_onehot(x, ohgM, e, slots)
                    spread_onehot(x, ohsM, e, slots)
                    v.wait_ge(x["gathered"], q + 1)
                    pair_out(x, xsM1) if n == 1 else xs_out(x, xsM)
                    units(x, q + 1)
                    v.wait_ge(x["down"], q + 1)
                    ys_out(x, ysM, ysM1)

                def first(it, u, e):
                    units(s, e + 1)
                    if n == 2:
                        select(esel[(u + 1) % 2], e + 1)
                    v.wait_ge(s["gathered"], e + 2)
                    pair_out(s, xsP) if n == 1 else xs_out(s, xsF)
                    gather_onehot(s, ohgF, e + 2, slots0)
                    v.wait_ge(s["spreadT"], e + 1)
                    spread_onehot(s, ohsF, e + 1, slots0)
                    v.wait_ge(s["down"], e + 1)
                    ys_out(s, ysF, ysF1)

                V.memset(rt[:, :, 13:14], 0.0).then_inc(s["ys"], 1)
                V.memset(crow[:, 3, 0:1], 0.0).then_inc(s["spread"], 1)
                if n == 2:
                    select(esel[0], 0)
                gather_onehot(s, ohgF, 0, slots0)
                spread_onehot(s, ohsF, 0, slots0)
                v.wait_ge(s["gathered"], 1)
                pair_out(s, xsP) if n == 1 else xs_out(s, xsF)
                gather_onehot(s, ohgF, 1, slots0)
                run_experts(v, n, further, first)

            moe_front("f1", gain[:, 1, :], mod1[:, 24:32], 36)
            moe(1)
            v.wait_ge(filled, nth(filled, "moe1"))
            for k in range(KD):
                last = stt(xT[:, k, :], ps[:, 4 + k // 2, (k % 2) * T:(k % 2 + 1) * T], mod1[:, 40 + k:41 + k], xT[:, k, :], ALU.mult, ALU.add)
            last.then_inc(madeV, mark(madeV, "moe1 out"))
            rms("fin", 0, rstd[:, 0:T])
            modulate(xT[:, :, :], xT[:, :, :], rstd[:, 0:T], cols[:, 0, 64:72], None, "x2")
            stt(gain[:, 2, :], mod2[:, 8:16, 0], 1.0, cols[:, 1, 48:56], ALU.add, ALU.mult)
            stt(gain[:, 3, :], mod2[:, 8:16, 1], 1.0, cols[:, 1, 48:56], ALU.add, ALU.mult)
            tt_(gain[:, 4, :], mod2[:, 16:24, 0], cols[:, 1, 56:64], ALU.mult)
            stt(gain[:, 5, :], mod2[:, 32:40, 0], 1.0, cols[:, 1, 64:72], ALU.add, ALU.mult)
            tt_(gain[:, 0, :], mod2[:, 40:48, 0], cols[:, 1, 72:80], ALU.mult)
            v.drain()
            rms("n2", 0, rstd[:, 0:T])
            modulate(hT[:, :, 0:T], xT[:, :, :], rstd[:, 0:T], gain[:, 2, :], mod2[:, 0:8, 0], "h2")
            rms("ctx", 5, rstd[:, T:2 * T])
            modulate(hT[:, :, T:2 * T], hT[:, :, T:2 * T], rstd[:, T:2 * T], gain[:, 3, :], mod2[:, 0:8, 1], "hctx")
            v.wait_ge(emptied, nth(emptied, ("p2", 3)))
            q3 = lambda x: x.rearrange("p t (h d) -> p (t h) d", d=HD)
            tt_(q3(qt1), q3(qbN), q3(qbN), ALU.mult)
            step(tt_(q3(kt1), q3(kbN), q3(kbN), ALU.mult))
            V.tensor_reduce(rn[:, 0:16], q3(qt1), AX.X, ALU.add)
            step(V.tensor_reduce(rn[:, 16:24], q3(kt1), AX.X, ALU.add))
            ts(rn[:, 0:24], rn[:, 0:24], 1.0 / HD, EPS, ALU.mult, ALU.add).then_inc(madeV, mark(madeV, ("var", "heads")))
            bias(0)
            v.wait_ge(madeA, nth(madeA, ("std", "heads")))
            step(V.reciprocal(rn[:, 0:24], rn[:, 0:24]))
            tt_(q3(qbN), q3(qbN), B(rn[:, 0:16], HD), ALU.mult)
            step(tt_(q3(kbN), q3(kbN), B(rn[:, 16:24], HD), ALU.mult))
            tt_(q3(qbN), q3(qbN), over(gqk[:, 0, :], 16), ALU.mult)
            step(tt_(q3(kbN), q3(kbN), over(gqk[:, 1, :], 8), ALU.mult))
            for x, x1, x2, nh in ((qbN, qt1, qt2, 8), (kbN, kt1, qt2, 2)):
                for tt in range(TT):
                    h3 = lambda y: y[:, tt, 0:nh * HD].rearrange("p (h d) -> p h d", d=HD)
                    h5 = lambda y: y[:, tt, 0:nh * HD].rearrange("p (h a b c) -> p h a b c", a=2, b=2, c=16)
                    tt_(h3(x1), h3(x), over(cst("ropecos", tt * HD, (tt + 1) * HD), nh), ALU.mult)
                    sn = cst("ropesin", tt * HD, (tt + 1) * HD).rearrange("p (a b c) -> p a b c", a=2, b=2)
                    for b in range(2):
                        tt_(h5(x2)[:, :, :, b, :], h5(x)[:, :, :, 1 - b, :],
                            sn[:, None, :, b, :].broadcast_to([P, nh, 2, 16]), ALU.mult)
                    v.drain()
                    step(tt_(h3(x), h3(x1), h3(x2), ALU.add))
            V.tensor_copy(kt1[:, :, 0:HD], kbN[:, :, HD:2 * HD])
            V.tensor_copy(kt1[:, :, HD:2 * HD], kbN[:, :, 0:HD]).then_inc(madeV, mark(madeV, "rope"))
            attention(2, units2)
            merge("branch2", "gates2", "mgd2")

            def residual(key, g_, out_key):
                rms(key, 0, rstd[:, 0:T])
                step(tt_(o2[:, :, :], o2[:, :, :], over(rstd[:, 0:T], KD), ALU.mult))
                for k in range(KD):
                    last = stt(xT[:, k, :], o2[:, k, :], g_[:, k:k + 1], xT[:, k, :], ALU.mult, ALU.add)
                last.then_inc(madeV, mark(madeV, out_key))

            residual("post", gain[:, 4, :], "xf2")
            moe_front("f2", gain[:, 5, :], mod2[:, 24:32, 0], 32)
            moe(2)
            residual("postf", gain[:, 0, :], "xout")
    return counts.values


_SQUEEZE = ["ada_w", "ada_b", "norm1_g", "w_in", "ssm_lam_re", "ssm_lam_im", "ssm_log_dt", "ssm_b_re", "ssm_b_im",
            "ssm_c_re", "ssm_c_im", "ssm_d", "ssm_w_glu", "ssm_w_o", "nsa_cmp_pos", "nsa_cmp_w1", "nsa_cmp_w2",
            "nsa_w_o", "w_out", "norm2_g", "moe_w_group", "moe_b_group", "moe_w_expert", "moe_b_expert",
            "moe_w_gate", "moe_w_up", "moe_w_down", "w_mod_2", "b_mod_2", "g_pre_mix_2", "g_post_mix_2",
            "g_pre_ffn_2", "g_post_ffn_2", "w_in_2", "rpb_2", "g_qnorm_2", "g_knorm_2", "w_out_a_2", "w_out_b_2",
            "w_o_2", "w_router_2", "b_router_2", "w_gu_2", "b_gu_2", "w_dn_2", "b_dn_2"]
_SMALLER = ["x", "ctx_2"]
_PLAIN = ["c", "final_g", "c_2", "c_ctx_2"]


def kernel(**inputs):
    import concourse.bacc as _bacc
    from concourse.bass_utils import run_bass_kernel_spmd as _run

    arrays, shapes = {}, {}
    for name in _SQUEEZE + _SMALLER + _PLAIN:
        a = np.ascontiguousarray(inputs[name])
        if name not in _PLAIN:
            a = a.reshape(a.shape[1:])
        arrays[f"in_{name}_dram"] = a
        shapes[name] = a.shape
    arrays["constants_dram"] = CONST_ARRAY
    known = None
    for _ in range(2):
        nc = _bacc.Bacc("TRN2", target_bir_lowering=False, num_devices=1)
        A = {name: nc.dram_tensor(f"in_{name}_dram", shape, F32, kind="ExternalInput").ap()
             for name, shape in shapes.items()}
        const = nc.dram_tensor("constants_dram", CONST_ARRAY.shape, F32, kind="ExternalInput").ap()
        out = nc.dram_tensor("out_0_dram", (T, D), F32, kind="ExternalOutput").ap()
        known = program(nc, A, const, out, known)
    r = _run(nc, [arrays], core_ids=[0])
    return r.results[0]["out_0_dram"].reshape(1, T, D)
```
